# Optimizing a Trainium2 kernel written in Bass

```python
import math
import jax, jax.numpy as jnp
from jax import lax
import numpy as np

D_MODEL = 1024
BATCH = 1
SEQ = 1024
DEPTH = 1

GLA_HEADS = 4
GLA_DK = D_MODEL // 2 // GLA_HEADS
GLA_DV = D_MODEL // GLA_HEADS
GLA_GATE_RANK = 16
GLA_TAU = 16.0
GLA_CHUNK = 64
MLA_HEADS = 8
MLA_NOPE = 128
MLA_ROPE = 64
MLA_V = 128
MLA_Q_RANK = 384
MLA_KV_RANK = 256
ROPE_THETA = 10000.0
Q_BLOCK = 128
N_BRANCHES = 2
N_EXPERTS = 16
EC_CAPACITY = 2
EXPERT_FF = 1024
EPS = 1e-6

IN_SPLITS = (
    GLA_HEADS * GLA_DK,
    GLA_HEADS * GLA_DK,
    GLA_HEADS * GLA_DV,
    GLA_HEADS * GLA_DV,
    GLA_GATE_RANK,
    GLA_GATE_RANK,
    MLA_Q_RANK,
    MLA_KV_RANK,
    MLA_ROPE,
    N_BRANCHES * D_MODEL,
)
IN_WIDTH = sum(IN_SPLITS)

kernel_name = "hybrid_gla_mla_expert_choice_block"

def rmsnorm(x, g):
    x32 = x.astype(jnp.float32)
    y = x32 * lax.rsqrt(jnp.mean(x32 * x32, axis=-1, keepdims=True) + EPS)
    return (y * g.astype(jnp.float32)).astype(x.dtype)

def rope(x, pos):
    half = x.shape[-1] // 2
    freqs = ROPE_THETA ** (-jnp.arange(half, dtype=jnp.float32) / half)
    ang = pos.astype(jnp.float32)[..., None] * freqs
    cos = jnp.cos(ang)[:, :, None, :]
    sin = jnp.sin(ang)[:, :, None, :]
    x32 = x.astype(jnp.float32)
    x1, x2 = x32[..., :half], x32[..., half:]
    return jnp.concatenate([x1 * cos - x2 * sin, x2 * cos + x1 * sin], axis=-1).astype(x.dtype)

def gla_direction(q, k, v, log_a, inclusive):
    B, H, S, dk = q.shape
    dv = v.shape[-1]
    nc = S // GLA_CHUNK
    q = q.reshape(B, H, nc, GLA_CHUNK, dk)
    k = k.reshape(B, H, nc, GLA_CHUNK, dk)
    v = v.reshape(B, H, nc, GLA_CHUNK, dv)
    b = jnp.cumsum(log_a.reshape(B, H, nc, GLA_CHUNK, dk), axis=3)
    q_t = q * jnp.exp(b)
    k_t = k * jnp.exp(-b)
    mask = jnp.tril(jnp.ones((GLA_CHUNK, GLA_CHUNK), bool), k=0 if inclusive else -1)
    att = jnp.where(mask, jnp.einsum('bhncd,bhnmd->bhncm', q_t, k_t), 0.0)
    o_intra = jnp.einsum('bhncm,bhnme->bhnce', att, v)
    b_last = b[..., -1:, :]
    k_dec = k * jnp.exp(b_last - b)
    d_state = jnp.einsum('bhncd,bhnce->nbhde', k_dec, v)
    decay = jnp.moveaxis(jnp.exp(b_last[..., 0, :]), 2, 0)

    def step(state, inp):
        dec, ds = inp
        return dec[..., None] * state + ds, state

    init = jnp.zeros((B, H, dk, dv), jnp.float32)
    _, s_prev = lax.scan(step, init, (decay, d_state))
    o_inter = jnp.einsum('bhncd,nbhde->bhnce', q_t, s_prev)
    return (o_intra + o_inter).reshape(B, H, S, dv)

def setup_inputs(seed: int = 0) -> dict:
    key = jax.random.key(seed)
    ks = jax.random.split(key, 24)

    def w(k, shape, fan_in):
        return jax.random.normal(k, shape, jnp.float32) * (fan_in ** -0.5)

    def gain(k, n):
        return 1.0 + 0.02 * jax.random.normal(k, (n,), jnp.float32)

    hq = MLA_NOPE + MLA_ROPE
    return {
        "x": jax.random.normal(ks[0], (BATCH, SEQ, D_MODEL), jnp.float32),
        "positions": jnp.tile(jnp.arange(SEQ, dtype=jnp.int32)[None, :], (BATCH, 1)),
        "g_mix": gain(ks[1], D_MODEL),
        "w_in": w(ks[2], (D_MODEL, IN_WIDTH), D_MODEL),
        "gla_wa2_f": w(ks[3], (GLA_GATE_RANK, GLA_HEADS * GLA_DK), GLA_GATE_RANK),
        "gla_ba_f": 0.1 * jax.random.normal(ks[4], (GLA_HEADS * GLA_DK,), jnp.float32),
        "gla_wa2_b": w(ks[5], (GLA_GATE_RANK, GLA_HEADS * GLA_DK), GLA_GATE_RANK),
        "gla_ba_b": 0.1 * jax.random.normal(ks[6], (GLA_HEADS * GLA_DK,), jnp.float32),
        "gla_onorm": gain(ks[7], GLA_DV),
        "w_gla_out": w(ks[8], (GLA_HEADS * GLA_DV, D_MODEL), GLA_HEADS * GLA_DV),
        "mla_q_norm": gain(ks[9], MLA_Q_RANK),
        "w_uq": w(ks[10], (MLA_Q_RANK, MLA_HEADS * hq), MLA_Q_RANK),
        "mla_kv_norm": gain(ks[11], MLA_KV_RANK),
        "w_ukv": w(ks[12], (MLA_KV_RANK, MLA_HEADS * (MLA_NOPE + MLA_V)), MLA_KV_RANK),
        "q_head_norm": gain(ks[13], hq),
        "k_head_norm": gain(ks[14], hq),
        "w_mla_out": w(ks[15], (MLA_HEADS * MLA_V, D_MODEL), MLA_HEADS * MLA_V),
        "w_o": w(ks[16], (D_MODEL, D_MODEL), D_MODEL),
        "g_ffn": gain(ks[17], D_MODEL),
        "w_router": w(ks[18], (D_MODEL, N_EXPERTS), D_MODEL),
        "w_gate_e": w(ks[19], (N_EXPERTS, D_MODEL, EXPERT_FF), D_MODEL),
        "w_up_e": w(ks[20], (N_EXPERTS, D_MODEL, EXPERT_FF), D_MODEL),
        "w_down_e": w(ks[21], (N_EXPERTS, EXPERT_FF, D_MODEL), EXPERT_FF),
    }

def token_mixer(x, positions, g_mix, w_in, gla_wa2_f, gla_ba_f, gla_wa2_b, gla_ba_b,
                gla_onorm, w_gla_out, mla_q_norm, w_uq, mla_kv_norm, w_ukv,
                q_head_norm, k_head_norm, w_mla_out, w_o):
    B, S, D = x.shape
    h = rmsnorm(x, g_mix)
    proj = h @ w_in
    offs = [int(o) for o in np.cumsum(IN_SPLITS)[:-1]]
    (gq, gk, gv, gr, gaf, gab, cq, ckv, kr, gates) = jnp.split(proj, offs, axis=-1)

    def heads(t, d):
        return t.reshape(B, S, GLA_HEADS, d).transpose(0, 2, 1, 3).astype(jnp.float32)

    q_a = heads(gq, GLA_DK) * (GLA_DK ** -0.5)
    k_a = heads(gk, GLA_DK)
    v_a = heads(gv, GLA_DV)
    la_f = heads(jax.nn.log_sigmoid(gaf @ gla_wa2_f + gla_ba_f), GLA_DK) / GLA_TAU
    la_b = heads(jax.nn.log_sigmoid(gab @ gla_wa2_b + gla_ba_b), GLA_DK) / GLA_TAU
    o_f = gla_direction(q_a, k_a, v_a, la_f, inclusive=True)
    flip = lambda t: jnp.flip(t, axis=2)
    o_b = flip(gla_direction(flip(q_a), flip(k_a), flip(v_a), flip(la_b), inclusive=False))
    o_a = (o_f + o_b).transpose(0, 2, 1, 3).astype(x.dtype)
    o_a = rmsnorm(o_a, gla_onorm) * jax.nn.silu(gr.reshape(B, S, GLA_HEADS, GLA_DV))
    y_a = o_a.reshape(B, S, GLA_HEADS * GLA_DV) @ w_gla_out

    hq = MLA_NOPE + MLA_ROPE
    q_b = (rmsnorm(cq, mla_q_norm) @ w_uq).reshape(B, S, MLA_HEADS, hq)
    kv = (rmsnorm(ckv, mla_kv_norm) @ w_ukv).reshape(B, S, MLA_HEADS, MLA_NOPE + MLA_V)
    k_nope, v_b = kv[..., :MLA_NOPE], kv[..., MLA_NOPE:]
    k_rope = jnp.broadcast_to(kr[:, :, None, :], (B, S, MLA_HEADS, MLA_ROPE))
    k_b = jnp.concatenate([k_nope, k_rope], axis=-1)
    q_b = rmsnorm(q_b, q_head_norm)
    k_b = rmsnorm(k_b, k_head_norm)
    q_b = jnp.concatenate([q_b[..., :MLA_NOPE], rope(q_b[..., MLA_NOPE:], positions)], axis=-1)
    k_b = jnp.concatenate([k_b[..., :MLA_NOPE], rope(k_b[..., MLA_NOPE:], positions)], axis=-1)
    k_t = k_b.transpose(0, 2, 1, 3)
    v_t = v_b.transpose(0, 2, 1, 3)
    nb = S // Q_BLOCK
    q_blocks = q_b.reshape(B, nb, Q_BLOCK, MLA_HEADS, hq).transpose(1, 0, 3, 2, 4)
    scale = 1.0 / math.sqrt(hq)

    def attend(qblk):
        s = jnp.einsum('bhqd,bhkd->bhqk', qblk, k_t).astype(jnp.float32) * scale
        p = jax.nn.softmax(s, axis=-1)
        return jnp.einsum('bhqk,bhkd->bhqd', p.astype(v_t.dtype), v_t)

    o_b = lax.map(attend, q_blocks)
    o_b = o_b.transpose(1, 0, 3, 2, 4).reshape(B, S, MLA_HEADS * MLA_V)
    y_b = o_b @ w_mla_out

    g = jax.nn.sigmoid(gates.astype(jnp.float32)).astype(x.dtype)
    merged = g[..., :D] * y_a + g[..., D:] * y_b
    return merged @ w_o

def expert_choice_ffn(x, g_ffn, w_router, w_gate_e, w_up_e, w_down_e):
    B, S, D = x.shape
    cap = EC_CAPACITY * S // N_EXPERTS
    h = rmsnorm(x, g_ffn)
    aff = jax.nn.softmax((h @ w_router).astype(jnp.float32), axis=-1)
    vals, idx = lax.top_k(aff.transpose(0, 2, 1), cap)
    xe = jax.vmap(lambda hb, ib: hb[ib])(h, idx)
    a = jnp.einsum('becd,edf->becf', xe, w_gate_e)
    u = jnp.einsum('becd,edf->becf', xe, w_up_e)
    ye = jnp.einsum('becf,efd->becd', jax.nn.silu(a) * u, w_down_e)
    ye = ye * vals[..., None].astype(ye.dtype)
    flat = (jnp.arange(B, dtype=jnp.int32)[:, None, None] * S + idx).reshape(-1)
    out = jax.ops.segment_sum(ye.reshape(-1, D), flat, num_segments=B * S)
    return out.reshape(B, S, D).astype(x.dtype)

def reference(x, positions, g_mix, w_in, gla_wa2_f, gla_ba_f, gla_wa2_b, gla_ba_b,
              gla_onorm, w_gla_out, mla_q_norm, w_uq, mla_kv_norm, w_ukv,
              q_head_norm, k_head_norm, w_mla_out, w_o, g_ffn, w_router,
              w_gate_e, w_up_e, w_down_e):
    for _ in range(DEPTH):
        x = x + token_mixer(x, positions, g_mix, w_in, gla_wa2_f, gla_ba_f, gla_wa2_b,
                            gla_ba_b, gla_onorm, w_gla_out, mla_q_norm, w_uq,
                            mla_kv_norm, w_ukv, q_head_norm, k_head_norm, w_mla_out, w_o)
        x = x + expert_choice_ffn(x, g_ffn, w_router, w_gate_e, w_up_e, w_down_e)
    return x


_drawn_inputs = setup_inputs


def setup_inputs(seed=0):
    import zlib

    import numpy as np

    out = dict(_drawn_inputs(seed))
    spreads = {}
    factors = {'g_mix': 2.991,
     'gla_ba_f': 3.733,
     'gla_ba_b': 4.099,
     'gla_onorm': 5.076,
     'mla_q_norm': 8.0,
     'mla_kv_norm': 8.0,
     'q_head_norm': 8.0,
     'k_head_norm': 8.0,
     'g_ffn': 3.82}
    for name, (base, spread) in spreads.items():
        noise = np.random.default_rng([zlib.crc32(name.encode()), seed]).standard_normal(out[name].shape)
        drawn = base * np.exp(spread * noise) if base else spread * noise
        out[name] = __import__('jax').numpy.asarray(drawn.astype(out[name].dtype))
    for name, factor in factors.items():
        out[name] = (out[name] * factor).astype(out[name].dtype)
    return out
```

```python
import math
from contextlib import ExitStack

import numpy as np

import concourse.bass as bass
from concourse import mybir

P = 128
F32 = mybir.dt.float32
F32R = mybir.dt.float32r
I32 = mybir.dt.int32
U32 = mybir.dt.uint32
ALU = mybir.AluOpType
ACT = mybir.ActivationFunctionType
AX = mybir.AxisListType.X

S = 1024
D = 1024
NT = S // P
KD = D // P
HALF = 512
GH, DK, DV, RANK, CH = 4, 128, 256, 16, 64
NCH = S // CH
GATE_DIV = 16.0
MH, NOPE, ROPE, MV = 8, 128, 64, 128
HQ = NOPE + ROPE
QR, KVR = 384, 256
RH = ROPE // 2
NE, CAP, FF = 16, 128, 1024
EPS = 1e-6
BIG = 3.0e38
UNIT = 1024
UNITS = 24
RING = 12
FIRST = 16
TURN = ([("d", 0, k) for k in range(4)] + [(m, 0, k) for k in range(4) for m in "gu"]
        + [("d", 1, k) for k in range(4)] + [(m, 1, k) for k in range(4) for m in "gu"])
LEAD = 3
CREDIT = 1
C_Q, C_K, C_V, C_R = 0, 512, 1024, 2048
C_LAT = 3072
LAT = 2 * RANK + QR + KVR + ROPE
LA = 2 * RANK + QR
LB = KVR + ROPE
C_GA = C_LAT + LAT
C_GB = C_GA + D


class Steps:

    def __init__(self, eng, sem, base=0, turn=0, per=0):
        self.eng, self.sem, self.base, self.turn, self.per, self.n = eng, sem, base, turn, per, 0

    def mark(self, ins):
        ins.then_inc(self.sem, 1)
        self.n += 1
        return self.n

    def wait(self, n=None):
        self.eng.wait_ge(self.sem, self.turn * self.per + self.base + (self.n if n is None else n))

    def link(self, ins):
        self.mark(ins)
        self.wait()

    def end(self):
        assert self.n == self.per, (self.n, self.per)


def rope_frequencies():
    return [float(np.float32(10000.0 ** (-j / RH))) for j in range(RH)]


def hybrid_layer(nc, x, positions, g_mix, w_in, gla_wa2_f, gla_ba_f, gla_wa2_b, gla_ba_b, gla_onorm,
                 w_gla_out, mla_q_norm, w_uq, mla_kv_norm, w_ukv, q_head_norm, k_head_norm,
                 w_mla_out, w_o, g_ffn, w_router, w_gate_e, w_up_e, w_down_e, out):
    x_rows = x[0]
    out_rows = out[0]
    h2_dram = nc.dram_tensor("h2_rows", (S, D), F32, kind="Internal").ap()
    oa_dram = nc.dram_tensor("gla_out_T", (KD, P, S), F32, kind="Internal").ap()
    ob_dram = nc.dram_tensor("mla_out_T", (KD, P, S), F32, kind="Internal").ap()

    def col(v, n):
        return v.rearrange("(k p) -> p k", p=P) if n > 1 else v.rearrange("(p a) -> p a", a=1)

    def spread(v, n):
        return v.rearrange("(a n) -> a n", a=1).broadcast_to((P, n))

    w_in_k = w_in.rearrange("(k p) n -> p k n", p=P)
    w_uq_k = w_uq.rearrange("(k p) n -> p k n", p=P)
    w_ukv_k = w_ukv.rearrange("(k p) n -> p k n", p=P)
    w_go_k = w_gla_out.rearrange("(k p) n -> p k n", p=P)
    w_mo_k = w_mla_out.rearrange("(k p) n -> p k n", p=P)
    w_o_k = w_o.rearrange("(k p) n -> p k n", p=P)

    with ExitStack() as ctx:
        def sb_in(stack, name, shape, dt=F32):
            return stack.enter_context(nc.sbuf_tensor(name, shape, dt))

        def sb(name, shape, dt=F32):
            return sb_in(ctx, name, shape, dt)

        def sem(name):
            return ctx.enter_context(nc.semaphore(name))

        ps = ctx.enter_context(nc.psum_tensor("ps", [P, 8, HALF], F32))

        ident = sb("ident", [P, P])
        g_mix_c = sb("g_mix_c", [P, KD])
        qn_c = sb("qn_c", [P, QR // P])
        kvn_c = sb("kvn_c", [P, KVR // P])
        onorm_c = sb("onorm_c", [P, DV // P])
        qhn_c = sb("qhn_c", [P, 1])
        khn_c = sb("khn_c", [P, 1])
        qhr_b = sb("qhr_b", [P, ROPE])
        khr_b = sb("khr_b", [P, ROPE])
        minus_half = sb("minus_half", [P, NT])
        stat = sb("stat", [P, 16, NT])
        idx_c = sb("idx_c", [P, NE], U32)
        val_c = sb("val_c", [P, NE])
        w_router_s = sb("w_router_s", [P, KD, NE])

        mix_mem = ExitStack()
        with mix_mem:
            hT = sb_in(mix_mem, "hT", [P, KD, S])
            gateT = sb_in(mix_mem, "gateT", [RANK, 2, S])

            gla_mem = ExitStack()
            with gla_mem:
                w_qk = sb_in(gla_mem, "w_qk", [P, KD, 2 * DK])
                w_vr = sb_in(gla_mem, "w_vr", [P, KD, 2 * DV])
                w_a2 = sb_in(gla_mem, "w_a2", [RANK, 2, DK])
                b_a2 = sb_in(gla_mem, "b_a2", [P, 2])
                mla_mem = ExitStack()
                with mla_mem:
                    cqT = sb_in(mla_mem, "cqT", [P, QR // P, S])
                    ckvT = sb_in(mla_mem, "ckvT", [P, KVR // P, S])
                    k_rot = sb_in(mla_mem, "k_rot", [P, NT, ROPE])
                    cos_t = sb_in(mla_mem, "cos_t", [P, NT, RH])
                    sin_t = sb_in(mla_mem, "sin_t", [P, NT, RH])
                    freq = sb_in(mla_mem, "freq", [P, RH])
                    w_uq_h = sb_in(mla_mem, "w_uq_h", [P, QR // P, HQ])
                    w_ukv_h = sb_in(mla_mem, "w_ukv_h", [P, KVR // P, NOPE + MV])
                    lat_mem = ExitStack()
                    with lat_mem:
                        xs = sb_in(lat_mem, "xs", [P, NT, D])
                        w_lat = sb_in(lat_mem, "w_lat", [P, KD, LAT])
                        lat_r = sb_in(lat_mem, "lat_r", [P, NT, LAT])
                        sq_a = sb_in(lat_mem, "sq_a", [P, D])
                        pos_i = sb_in(lat_mem, "pos_i", [P, NT], I32)
                        pos_f = sb_in(lat_mem, "pos_f", [P, NT])
                        ang = sb_in(lat_mem, "ang", [P, NT, RH])
                        turns_f = sb_in(lat_mem, "turns_f", [P, 2, NT, RH])
                        turns_i = sb_in(lat_mem, "turns_i", [P, 2, NT, RH], I32)
                        k_tmp = sb_in(lat_mem, "k_tmp", [P, 3, NT, RH])
                    head_mem = ExitStack()
                    with head_mem:
                        qR = sb_in(head_mem, "qR", [P, NT, HQ])
                        kvR = sb_in(head_mem, "kvR", [P, NT, NOPE + MV])
                        kRr = sb_in(head_mem, "kRr", [P, NT, ROPE])
                        sq_q = sb_in(head_mem, "sq_q", [P, NT, HQ])
                        r_tmp = sb_in(head_mem, "r_tmp", [P, 4, NT, RH])
                        qT = sb_in(head_mem, "qT", [P, S])
                        kT = sb_in(head_mem, "kT", [P, S])
                        qTr = sb_in(head_mem, "qTr", [ROPE, S])
                        kTr = sb_in(head_mem, "kTr", [ROPE, S])
                        vS = sb_in(head_mem, "vS", [P, NT, MV])
                        probs = sb_in(head_mem, "probs", [P, 3, S])
                        probsT = sb_in(head_mem, "probsT", [P, 2, NT, HALF])
                        obS = sb_in(head_mem, "obS", [P, S])
                        row_max = sb_in(head_mem, "row_max", [P, NT])
                        row_sum = sb_in(head_mem, "row_sum", [P, NT])
                        row_inv = sb_in(head_mem, "row_inv", [P, NT])
                gla_tmp = ExitStack()
                with gla_tmp:
                    qk_T = sb_in(gla_tmp, "qk_T", [P, 2, S])
                    vr = sb_in(gla_tmp, "vr", [P, NT, 2 * DV])
                    qt = sb_in(gla_tmp, "qt", [P, 2, S])
                    kt = sb_in(gla_tmp, "kt", [P, 2, S])
                    kd = sb_in(gla_tmp, "kd", [P, 2, S])
                    zT = sb_in(gla_tmp, "zT", [P, S])
                    eT = sb_in(gla_tmp, "eT", [P, S])
                    bT = sb_in(gla_tmp, "bT", [P, S])
                    decay = sb_in(gla_tmp, "decay", [P, 2, NCH])
                    kdR = sb_in(gla_tmp, "kdR", [P, 2, NT, DK])
                    state = sb_in(gla_tmp, "state", [P, 2, NCH, DV])
                    oR = sb_in(gla_tmp, "oR", [P, NT, DV])
                    oaS = sb_in(gla_tmp, "oaS", [P, 2, S])
                    keep_hi = sb_in(gla_tmp, "keep_hi", [P, 2, P])
                    keep_lo = sb_in(gla_tmp, "keep_lo", [P, 2, P])
                    scan_m = sb_in(gla_tmp, "scan_m", [P, S])
                    att = bT[:, :].rearrange("p (t c) -> p t c", t=NT)
                    att_f = zT[:, :].rearrange("p (t c) -> p t c", t=NT)
                    att_b = eT[:, :].rearrange("p (t c) -> p t c", t=NT)
            merge_mem = ExitStack()
            with merge_mem:
                w_cb = sb_in(merge_mem, "w_cb", [P, 4, KD, P])
                mT = sb_in(merge_mem, "mT", [P, KD, S])
                wo_a = sb_in(merge_mem, "wo_a", [P, KD, HALF])
                rows_mem = ExitStack()
                with rows_mem:
                    oaT = sb_in(rows_mem, "oaT", [P, KD, S])
                    obT = sb_in(rows_mem, "obT", [P, KD, S])
                    sg_a = sb_in(rows_mem, "sg_a", [P, S])
                    sg_b = sb_in(rows_mem, "sg_b", [P, S])
                ffn_mem = ExitStack()
                with ffn_mem:
                    x1 = sb_in(ffn_mem, "x1", [P, NT, D])
                    h2 = sb_in(ffn_mem, "h2", [P, NT, D])
                    h2T = sb_in(ffn_mem, "h2T", [P, 2, KD, P])
                    g_ffn_b = sb_in(ffn_mem, "g_ffn_b", [P, D])
            wo_b = hT[:, :, 0:HALF]
        route_mem = ExitStack()
        with route_mem:
            w_raw = sb_in(route_mem, "w_raw", [P, RING, UNIT])
            w_hi = sb_in(route_mem, "w_hi", [P, RING, UNIT], F32R)
            w_lo = sb_in(route_mem, "w_lo", [P, RING, UNIT], F32R)
            aff = sb_in(route_mem, "aff", [P, NT, NE])
            affT = sb_in(route_mem, "affT", [NE, 2, S])
            top_v = sb_in(route_mem, "top_v", [NE, CAP])
            top_i = sb_in(route_mem, "top_i", [NE, CAP], U32)
            top_f = sb_in(route_mem, "top_f", [NE, CAP])
            xe = sb_in(route_mem, "xe", [P, D])
            xeT_hi = sb_in(route_mem, "xeT_hi", [P, KD, CAP], F32R)
            xeT_lo = sb_in(route_mem, "xeT_lo", [P, KD, CAP], F32R)
            silu_g = sb_in(route_mem, "silu_g", [P, 2, HALF])
            act_r = sb_in(route_mem, "act_r", [P, 2, HALF])
            act_T_hi = sb_in(route_mem, "act_T_hi", [P, KD, CAP], F32R)
            act_T_lo = sb_in(route_mem, "act_T_lo", [P, KD, CAP], F32R)
            ye = sb_in(route_mem, "ye", [P, D])
            val_s = sb_in(route_mem, "val_s", [P, 1])

        x_in = [sem(f"x_in{t}") for t in range(NT)]
        small_in = sem("small_in")
        wlat_in = [sem(f"wlat_in{j}") for j in range(2)]
        consts = sem("consts")
        pool_step = sem("pool_step")
        gate_consts = sem("gate_consts")
        dve_a = sem("dve_a")
        act_a = sem("act_a")
        ssq_x = sem("ssq_x")
        ms_x = sem("ms_x")
        rstd_x = sem("rstd_x")
        xn = sem("xn")
        hT_tr = sem("hT_tr")
        hT_dve = sem("hT_dve")
        hT_act = sem("hT_act")
        lat_mm = sem("lat_mm")
        lat_ev = sem("lat_ev")
        lat_sq = sem("lat_sq")
        lat_ms = sem("lat_ms")
        lat_rs = sem("lat_rs")
        lat_n = sem("lat_n")
        lat_tr = sem("lat_tr")
        latT_dve = sem("latT_dve")
        latT_act = sem("latT_act")
        trig_arg = sem("trig_arg")
        trig = sem("trig")
        k_rot_ok = sem("k_rot_ok")

        wu_in = sem("wu_in")
        prj_mm = sem("prj_mm")
        prj_ev = sem("prj_ev")
        head_sq = sem("head_sq")
        head_ms = sem("head_ms")
        head_rs = sem("head_rs")
        head_n = sem("head_n")
        head_step = sem("head_step")
        seam_tr = sem("seam_tr")
        seam_dve = sem("seam_dve")
        seam_act = sem("seam_act")
        v_ok = sem("v_ok")
        s_mm = sem("s_mm")
        max_ok = sem("max_ok")
        exp_ok = sem("exp_ok")
        inv_ok = sem("inv_ok")
        p_ok = sem("p_ok")
        p_tr = sem("p_tr")
        pt_dve = sem("pt_dve")
        pt_act = sem("pt_act")
        pv_mm = sem("pv_mm")
        ob_ev = sem("ob_ev")
        ob_out = sem("ob_out")

        wqk_in = sem("wqk_in")
        wvr_in = sem("wvr_in")
        wa_in = sem("wa_in")
        qk_mm = sem("qk_mm")
        qk_ev = sem("qk_ev")
        z_mm = sem("z_mm")
        z_dve = sem("z_dve")
        z_act = sem("z_act")
        gla_step = sem("gla_step")
        ls_ok = sem("ls_ok")
        b_ok = sem("b_ok")
        e_ok = sem("e_ok")
        tail_ok = sem("tail_ok")
        ed_ok = sem("ed_ok")
        mats_ok = sem("mats_ok")
        vr_mm = sem("vr_mm")
        vr_ev = sem("vr_ev")
        silu_ok = sem("silu_ok")
        att_mm = sem("att_mm")
        att_ok = sem("att_ok")
        kd_tr = sem("kd_tr")
        kd_ev = sem("kd_ev")
        ds_mm = sem("ds_mm")
        st_ok = sem("st_ok")
        o_mm = sem("o_mm")
        o_ev = sem("o_ev")
        o_sq = sem("o_sq")
        o_ms = sem("o_ms")
        o_rs = sem("o_rs")
        o_n = sem("o_n")
        o_tr = sem("o_tr")
        oa_dve = sem("oa_dve")
        oa_act = sem("oa_act")
        oa_out = sem("oa_out")

        oT_in = sem("oT_in")
        wcb_in = [sem(f"wcb_in{j}") for j in range(4)]
        woa_in = sem("woa_in")
        wob_in = sem("wob_in")
        e_mm = sem("e_mm")
        sg_ok = sem("sg_ok")
        e_dve = sem("e_dve")
        x1_in = sem("x1_in")
        gf_in = sem("gf_in")
        f_mm = sem("f_mm")
        f_ev = sem("f_ev")
        x1_sq = sem("x1_sq")
        x1_ms = sem("x1_ms")
        x1_rs = sem("x1_rs")
        h2_half = sem("h2_half")
        h2_ok = sem("h2_ok")
        rows_out = sem("rows_out")
        h2_tr = sem("h2_tr")
        h2T_dve = sem("h2T_dve")
        h2T_act = sem("h2T_act")
        lg_mm = sem("lg_mm")
        soft = sem("soft")
        soft_exp = sem("soft_exp")
        aff_tr = sem("aff_tr")
        affT_ok = sem("affT_ok")
        top_ok = sem("top_ok")
        top_tr = sem("top_tr")
        idx_ok = sem("idx_ok")

        raw_in = [sem(f"raw_in{j}") for j in range(RING)]
        hi_ok = sem("hi_ok")
        lo_ok = sem("lo_ok")
        w_used = sem("w_used")
        xe_in = sem("xe_in")
        xe_tr = sem("xe_tr")
        xeT_hi_ok = sem("xeT_hi_ok")
        xeT_lo_ok = sem("xeT_lo_ok")
        gu_mm = sem("gu_mm")
        silu_e = sem("silu_e")
        act_ok = sem("act_ok")
        a_tr = sem("a_tr")
        aT_hi_ok = sem("aT_hi_ok")
        aT_lo_ok = sem("aT_lo_ok")
        d_mm = sem("d_mm")
        val_ok = sem("val_ok")
        ye_ok = sem("ye_ok")
        ye_out = sem("ye_out")
        ye_free = sem("ye_free")

        block = ctx.enter_context(nc.Block())
        small_loads = 10

        @block.sync
        def _(sp):
            for t in range(NT):
                sp.dma_start(xs[:, t, :], x_rows[t * P:(t + 1) * P, :]).then_inc(x_in[t], 16)
            for j in range(2):
                k0, k1 = j * KD // 2, (j + 1) * KD // 2
                sp.dma_start(w_lat[:, k0:k1, :], w_in_k[:, k0:k1, C_LAT:C_LAT + LAT]).then_inc(wlat_in[j], 16)

            def load_up(h):
                sp.dma_start(w_uq_h[:], w_uq_k[:, :, bass.ds(h * HQ, HQ)]).then_inc(wu_in, 16)
                sp.dma_start(w_ukv_h[:], w_ukv_k[:, :, bass.ds(h * (NOPE + MV), NOPE + MV)]).then_inc(wu_in, 16)

            def load_qk(h):
                sp.dma_start(w_qk[:, :, 0:DK], w_in_k[:, :, bass.ds(C_Q + h * DK, DK)]).then_inc(wqk_in, 16)
                sp.dma_start(w_qk[:, :, DK:2 * DK], w_in_k[:, :, bass.ds(C_K + h * DK, DK)]).then_inc(wqk_in, 16)

            def load_vr(h):
                sp.dma_start(w_vr[:, :, 0:DV], w_in_k[:, :, bass.ds(C_V + h * DV, DV)]).then_inc(wvr_in, 16)
                sp.dma_start(w_vr[:, :, DV:2 * DV], w_in_k[:, :, bass.ds(C_R + h * DV, DV)]).then_inc(wvr_in, 16)

            def load_a2(h):
                sp.dma_start(w_a2[:, 0, :], gla_wa2_f[:, bass.ds(h * DK, DK)]).then_inc(wa_in, 16)
                sp.dma_start(w_a2[:, 1, :], gla_wa2_b[:, bass.ds(h * DK, DK)]).then_inc(wa_in, 16)
                for d, b in enumerate((gla_ba_f, gla_ba_b)):
                    sp.dma_start(b_a2[:, d:d + 1], b[bass.ds(h * DK, DK)].rearrange("(p a) -> p a", a=1),
                                 allow_slow_non_contiguous=True).then_inc(wa_in, 16)

            load_up(0)
            load_qk(0)
            load_vr(0)
            load_a2(0)

            def mla_turn(h, last):
                if not last:
                    sp.wait_ge(prj_mm, h * 8 + 8)
                    load_up(h + 1)
                for j in range(2):
                    sp.wait_ge(ob_ev, h * 2 + j + 1 + CREDIT)
                    sp.dma_start(ob_dram[bass.ds(h, 1), :, j * HALF:(j + 1) * HALF].rearrange("a p s -> p (a s)"),
                                 obS[:, j * HALF:(j + 1) * HALF]).then_inc(ob_out, 16)

            with sp.Fori(0, MH - 1) as h:
                mla_turn(h, False)
            mla_turn(MH - 1, True)

            def gla_turn(h, last):
                if not last:
                    sp.wait_ge(qk_mm, h * 4 + 4)
                    load_qk(h + 1)
                    sp.wait_ge(z_dve, h * 2 + 2)
                    load_a2(h + 1)
                    sp.wait_ge(vr_mm, h * NT + NT)
                    load_vr(h + 1)
                sp.wait_ge(oa_dve, h * 2 + 2 + CREDIT)
                sp.wait_ge(oa_act, h * 2 + 2 + CREDIT)
                sp.dma_start(oa_dram[bass.ds(h * 2, 2)].rearrange("a p s -> p a s"), oaS[:]).then_inc(oa_out, 16)

            with sp.Fori(0, GH - 1) as h:
                gla_turn(h, False)
            gla_turn(GH - 1, True)

            sp.wait_ge(oa_out, 16 * GH + CREDIT)
            sp.wait_ge(ob_out, 32 * MH + CREDIT)

            def load_cb(col, j):
                src = (w_in_k[:, :, C_GA:C_GB], w_go_k, w_in_k[:, :, C_GB:C_GB + D], w_mo_k)[j]
                src = src[:, :, bass.ds(col, P)]
                sp.dma_start(w_cb[:, j], src).then_inc(wcb_in[j], 16)

            for j in range(4):
                load_cb(0, j)
                if j == 0:
                    sp.dma_start(oaT[:], oa_dram.rearrange("k p s -> p k s")).then_inc(oT_in, 16)
                if j == 2:
                    sp.dma_start(obT[:], ob_dram.rearrange("k p s -> p k s")).then_inc(oT_in, 16)
            sp.dma_start(wo_a[:], w_o_k[:, :, 0:HALF]).then_inc(woa_in, 16)
            with sp.Fori(0, KD - 1) as cb:
                for j in (0, 2):
                    sp.wait_ge(e_mm, cb * 4 + j + 2)
                    load_cb((cb + 1) * P, j)
                    load_cb((cb + 1) * P, j + 1)
            sp.wait_ge(e_mm, KD * 4)
            sp.dma_start(wo_b, w_o_k[:, :, HALF:D]).then_inc(wob_in, 16)
            sp.wait_ge(e_dve, KD * 3 + CREDIT)
            sp.dma_start(g_ffn_b[:], spread(g_ffn, D)).then_inc(gf_in, 16)
            for t in range(NT):
                sp.dma_start(x1[:, t, :], x_rows[t * P:(t + 1) * P, :]).then_inc(x1_in, 16)
            for t in range(NT):
                sp.wait_ge(h2_ok, t + 1)
                sp.dma_start(h2_dram[t * P:(t + 1) * P, :], h2[:, t, :]).then_inc(rows_out, 16)
                sp.dma_start(out_rows[t * P:(t + 1) * P, :], x1[:, t, :]).then_inc(rows_out, 16)
            sp.wait_ge(rows_out, 32 * NT)

            def load_unit(e, unit, n, turn=0):
                m, j, k = unit
                if n >= RING:
                    sp.wait_ge(lo_ok, turn * UNITS + n - RING + 1)
                w = {"g": w_gate_e, "u": w_up_e, "d": w_down_e}[m]
                src = w[bass.ds(e, 1)].rearrange("a (k p) f -> p (a k) f", p=P)
                if m == "d":
                    src = src[:, 4 * j + k, :]
                    dst = w_raw[:, n % RING, :]
                else:
                    src = src[:, 2 * k:2 * k + 2, j * HALF:(j + 1) * HALF]
                    dst = w_raw[:, n % RING, :].rearrange("p (a c) -> p a c", a=2)
                sp.dma_start(dst, src).then_inc(raw_in[n % RING], 16)

            sp.wait_ge(lg_mm, NT)
            first = TURN[4:12] + TURN[16:24]
            for n in range(FIRST):
                load_unit(0, first[n], n)
            with sp.Fori(0, NE - 1) as e:
                for u, unit in enumerate(TURN):
                    load_unit(e if unit[0] == "d" else e + 1, unit, FIRST + u, e)
            for u, unit in enumerate(TURN[0:4] + TURN[12:16]):
                load_unit(NE - 1, unit, FIRST + (NE - 1) * UNITS + u)

        @block.gpsimd
        def _(pool):
            for s in (ob_ev, pt_dve, pt_act, oa_dve, oa_act, sg_ok, e_dve, ye_ok, ob_out, oa_out, ye_free):
                pool.sem_inc(s, CREDIT)
            st = Steps(pool, pool_step)
            pool.memset(minus_half[:], -0.5).then_inc(consts, 1)
            st.link(pool.memset(ident[:], 0.0))
            pool.affine_select(out=ident[:], in_=ident[:], compare_op=ALU.not_equal, fill=1.0, base=0,
                               pattern=[[-1, P]], channel_multiplier=1).then_inc(consts, 1)
            for j, f in enumerate(rope_frequencies()):
                ins = pool.memset(freq[:, j:j + 1], f)
            ins.then_inc(consts, 1)

            def rsqrt(dst, ready, count, done):
                pool.wait_ge(ready, count)
                pool.tensor_tensor(dst, dst, minus_half[:, 0:dst.shape[1]], ALU.pow).then_inc(done, 1)

            pool.wait_ge(consts, 3)
            for t in range(NT):
                rsqrt(stat[:, 0, t:t + 1], ms_x, t + 1, rstd_x)
            for t in range(NT):
                rsqrt(stat[:, 1:3, t], lat_ms, t + 1, lat_rs)
            for h in range(MH):
                rsqrt(stat[:, 4, :], head_ms, 2 * h + 1, head_rs)
                rsqrt(stat[:, 5, :], head_ms, 2 * h + 2, head_rs)
            pool.wait_ge(pv_mm, 2 * MH)
            pool.wait_ge(ob_out, 32 * MH + CREDIT)
            st.mark(pool.memset(keep_hi[:], BIG))
            st.link(pool.memset(scan_m[:], 1.0))
            st.mark(pool.memset(scan_m[:, 0:S:CH], 0.0))
            st.mark(pool.affine_select(out=keep_hi[:, 0, :], in_=keep_hi[:, 0, :], compare_op=ALU.is_ge, fill=0.0,
                                       base=0, pattern=[[1, P]], channel_multiplier=-1))
            st.link(pool.affine_select(out=keep_hi[:, 1, :], in_=keep_hi[:, 1, :], compare_op=ALU.is_gt, fill=0.0,
                                       base=0, pattern=[[-1, P]], channel_multiplier=1))
            st.mark(pool.memset(keep_hi[0:CH, 0, CH:P], 0.0))
            st.link(pool.memset(keep_hi[CH:P, 1, 0:CH], 0.0))
            pool.tensor_scalar(keep_lo[:], keep_hi[:], -1.0, 0.0, ALU.mult, ALU.add).then_inc(gate_consts, 1)
            for h in range(GH):
                for j in range(2):
                    rsqrt(stat[:, 6, 4 * j:4 * j + 4], o_ms, 2 * h + j + 1, o_rs)
            for t in range(NT):
                rsqrt(stat[:, 7, t:t + 1], x1_ms, t + 1, x1_rs)

            pool.wait_ge(idx_ok, 2)
            pool.wait_ge(rows_out, 32 * NT)

            def gather(e):
                if e:
                    pool.wait_ge(xe_tr, 2 * e)
                pool.indirect_dma_start(xe[:], None, h2_dram,
                                        bass.IndirectOffsetOnAxis(ap=idx_c[:, e:e + 1], axis=0)).then_inc(xe_in, 16)

            gather(0)
            for e in range(NE):
                if e + 1 < NE:
                    gather(e + 1)
                if e:
                    pool.wait_ge(ye_out, 16 * e)
                    pool.sem_inc(ye_free, 1)
                pool.wait_ge(ye_ok, e + 1 + CREDIT)
                pool.indirect_dma_start(out_rows, bass.IndirectOffsetOnAxis(ap=idx_c[:, e:e + 1], axis=0),
                                        ye[:], None, compute_op=ALU.add).then_inc(ye_out, 16)
            pool.wait_ge(ye_out, 16 * NE)

        @block.tensor
        def _(pe):
            def transpose4(bank, rows, srcs):
                for j, src in enumerate(srcs):
                    ins = pe.transpose(ps[0:rows, bank, j * P:(j + 1) * P], src, ident[:])
                return ins

            pe.wait_ge(consts, 3)
            for c in range(2 * KD):
                half, k = divmod(c, KD)
                pe.wait_ge(xn, 4 * half + 4)
                if c >= 4:
                    pe.wait_ge(hT_dve if c % 2 == 0 else hT_act, (c - 4) // 2 + 1)
                transpose4(c % 4, P, [xs[:, 4 * half + j, k * P:(k + 1) * P] for j in range(4)]).then_inc(hT_tr, 1)

            for t in range(NT):
                pe.wait_ge(hT_dve, 4 * (t // 4) + 4)
                pe.wait_ge(hT_act, 4 * (t // 4) + 4)
                if t >= 2:
                    pe.wait_ge(lat_ev, t - 1)
                a, b = 4 + 2 * (t % 2), 5 + 2 * (t % 2)
                for k in range(KD):
                    if t == 0 and k % 4 == 0:
                        pe.wait_ge(wlat_in[k // 4], 16)
                    lhs = hT[:, k, t * P:(t + 1) * P]
                    pe.matmul(ps[:, a, 0:LA], lhs, w_lat[:, k, 0:LA], start=k == 0, stop=k == KD - 1)
                    mm = pe.matmul(ps[:, b, 0:LB], lhs, w_lat[:, k, LA:LAT], start=k == 0, stop=k == KD - 1)
                mm.then_inc(lat_mm, 1)
            for c in range(14):
                half, j = divmod(c, 7)
                pe.wait_ge(lat_n, 4 * half + 4)
                if c >= 4:
                    pe.wait_ge(latT_dve if c % 2 == 0 else latT_act, (c - 4) // 2 + 1)
                lo = (0, RANK)[j] if j < 2 else 2 * RANK + (j - 2) * P
                w = RANK if j < 2 else P
                transpose4(c % 4, w, [lat_r[:, 4 * half + t, lo:lo + w] for t in range(4)]).then_inc(lat_tr, 1)

            pe.wait_ge(latT_dve, 7)
            pe.wait_ge(latT_act, 7)
            pe.wait_ge(lat_ev, NT)

            def project(n, g):
                if g == 0:
                    pe.wait_ge(wu_in, n * 32 + 32)
                pe.wait_ge(prj_ev, n * 8 + g)
                width = HQ if g < 4 else NOPE + MV
                src, w, kc = (cqT, w_uq_h, QR // P) if g < 4 else (ckvT, w_ukv_h, KVR // P)
                for j in range(2):
                    t = 2 * (g % 4) + j
                    for k in range(kc):
                        mm = pe.matmul(ps[:, 7, j * width:(j + 1) * width], src[:, k, t * P:(t + 1) * P], w[:, k, :],
                                       start=k == 0, stop=k == kc - 1)
                mm.then_inc(prj_mm, 1)

            for g in range(8):
                project(0, g)

            def mla_head(i, last):
                pe.wait_ge(prj_ev, i * 8 + 8)
                pe.wait_ge(ob_ev, i * 2 + CREDIT)
                for c in range(8):
                    what, half = divmod(c, 2)
                    if c in (0, 4):
                        pe.wait_ge(head_n, i * 2 + c // 4 + 1)
                    srcs = []
                    for j in range(4):
                        t = 4 * half + j
                        srcs.append((qR[:, t, 0:NOPE], qR[:, t, NOPE:HQ], kvR[:, t, 0:NOPE], kRr[:, t, :])[what])
                    transpose4((4 + c) % 8, NOPE if what % 2 == 0 else ROPE, srcs).then_inc(seam_tr, 1)
                pe.wait_ge(seam_dve, i * 4 + 4)
                pe.wait_ge(seam_act, i * 4 + 4)
                for n in range(10):
                    if n < 8:
                        if n >= 2:
                            pe.wait_ge(exp_ok, i * 8 + n - 1)
                        for j in range(2):
                            cols = slice(j * HALF, (j + 1) * HALF)
                            bank = ps[:, 2 * (n % 2) + j, :]
                            pe.matmul(bank, qT[:, n * P:(n + 1) * P], kT[:, cols], start=True, stop=False)
                            mm = pe.matmul(bank, qTr[:, n * P:(n + 1) * P], kTr[:, cols], start=False, stop=True)
                        mm.then_inc(s_mm, 1)
                        if not last:
                            project(i + 1, n)
                    if n >= 2:
                        q = n - 2
                        pe.wait_ge(p_ok, i * 8 + q + 1)
                        pe.wait_ge(pt_dve, i * 8 + q + CREDIT)
                        pe.wait_ge(pt_act, i * 8 + q + CREDIT)
                        for b in range(2):
                            transpose4(4 + b, P, [probs[:, q % 3, (4 * b + j) * P:(4 * b + j + 1) * P]
                                                  for j in range(4)]).then_inc(p_tr, 1)
                    if n in (5, 9):
                        j = (n - 5) // 4
                        pe.wait_ge(pt_dve, i * 8 + 4 * j + 4 + CREDIT)
                        pe.wait_ge(pt_act, i * 8 + 4 * j + 4 + CREDIT)
                        if j == 0:
                            pe.wait_ge(v_ok, i + 1)
                        else:
                            pe.wait_ge(ob_ev, i * 2 + 1 + CREDIT)
                        for k in range(NT):
                            mm = pe.matmul(ps[:, 6, :], vS[:, k, :], probsT[:, j, k, :], start=k == 0, stop=k == NT - 1)
                        mm.then_inc(pv_mm, 1)

            with pe.Fori(0, MH - 1) as i:
                mla_head(i, False)
            mla_head(MH - 1, True)

            pe.wait_ge(ob_ev, 2 * MH + CREDIT)

            def gla_head(h):
                pe.wait_ge(wqk_in, h * 32 + 32)
                for j in range(2):
                    for half in range(2):
                        for k in range(KD):
                            mm = pe.matmul(ps[:, 2 * j + half, :], w_qk[:, k, j * DK:(j + 1) * DK],
                                           hT[:, k, half * HALF:(half + 1) * HALF], start=k == 0, stop=k == KD - 1)
                        mm.then_inc(qk_mm, 1)
                pe.wait_ge(wa_in, h * 64 + 64)
                pe.wait_ge(oa_dve, h * 2 + CREDIT)
                pe.wait_ge(oa_act, h * 2 + CREDIT)
                for d in range(2):
                    for half in range(2):
                        mm = pe.matmul(ps[:, 4 + 2 * d + half, :], w_a2[:, d, :],
                                       gateT[:, d, half * HALF:(half + 1) * HALF], start=True, stop=True)
                    mm.then_inc(z_mm, 1)
                pe.wait_ge(wvr_in, h * 32 + 32)
                for t in range(NT):
                    if t < 4:
                        pe.wait_ge(qk_ev, h * 4 + t + 1)
                    else:
                        pe.wait_ge(vr_ev, h * NT + t - 3)
                    for k in range(KD):
                        mm = pe.matmul(ps[:, t % 4, :], hT[:, k, t * P:(t + 1) * P], w_vr[:, k, :],
                                       start=k == 0, stop=k == KD - 1)
                    mm.then_inc(vr_mm, 1)
                for d in range(2):
                    pe.wait_ge(mats_ok, h * 6 + 3 * d + 3)
                    for half in range(2):
                        c = 2 * d + half
                        pe.wait_ge(vr_ev, h * NT + c + 5)
                        transpose4(c, P, [kd[:, d, (4 * half + j) * P:(4 * half + j + 1) * P]
                                          for j in range(4)]).then_inc(kd_tr, 1)
                for half in range(2):
                    for d in range(2):
                        for j in range(4):
                            cols = slice((4 * half + j) * P, (4 * half + j + 1) * P)
                            mm = pe.matmul(ps[:, 4 + 2 * half + d, j * P:(j + 1) * P], kt[:, d, cols], qt[:, d, cols],
                                           start=True, stop=True)
                        mm.then_inc(att_mm, 1)
                pe.wait_ge(kd_ev, h * 4 + 4)
                pe.wait_ge(att_ok, h * 10 + 10)
                for n in range(30):
                    d, c = (1, NCH - 1 - n) if n < 15 else (0, n - 15)
                    if n >= 4:
                        pe.wait_ge(st_ok, h * 32 + n - 1)
                    r0 = CH * (c % 2)
                    mm = pe.matmul(ps[:, 4 + n % 4, 0:DV],
                                   kdR[r0:r0 + CH, d, c // 2, :], vr[r0:r0 + CH, c // 2, 0:DV], start=True, stop=True)
                    mm.then_inc(ds_mm, 1)
                for t in range(NT):
                    pe.wait_ge(st_ok, h * 32 + 17 + min(2 * t + 1, NCH - 1))
                    if t >= 4:
                        pe.wait_ge(o_ev, h * NT + t - 3)
                    pe.matmul(ps[:, t % 4, 0:DV], att[:, t, :], vr[:, t, 0:DV], start=True, stop=False,
                              skip_group_check=True)
                    for c in (2 * t, 2 * t + 1):
                        r0 = CH * (c % 2)
                        for d in range(2):
                            mm = pe.matmul(ps[r0:r0 + CH, t % 4, 0:DV], qt[:, d, c * CH:(c + 1) * CH],
                                           state[:, d, c, :], start=False, stop=True, skip_group_check=True)
                    mm.then_inc(o_mm, 1)
                for c in range(4):
                    half, j = divmod(c, 2)
                    pe.wait_ge(o_n, h * 2 + half + 1)
                    transpose4(4 + c, P, [oR[:, 4 * half + t, j * P:(j + 1) * P] for t in range(4)]).then_inc(o_tr, 1)

            with pe.Fori(0, GH) as h:
                gla_head(h)

            pe.wait_ge(oa_dve, 2 * GH + CREDIT)
            pe.wait_ge(oa_act, 2 * GH + CREDIT)

            with pe.Fori(0, KD) as cb:
                for j in range(4):
                    pe.wait_ge(wcb_in[j], cb * 16 + 16)
                    if j % 2 == 0:
                        pe.wait_ge(sg_ok, cb * 2 + j // 2 + CREDIT)
                        rhs = hT
                    else:
                        pe.wait_ge(e_dve, cb * 3 + CREDIT)
                        rhs = oaT if j == 1 else obT
                        pe.wait_ge(oT_in, 32)
                    for half in range(2):
                        for k in range(KD):
                            mm = pe.matmul(ps[:, 2 * j + half, :], w_cb[:, j, k, :],
                                           rhs[:, k, half * HALF:(half + 1) * HALF], start=k == 0, stop=k == KD - 1)
                    mm.then_inc(e_mm, 1)

            pe.wait_ge(e_dve, 3 * KD + CREDIT)
            pe.wait_ge(woa_in, 16)
            for g in range(2):
                for half in range(2):
                    if half:
                        pe.wait_ge(wob_in, 16)
                    w = wo_b if half else wo_a
                    for j in range(4):
                        t = 4 * g + j
                        if g:
                            pe.wait_ge(f_ev, 4 * half + j + 1)
                        for k in range(KD):
                            mm = pe.matmul(ps[:, 4 * half + j, :], mT[:, k, t * P:(t + 1) * P], w[:, k, :],
                                           start=k == 0, stop=k == KD - 1)
                        mm.then_inc(f_mm, 1)

            pe.wait_ge(f_ev, 16)

            def rows_T(t):
                pe.wait_ge(h2_ok, t + 1)
                if t >= 2:
                    pe.wait_ge(h2T_dve, t - 1)
                    pe.wait_ge(h2T_act, t - 1)
                for b in range(2):
                    transpose4(2 * (t % 2) + b, P, [h2[:, t, (4 * b + j) * P:(4 * b + j + 1) * P]
                                                    for j in range(4)]).then_inc(h2_tr, 1)

            def logits(t):
                pe.wait_ge(h2T_dve, t + 1)
                pe.wait_ge(h2T_act, t + 1)
                for k in range(KD):
                    mm = pe.matmul(ps[:, 7, t * NE:(t + 1) * NE], h2T[:, t % 2, k, :], w_router_s[:, k, :],
                                   start=k == 0, stop=k == KD - 1)
                mm.then_inc(lg_mm, 1)

            for t in range(NT + 1):
                if t < NT:
                    rows_T(t)
                if t:
                    logits(t - 1)
            pe.wait_ge(soft, 5)
            for t in range(NT):
                mm = pe.transpose(ps[0:NE, t // 4, (t % 4) * P:(t % 4 + 1) * P], aff[:, t, :], ident[:])
            mm.then_inc(aff_tr, 1)
            pe.wait_ge(top_ok, 1)
            pe.transpose(ps[:, 2, 0:NE], top_v[:], ident[0:NE, 0:NE])
            pe.transpose(ps[:, 2, NE:2 * NE], top_f[:], ident[0:NE, 0:NE]).then_inc(top_tr, 1)

            def expert_rows_T(e):
                pe.wait_ge(xe_in, e * 16 + 16)
                if not isinstance(e, int):
                    pe.wait_ge(act_ok, e * 2 - 1)
                for b in range(2):
                    transpose4(b, P, [xe[:, (4 * b + j) * P:(4 * b + j + 1) * P] for j in range(4)]).then_inc(xe_tr, 1)

            def three(out_ap, a_hi, a_lo, n, cols, start, stop):
                pe.matmul(out_ap, a_hi, w_hi[:, n % RING, cols], start=start, stop=False)
                pe.matmul(out_ap, a_hi, w_lo[:, n % RING, cols], start=False, stop=False)
                return pe.matmul(out_ap, a_lo, w_hi[:, n % RING, cols], start=False, stop=stop)

            def gate_up(e, j, n, turn=0):
                pe.wait_ge(xeT_lo_ok, e * 2 + 2)
                for u in range(8):
                    pe.wait_ge(lo_ok, turn * UNITS + n + u + 1)
                    for i in range(2):
                        k = u // 2 * 2 + i
                        mm = three(ps[:, 2 * j + u % 2, :], xeT_hi[:, k, :], xeT_lo[:, k, :], n + u,
                                   slice(i * HALF, (i + 1) * HALF), k == 0, k == KD - 1)
                    mm.then_inc(w_used, 1)

            def act_rows_T(e, j):
                pe.wait_ge(act_ok, e * 2 + j + 1)
                transpose4(6 + j, P, [act_r[:, j, c * P:(c + 1) * P] for c in range(4)]).then_inc(a_tr, 1)

            def down(e, j, n, turn=0):
                pe.wait_ge(aT_lo_ok, e * 2 + j + 1)
                if j == 0:
                    pe.wait_ge(ye_ok, e + CREDIT)
                for k in range(4):
                    pe.wait_ge(lo_ok, turn * UNITS + n + k + 1)
                    for half in range(2):
                        mm = three(ps[:, 4 + half, :], act_T_hi[:, 4 * j + k, :], act_T_lo[:, 4 * j + k, :], n + k,
                                   slice(half * HALF, (half + 1) * HALF), j == 0 and k == 0, j == 1 and k == 3)
                    mm.then_inc(w_used, 1)

            expert_rows_T(0)
            gate_up(0, 0, 0)
            gate_up(0, 1, 8)
            with pe.Fori(0, NE - 1) as e:
                act_rows_T(e, 0)
                expert_rows_T(e + 1)
                down(e, 0, FIRST, e)
                act_rows_T(e, 1)
                gate_up(e + 1, 0, FIRST + 4, e)
                down(e, 1, FIRST + 12, e)
                gate_up(e + 1, 1, FIRST + 16, e)
            end = FIRST + (NE - 1) * UNITS
            act_rows_T(NE - 1, 0)
            down(NE - 1, 0, end)
            act_rows_T(NE - 1, 1)
            down(NE - 1, 1, end + 4)

        @block.vector
        def _(dve):
            st = Steps(dve, dve_a)

            def mean_eps(dst, src, n):
                return dve.tensor_scalar(dst, src, 1.0 / n, EPS, ALU.mult, ALU.add)

            dve.wait_ge(small_in, 16 * small_loads)
            scale = 1.0 / math.sqrt(HQ)
            st.mark(dve.tensor_scalar(qhn_c[:], qhn_c[:], scale, None, ALU.mult))
            st.mark(dve.tensor_scalar(qhr_b[:], qhr_b[:], scale, None, ALU.mult))

            def x_scale(t):
                dve.wait_ge(rstd_x, t + 1)
                dve.tensor_scalar(xs[:, t, :], xs[:, t, :], stat[:, 0, t:t + 1], None, ALU.mult).then_inc(xn, 1)

            for t in range(NT):
                dve.wait_ge(ssq_x, t + 1)
                mean_eps(stat[:, 0, t:t + 1], stat[:, 0, t:t + 1], D).then_inc(ms_x, 1)
                if t:
                    x_scale(t - 1)
            x_scale(NT - 1)
            dve.wait_ge(consts, 3)
            st.link(dve.tensor_copy(pos_f[:], pos_i[:]))
            st.link(dve.tensor_tensor(ang[:], pos_f[:].unsqueeze(2).broadcast_to((P, NT, RH)),
                                      freq[:].unsqueeze(1).broadcast_to((P, NT, RH)), ALU.mult))
            two_pi = 2 * math.pi
            part1 = 6.25
            part2 = float(np.float32(round((two_pi - part1) * 2 ** 14) / 2 ** 14))
            part3 = two_pi - part1 - part2
            for j, shift in enumerate((0.0, 0.25)):
                st.mark(dve.tensor_scalar(turns_f[:, j], ang[:], 1 / two_pi, shift, ALU.mult, ALU.add))
            st.wait()
            st.link(dve.tensor_copy(turns_i[:], turns_f[:]))
            st.link(dve.tensor_copy(turns_f[:], turns_i[:]))
            for j, (dst, shift) in enumerate(((sin_t, 0.0), (cos_t, math.pi / 2))):
                st.link(dve.scalar_tensor_tensor(out=dst[:], in0=turns_f[:, j], scalar=-part1, in1=ang[:],
                                                 op0=ALU.mult, op1=ALU.add))
                for part in (part2, part3):
                    st.link(dve.scalar_tensor_tensor(out=dst[:], in0=turns_f[:, j], scalar=-part, in1=dst[:],
                                                     op0=ALU.mult, op1=ALU.add))
                st.link(dve.tensor_scalar(dst[:], dst[:], shift, 3.1415925, ALU.add, ALU.min))
                dve.tensor_scalar(dst[:], dst[:], -3.1415925, None, ALU.max).then_inc(trig_arg, 1)

            for c in range(0, 2 * KD, 2):
                half, k = divmod(c, KD)
                dve.wait_ge(hT_tr, c + 1)
                dve.tensor_scalar(hT[:, k, half * HALF:(half + 1) * HALF], ps[:, c % 4, :], g_mix_c[:, k:k + 1], None,
                                  ALU.mult).then_inc(hT_dve, 1)

            def lat_scale(t):
                dve.wait_ge(lat_rs, t + 1)
                st.mark(dve.tensor_scalar(lat_r[:, t, 2 * RANK:LA], lat_r[:, t, 2 * RANK:LA], stat[:, 1, t:t + 1], None,
                                          ALU.mult))
                dve.tensor_scalar(lat_r[:, t, LA:LA + KVR], lat_r[:, t, LA:LA + KVR], stat[:, 2, t:t + 1], None,
                                  ALU.mult).then_inc(lat_n, 1)

            for t in range(NT):
                a, b = 4 + 2 * (t % 2), 5 + 2 * (t % 2)
                dve.wait_ge(lat_mm, t + 1)
                dve.tensor_copy(lat_r[:, t, 0:LA], ps[:, a, 0:LA])
                dve.tensor_copy(lat_r[:, t, LA:LAT], ps[:, b, 0:LB]).then_inc(lat_ev, 1)
                if t:
                    lat_scale(t - 1)
                dve.wait_ge(lat_sq, t + 1)
                st.mark(mean_eps(stat[:, 1, t:t + 1], stat[:, 1, t:t + 1], QR))
                mean_eps(stat[:, 2, t:t + 1], stat[:, 2, t:t + 1], KVR).then_inc(lat_ms, 1)
            lat_scale(NT - 1)

            def lat_out(c):
                half, j = divmod(c, 7)
                cols = slice(half * HALF, (half + 1) * HALF)
                if j < 2:
                    return gateT[:, j, cols], ps[0:RANK, c % 4, :], 1.0
                if j < 5:
                    return cqT[:, j - 2, cols], ps[:, c % 4, :], qn_c[:, j - 2:j - 1]
                return ckvT[:, j - 5, cols], ps[:, c % 4, :], kvn_c[:, j - 5:j - 4]

            for c in range(0, 14, 2):
                dve.wait_ge(lat_tr, c + 1)
                dst, src, gain = lat_out(c)
                dve.tensor_scalar(dst, src, gain, None, ALU.mult).then_inc(latT_dve, 1)

            def rotate(dst, src, tmp, steps):
                x1r, x2r = src[:, :, 0:RH], src[:, :, RH:ROPE]
                steps.mark(dve.tensor_tensor(tmp[:, 0], x1r, cos_t[:], ALU.mult))
                steps.mark(dve.tensor_tensor(tmp[:, 1], x2r, sin_t[:], ALU.mult))
                steps.mark(dve.tensor_tensor(tmp[:, 2], x2r, cos_t[:], ALU.mult))
                steps.mark(dve.tensor_tensor(tmp[:, 3], x1r, sin_t[:], ALU.mult))
                steps.wait()
                steps.mark(dve.tensor_tensor(dst[:, :, 0:RH], tmp[:, 0], tmp[:, 1], ALU.subtract))
                return dve.tensor_tensor(dst[:, :, RH:ROPE], tmp[:, 2], tmp[:, 3], ALU.add)

            st.link(dve.tensor_tensor(k_rot[:], lat_r[:, :, LA + KVR:LAT],
                                      khr_b[:].unsqueeze(1).broadcast_to((P, NT, ROPE)), ALU.mult))
            dve.wait_ge(trig, 2)
            rotate(k_rot[:], k_rot[:], lat_r[:, 0:4, 0:NT * RH].rearrange("p a (t r) -> p a t r", t=NT), st) \
                .then_inc(k_rot_ok, 1)

            dve.wait_ge(latT_act, 7)

            def q_stats(n, s):
                dve.wait_ge(head_sq, n * 2 + 1)
                s.link(dve.tensor_reduce(stat[:, 4, :], sq_q[:], AX, ALU.add))
                mean_eps(stat[:, 4, :], stat[:, 4, :], HQ).then_inc(head_ms, 1)

            def q_norm(n, s):
                dve.wait_ge(head_rs, n * 2 + 1)
                s.link(dve.tensor_tensor(qR[:], qR[:], stat[:, 4, :].unsqueeze(2).broadcast_to((P, NT, HQ)), ALU.mult))
                s.link(dve.tensor_tensor(qR[:, :, NOPE:HQ], qR[:, :, NOPE:HQ],
                                         qhr_b[:].unsqueeze(1).broadcast_to((P, NT, ROPE)), ALU.mult))
                rotate(qR[:, :, NOPE:HQ], qR[:, :, NOPE:HQ], r_tmp, s).then_inc(head_n, 1)

            def k_stats(n, s):
                dve.wait_ge(head_sq, n * 2 + 2)
                s.link(dve.tensor_reduce(stat[:, 5, :], sq_q[:, :, 0:NOPE], AX, ALU.add))
                s.link(dve.tensor_tensor(stat[:, 5, :], stat[:, 5, :], stat[:, 3, :], ALU.add))
                mean_eps(stat[:, 5, :], stat[:, 5, :], HQ).then_inc(head_ms, 1)

            def k_norm(n, s):
                dve.wait_ge(head_rs, n * 2 + 2)
                s.mark(dve.tensor_tensor(kvR[:, :, 0:NOPE], kvR[:, :, 0:NOPE],
                                         stat[:, 5, :].unsqueeze(2).broadcast_to((P, NT, NOPE)), ALU.mult))
                dve.tensor_tensor(kRr[:], k_rot[:], stat[:, 5, :].unsqueeze(2).broadcast_to((P, NT, ROPE)),
                                  ALU.mult).then_inc(head_n, 1)

            prep = 1 + 1 + 1 + 5 + 1 + 1 + 1
            s0 = Steps(dve, head_step, per=prep)
            dve.wait_ge(lat_sq, NT)
            dve.wait_ge(k_rot_ok, 1)
            q_stats(0, s0)
            q_norm(0, s0)
            k_stats(0, s0)
            k_norm(0, s0)
            s0.end()

            def mla_head(i, last):
                s = Steps(dve, head_step, base=prep, turn=i, per=prep)
                for c in range(0, 8, 2):
                    what = c // 2
                    dve.wait_ge(seam_tr, i * 8 + c + 1)
                    if what == 0:
                        ins = dve.tensor_scalar(qT[:, 0:HALF], ps[:, 4, :], qhn_c[:, 0:1], None, ALU.mult)
                    elif what == 1:
                        ins = dve.tensor_copy(qTr[:, 0:HALF], ps[0:ROPE, 6, :])
                    elif what == 2:
                        ins = dve.tensor_scalar(kT[:, 0:HALF], ps[:, 0, :], khn_c[:, 0:1], None, ALU.mult)
                    else:
                        ins = dve.tensor_copy(kTr[:, 0:HALF], ps[0:ROPE, 2, :])
                    ins.then_inc(seam_dve, 1)
                dve.tensor_copy(vS[:], kvR[:, :, NOPE:NOPE + MV]).then_inc(v_ok, 1)

                def normalise(q):
                    dve.wait_ge(exp_ok, i * 8 + q + 1)
                    dve.reciprocal(row_inv[:, q:q + 1], row_sum[:, q:q + 1]).then_inc(inv_ok, 1)
                    dve.wait_ge(inv_ok, i * 8 + q + 1)
                    dve.tensor_scalar(probs[:, q % 3, :], probs[:, q % 3, :], row_inv[:, q:q + 1], None,
                                      ALU.mult).then_inc(p_ok, 1)

                def head_out(j):
                    dve.wait_ge(pv_mm, i * 2 + j + 1)
                    dve.wait_ge(ob_out, i * 32 + CREDIT)
                    dve.tensor_copy(obS[:, j * HALF:(j + 1) * HALF], ps[:, 6, :]).then_inc(ob_ev, 1)

                for n in range(10):
                    if n < 8:
                        dve.wait_ge(s_mm, i * 8 + n + 1)
                        dve.tensor_reduce(row_max[:, n:n + 1], ps[:, 2 * (n % 2):2 * (n % 2) + 2, :],
                                          mybir.AxisListType.XY, ALU.max, negate=True).then_inc(max_ok, 1)
                    if 1 <= n <= 8:
                        normalise(n - 1)
                    if n >= 2:
                        q = n - 2
                        dve.wait_ge(p_tr, i * 16 + 2 * q + 1)
                        dve.tensor_copy(probsT[:, q // 4, 0:4, (q % 4) * P:(q % 4 + 1) * P],
                                        ps[:, 4, :].rearrange("p (a c) -> p a c", a=4)).then_inc(pt_dve, 1)
                    if not last:
                        if n == 4:
                            q_stats(i + 1, s)
                        if n == 5:
                            q_norm(i + 1, s)
                        if n == 8:
                            k_stats(i + 1, s)
                        if n == 9:
                            k_norm(i + 1, s)
                    if n == 6:
                        head_out(0)
                head_out(1)
                if not last:
                    s.end()

            with dve.Fori(0, MH - 1) as i:
                mla_head(i, False)
            mla_head(MH - 1, True)

            dve.wait_ge(gate_consts, 1)
            dve.wait_ge(ob_out, 32 * MH + CREDIT)
            per = 27

            def gla_head(h):
                s = Steps(dve, gla_step, turn=h, per=per)
                for d in range(2):
                    dve.wait_ge(z_mm, h * 2 + d + 1)
                    if d == 0:
                        dve.wait_ge(wa_in, h * 64 + 64)
                    zb = ps[:, 4 + 2 * d:6 + 2 * d, :]
                    z3 = zT[:].rearrange("p (a c) -> p a c", a=2)
                    if d == 1:
                        dve.wait_ge(ed_ok, h * 2 + 1)
                    dve.tensor_scalar(z3, zb, b_a2[:, d:d + 1], None, ALU.add).then_inc(z_dve, 1)
                    dve.wait_ge(z_act, h * 6 + 3 * d + 3)
                    dve.scalar_tensor_tensor(out=eT[:], in0=zT[:], scalar=0.0, in1=eT[:], op0=ALU.min,
                                             op1=ALU.subtract).then_inc(ls_ok, 1)
                    dve.wait_ge(ls_ok, h * 2 + d + 1)
                    rev = slice(None, None, -1) if d else slice(None)
                    if d == 1:
                        dve.wait_ge(e_ok, h * 4 + 2)
                    dve.tensor_tensor_scan(bT[:, rev], scan_m[:], eT[:, rev], 0.0, ALU.mult,
                                           ALU.add).then_inc(b_ok, 1)
                    dve.wait_ge(b_ok, h * 2 + d + 1)
                    b3 = bT[:].rearrange("p (n c) -> p n c", c=CH)
                    last = b3[:, :, 0:1] if d else b3[:, :, CH - 1:CH]
                    dve.tensor_tensor(zT[:].rearrange("p (n c) -> p n c", c=CH), last.broadcast_to((P, NCH, CH)), b3,
                                      ALU.subtract).then_inc(tail_ok, 1)
                    dve.wait_ge(e_ok, h * 4 + 2 * d + 1)
                    e3 = qt[:, d, :].rearrange("p (n c) -> p n c", c=CH)
                    s.link(dve.tensor_copy(decay[:, d, :].unsqueeze(2), e3[:, :, 0:1] if d else e3[:, :, CH - 1:CH]))
                    if d == 0:
                        dve.wait_ge(qk_ev, h * 4 + 4)
                    dve.tensor_tensor(qt[:, d, :], qt[:, d, :], qk_T[:, 0, :], ALU.mult).then_inc(mats_ok, 1)
                    dve.wait_ge(e_ok, h * 4 + 2 * d + 2)
                    dve.tensor_tensor(kt[:, d, :], kt[:, d, :], qk_T[:, 1, :], ALU.mult).then_inc(mats_ok, 1)
                    dve.wait_ge(ed_ok, h * 2 + d + 1)
                    dve.tensor_tensor(kd[:, d, :], kd[:, d, :], qk_T[:, 1, :], ALU.mult).then_inc(mats_ok, 1)
                for c in range(4):
                    d, half = divmod(c, 2)
                    dve.wait_ge(kd_tr, h * 4 + c + 1)
                    dve.tensor_copy(kdR[:, d, 4 * half:4 * half + 4, :],
                                    ps[:, c, :].rearrange("p (a c) -> p a c", a=4)).then_inc(kd_ev, 1)
                for half in range(2):
                    t4 = slice(4 * half, 4 * half + 4)
                    for d in range(2):
                        dve.wait_ge(att_mm, h * 4 + 2 * half + d + 1)
                        dst = (att_f, att_b)[d][:, t4, :]
                        src = ps[:, 4 + 2 * half + d, :].rearrange("p (a c) -> p a c", a=4)
                        dve.tensor_tensor(dst, src, keep_hi[:, d, :].unsqueeze(1).broadcast_to((P, 4, P)),
                                          ALU.min).then_inc(att_ok, 1)
                        dve.wait_ge(att_ok, h * 10 + half * 5 + 2 * d + 1)
                        dve.tensor_tensor(dst, dst, keep_lo[:, d, :].unsqueeze(1).broadcast_to((P, 4, P)),
                                          ALU.max).then_inc(att_ok, 1)
                    dve.wait_ge(att_ok, h * 10 + half * 5 + 4)
                    dve.tensor_tensor(att[:, t4, :], att_f[:, t4, :], att_b[:, t4, :], ALU.add).then_inc(att_ok, 1)
                dve.memset(state[:, 1, NCH - 1, :], 0.0).then_inc(st_ok, 1)
                dve.memset(state[:, 0, 0, :], 0.0).then_inc(st_ok, 1)
                for n in range(30):
                    d, c = (1, NCH - 1 - n) if n < 15 else (0, n - 15)
                    to = c - 1 if d else c + 1
                    dve.wait_ge(ds_mm, h * 30 + n + 1)
                    dve.wait_ge(st_ok, h * 32 + n + 2)
                    dve.scalar_tensor_tensor(out=state[:, d, to, :], in0=state[:, d, c, :], scalar=decay[:, d, c:c + 1],
                                             in1=ps[:, 4 + n % 4, 0:DV],
                                             op0=ALU.mult, op1=ALU.add).then_inc(st_ok, 1)

                def o_scale(half):
                    dve.wait_ge(o_sq, h * NT + 4 * half + 4)
                    mean_eps(stat[:, 6, 4 * half:4 * half + 4], stat[:, 6, 4 * half:4 * half + 4], DV).then_inc(o_ms, 1)
                    dve.wait_ge(o_rs, h * 2 + half + 1)
                    if half == 0:
                        dve.wait_ge(silu_ok, h + 1)
                    for t in range(4 * half, 4 * half + 4):
                        ins = dve.scalar_tensor_tensor(out=oR[:, t, :], in0=oR[:, t, :], scalar=stat[:, 6, t:t + 1],
                                                       in1=vr[:, t, DV:2 * DV], op0=ALU.mult, op1=ALU.mult)
                    ins.then_inc(o_n, 1)

                for t in range(NT):
                    dve.wait_ge(o_mm, h * NT + t + 1)
                    dve.tensor_copy(oR[:, t, :], ps[:, t % 4, 0:DV]).then_inc(o_ev, 1)
                    if t == 5:
                        o_scale(0)
                o_scale(1)
                dve.wait_ge(oa_out, h * 16 + CREDIT)
                for c in (0, 2):
                    half, j = divmod(c, 2)
                    dve.wait_ge(o_tr, h * 4 + c + 1)
                    dve.tensor_scalar(oaS[:, j, half * HALF:(half + 1) * HALF], ps[:, 4 + c, :], onorm_c[:, j:j + 1],
                                      None, ALU.mult).then_inc(oa_dve, 1)
                s.per = per
                return s.n

            per = 2
            with dve.Fori(0, GH) as h:
                used = gla_head(h)
                assert used == per

            with dve.Fori(0, KD) as cb:
                for j, sg in enumerate((sg_a, sg_b)):
                    dve.wait_ge(e_mm, cb * 4 + 2 * j + 2)
                    dve.wait_ge(sg_ok, cb * 2 + j + 1 + CREDIT)
                    s3 = sg[:].rearrange("p (a c) -> p a c", a=2)
                    dve.tensor_tensor(s3, ps[:, 4 * j + 2:4 * j + 4, :], s3, ALU.mult).then_inc(e_dve, 1)
                dve.wait_ge(e_dve, cb * 3 + 2 + CREDIT)
                dve.tensor_tensor(mT[:, bass.ds(cb, 1), :].rearrange("p a s -> p (a s)"), sg_a[:], sg_b[:],
                                  ALU.add).then_inc(e_dve, 1)

            dve.wait_ge(x1_in, 16 * NT)
            dve.wait_ge(gf_in, 16)

            def ffn_norm(t):
                dve.wait_ge(x1_sq, t + 1)
                mean_eps(stat[:, 7, t:t + 1], stat[:, 7, t:t + 1], D).then_inc(x1_ms, 1)
                dve.wait_ge(x1_rs, t + 1)
                dve.scalar_tensor_tensor(out=h2[:, t, :], in0=x1[:, t, :], scalar=stat[:, 7, t:t + 1], in1=g_ffn_b[:],
                                         op0=ALU.mult, op1=ALU.mult).then_inc(h2_ok, 1)

            for g in range(2):
                for half in range(2):
                    for j in range(4):
                        t = 4 * g + j
                        dve.wait_ge(f_mm, g * 8 + half * 4 + j + 1)
                        cols = slice(half * HALF, (half + 1) * HALF)
                        dve.tensor_tensor(x1[:, t, cols], ps[:, 4 * half + j, :], x1[:, t, cols], ALU.add) \
                            .then_inc(f_ev, 1)
                for j in range(4):
                    ffn_norm(4 * g + j)
            for t in range(NT):
                dve.wait_ge(h2_tr, 2 * t + 1)
                if t >= 2:
                    dve.wait_ge(lg_mm, t - 1)
                dve.tensor_copy(h2T[:, t % 2, 0:4, :], ps[:, 2 * (t % 2), :].rearrange("p (a c) -> p a c", a=4)) \
                    .then_inc(h2T_dve, 1)

            dve.wait_ge(lg_mm, NT)
            dve.wait_ge(rows_out, 32 * NT)
            lg = ps[:, 7, 0:NT * NE].rearrange("p (t e) -> p t e", t=NT)
            s = Steps(dve, soft)
            s.link(dve.tensor_reduce(stat[:, 8, :], lg, AX, ALU.max))
            s.mark(dve.tensor_tensor(aff[:], lg, stat[:, 8, :].unsqueeze(2).broadcast_to((P, NT, NE)), ALU.subtract))
            dve.wait_ge(soft_exp, 1)
            s.link(dve.tensor_reduce(stat[:, 9, :], aff[:], AX, ALU.add))
            s.link(dve.reciprocal(stat[:, 10, :], stat[:, 9, :]))
            s.mark(dve.tensor_tensor(aff[:], aff[:], stat[:, 10, :].unsqueeze(2).broadcast_to((P, NT, NE)), ALU.mult))
            dve.wait_ge(aff_tr, 1)
            t = Steps(dve, affT_ok)
            t.link(dve.tensor_copy(affT[:, 0, :].rearrange("p (a c) -> p a c", a=2), ps[0:NE, 0:2, :]))
            for r in range(CAP // 8):
                src, v8 = affT[:, r % 2, :], top_v[:, 8 * r:8 * r + 8]
                t.link(dve.max(v8, src))
                t.mark(dve.max_index(top_i[:, 8 * r:8 * r + 8], v8, src))
                t.link(dve.match_replace(affT[:, (r + 1) % 2, :], v8, src, -1.0))
            dve.tensor_copy(top_f[:], top_i[:]).then_inc(top_ok, 1)
            dve.wait_ge(top_tr, 1)
            dve.tensor_copy(val_c[:], ps[:, 2, 0:NE]).then_inc(idx_ok, 1)
            dve.tensor_copy(idx_c[:], ps[:, 2, NE:2 * NE]).then_inc(idx_ok, 1)
            dve.wait_ge(idx_ok, 2)

            def low_part(dst, whole, high):
                return dve.tensor_tensor(dst, whole, high.bitcast(F32), ALU.subtract)

            def split(n, turn=0):
                dve.wait_ge(hi_ok, turn * UNITS + n + 1)
                low_part(w_lo[:, n % RING, :], w_raw[:, n % RING, :], w_hi[:, n % RING, :]).then_inc(lo_ok, 1)

            def rows_in(e):
                for b in range(2):
                    dve.wait_ge(xeT_hi_ok, e * 2 + b + 1)
                    rows = slice(4 * b, 4 * b + 4)
                    low_part(xeT_lo[:, rows, :], ps[:, b, :].rearrange("p (a c) -> p a c", a=4),
                             xeT_hi[:, rows, :]).then_inc(xeT_lo_ok, 1)

            def activate(e, j):
                dve.wait_ge(silu_e, e * 2 + j + 1)
                dve.tensor_tensor(act_r[:, j, :], ps[:, 2 * j + 1, :], silu_g[:, j, :], ALU.mult).then_inc(act_ok, 1)

            def act_in(e, j):
                dve.wait_ge(aT_hi_ok, e * 2 + j + 1)
                rows = slice(4 * j, 4 * j + 4)
                low_part(act_T_lo[:, rows, :], ps[:, 6 + j, :].rearrange("p (a c) -> p a c", a=4),
                         act_T_hi[:, rows, :]).then_inc(aT_lo_ok, 1)

            def affinity(e):
                dve.tensor_copy(val_s[:], val_c[:, bass.ds(e, 1)]).then_inc(val_ok, 1)

            rows_in(0)
            for n in range(FIRST):
                split(n)
                if n == 8 + LEAD - 1:
                    activate(0, 0)
            with dve.Fori(0, NE - 1) as e:
                for u in range(UNITS):
                    split(FIRST + u, e)
                    if u == LEAD - 1:
                        act_in(e, 0)
                        activate(e, 1)
                        rows_in(e + 1)
                    if u == 4 + LEAD - 1:
                        act_in(e, 1)
                    if u == 12 + LEAD - 1:
                        activate(e + 1, 0)
                        dve.wait_ge(ye_ok, e + CREDIT)
                        affinity(e)
            for u in range(8):
                split(FIRST + (NE - 1) * UNITS + u)
                if u == LEAD - 1:
                    act_in(NE - 1, 0)
                    activate(NE - 1, 1)
                if u == 4 + LEAD - 1:
                    act_in(NE - 1, 1)
            dve.wait_ge(ye_ok, NE - 1 + CREDIT)
            affinity(NE - 1)

        @block.scalar
        def _(act):
            nc.scalar.preload_act_table_set("natural_log_exp_and_others")
            loads = [(g_mix_c[:], col(g_mix, KD)), (qn_c[:], col(mla_q_norm, QR // P)),
                     (kvn_c[:], col(mla_kv_norm, KVR // P)), (onorm_c[:], col(gla_onorm, DV // P)),
                     (qhn_c[:], col(q_head_norm[0:NOPE], 1)), (khn_c[:], col(k_head_norm[0:NOPE], 1)),
                     (qhr_b[:], spread(q_head_norm[NOPE:HQ], ROPE)), (khr_b[:], spread(k_head_norm[NOPE:HQ], ROPE)),
                     (pos_i[:], positions.rearrange("b (t p) -> p (b t)", p=P)),
                     (w_router_s[:], w_router.rearrange("(k p) e -> p k e", p=P))]
            for dst, src in loads:
                act.dma_start(dst, src, allow_slow_non_contiguous=True).then_inc(small_in, 16)
            assert len(loads) == small_loads

            a_st = Steps(act, act_a)
            for t in range(NT):
                act.wait_ge(x_in[t], 16)
                nc.scalar.activation(sq_a[:], xs[:, t, :], ACT.Square, accum_out=stat[:, 0, t:t + 1]).then_inc(ssq_x, 1)
                act.wait_ge(ssq_x, t + 1)
            act.wait_ge(small_in, 16 * small_loads)
            for c in range(1, 2 * KD, 2):
                half, k = divmod(c, KD)
                act.wait_ge(hT_tr, c + 1)
                nc.scalar.activation(hT[:, k, half * HALF:(half + 1) * HALF], ps[:, c % 4, :], ACT.Copy,
                                     scale=g_mix_c[:, k:k + 1]).then_inc(hT_act, 1)
            for j, tbl in enumerate((sin_t, cos_t)):
                act.wait_ge(trig_arg, j + 1)
                nc.scalar.activation(tbl[:], tbl[:], ACT.Sin).then_inc(trig, 1)
            for t in range(NT):
                act.wait_ge(lat_ev, t + 1)
                a_st.link(nc.scalar.activation(sq_a[:, 0:QR], lat_r[:, t, 2 * RANK:LA], ACT.Square,
                                               accum_out=stat[:, 1, t:t + 1]))
                a_st.link(nc.scalar.activation(sq_a[:, 0:KVR], lat_r[:, t, LA:LA + KVR], ACT.Square,
                                               accum_out=stat[:, 2, t:t + 1]))
                nc.scalar.activation(sq_a[:, 0:ROPE], lat_r[:, t, LA + KVR:LAT], ACT.Square,
                                     accum_out=stat[:, 3, t:t + 1]).then_inc(lat_sq, 1)
                act.wait_ge(lat_sq, t + 1)
            for c in range(1, 14, 2):
                half, j = divmod(c, 7)
                cols = slice(half * HALF, (half + 1) * HALF)
                act.wait_ge(lat_tr, c + 1)
                if j < 2:
                    ins = nc.scalar.activation(gateT[:, j, cols], ps[0:RANK, c % 4, :], ACT.Copy)
                elif j < 5:
                    ins = nc.scalar.activation(cqT[:, j - 2, cols], ps[:, c % 4, :], ACT.Copy,
                                               scale=qn_c[:, j - 2:j - 1])
                else:
                    ins = nc.scalar.activation(ckvT[:, j - 5, cols], ps[:, c % 4, :], ACT.Copy,
                                               scale=kvn_c[:, j - 5:j - 4])
                ins.then_inc(latT_act, 1)

            act.wait_ge(k_rot_ok, 1)
            act.wait_ge(lat_tr, 14)

            def take(n, g):
                act.wait_ge(prj_mm, n * 8 + g + 1)
                width = HQ if g < 4 else NOPE + MV
                dst = (qR if g < 4 else kvR)[:, 2 * (g % 4):2 * (g % 4) + 2, :]
                if g == 4:
                    act.wait_ge(v_ok, n)
                nc.scalar.activation(dst, ps[:, 7, 0:2 * width].rearrange("p (a c) -> p a c", a=2),
                                     ACT.Copy).then_inc(prj_ev, 1)
                if g == 3:
                    act.wait_ge(prj_ev, n * 8 + 4)
                    act.wait_ge(head_ms, n * 2)
                    nc.scalar.activation(sq_q[:], qR[:], ACT.Square).then_inc(head_sq, 1)
                if g == 7:
                    act.wait_ge(prj_ev, n * 8 + 8)
                    act.wait_ge(head_ms, n * 2 + 1)
                    nc.scalar.activation(sq_q[:, :, 0:NOPE], kvR[:, :, 0:NOPE], ACT.Square).then_inc(head_sq, 1)

            for g in range(8):
                take(0, g)

            def mla_head(i, last):
                for c in range(1, 8, 2):
                    what = c // 2
                    act.wait_ge(seam_tr, i * 8 + c + 1)
                    if what == 0:
                        ins = nc.scalar.activation(qT[:, HALF:S], ps[:, 5, :], ACT.Copy, scale=qhn_c[:, 0:1])
                    elif what == 1:
                        ins = nc.scalar.activation(qTr[:, HALF:S], ps[0:ROPE, 7, :], ACT.Copy)
                    elif what == 2:
                        ins = nc.scalar.activation(kT[:, HALF:S], ps[:, 1, :], ACT.Copy, scale=khn_c[:, 0:1])
                    else:
                        ins = nc.scalar.activation(kTr[:, HALF:S], ps[0:ROPE, 3, :], ACT.Copy)
                    ins.then_inc(seam_act, 1)
                for n in range(10):
                    if n < 8:
                        act.wait_ge(max_ok, i * 8 + n + 1)
                        if n >= 3:
                            act.wait_ge(p_tr, i * 16 + 2 * (n - 3) + 2)
                        nc.scalar.activation(probs[:, n % 3, :].rearrange("p (a c) -> p a c", a=2),
                                             ps[:, 2 * (n % 2):2 * (n % 2) + 2, :], ACT.Exp, bias=row_max[:, n:n + 1],
                                             accum_out=row_sum[:, n:n + 1]).then_inc(exp_ok, 1)
                        if not last:
                            take(i + 1, n)
                    if n >= 2:
                        q = n - 2
                        act.wait_ge(p_tr, i * 16 + 2 * q + 2)
                        nc.scalar.activation(probsT[:, q // 4, 4:8, (q % 4) * P:(q % 4 + 1) * P],
                                             ps[:, 5, :].rearrange("p (a c) -> p a c", a=4), ACT.Copy).then_inc(pt_act, 1)

            with act.Fori(0, MH - 1) as i:
                mla_head(i, False)
            mla_head(MH - 1, True)

            act.wait_ge(gate_consts, 1)

            def gla_head(h):
                for c in range(4):
                    act.wait_ge(qk_mm, h * 4 + c + 1)
                    j, half = divmod(c, 2)
                    nc.scalar.activation(qk_T[:, j, half * HALF:(half + 1) * HALF], ps[:, c, :], ACT.Copy,
                                         scale=DK ** -0.5 if j == 0 else 1.0).then_inc(qk_ev, 1)

                def take_vr(t):
                    act.wait_ge(vr_mm, h * NT + t + 1)
                    nc.scalar.activation(vr[:, t, :], ps[:, t % 4, :], ACT.Copy).then_inc(vr_ev, 1)

                for d in range(2):
                    act.wait_ge(z_dve, h * 2 + d + 1)
                    if d == 1:
                        act.wait_ge(b_ok, h * 2 + 1)
                    nc.scalar.activation(eT[:], zT[:], ACT.Abs).then_inc(z_act, 1)
                    act.wait_ge(z_act, h * 6 + 3 * d + 1)
                    nc.scalar.activation(eT[:], eT[:], ACT.Exp, scale=-1.0).then_inc(z_act, 1)
                    act.wait_ge(z_act, h * 6 + 3 * d + 2)
                    nc.scalar.activation(eT[:], eT[:], ACT.Ln, bias=1.0).then_inc(z_act, 1)
                    take_vr(2 * d)
                    act.wait_ge(b_ok, h * 2 + d + 1)
                    nc.scalar.activation(qt[:, d, :], bT[:], ACT.Exp, scale=1 / GATE_DIV).then_inc(e_ok, 1)
                    nc.scalar.activation(kt[:, d, :], bT[:], ACT.Exp, scale=-1 / GATE_DIV).then_inc(e_ok, 1)
                    act.wait_ge(tail_ok, h * 2 + d + 1)
                    nc.scalar.activation(kd[:, d, :], zT[:], ACT.Exp, scale=1 / GATE_DIV).then_inc(ed_ok, 1)
                    take_vr(2 * d + 1)
                for t in range(4, NT):
                    take_vr(t)
                act.wait_ge(vr_ev, h * NT + NT)
                nc.scalar.activation(vr[:, :, DV:2 * DV], vr[:, :, DV:2 * DV], ACT.Silu).then_inc(silu_ok, 1)
                act.wait_ge(oa_out, h * 16 + CREDIT)
                for t in range(NT):
                    act.wait_ge(o_ev, h * NT + t + 1)
                    nc.scalar.activation(oaS[:, 0, 0:DV], oR[:, t, :], ACT.Square,
                                         accum_out=stat[:, 6, t:t + 1]).then_inc(o_sq, 1)
                    act.wait_ge(o_sq, h * NT + t + 1)
                for c in (1, 3):
                    half, j = divmod(c, 2)
                    act.wait_ge(o_tr, h * 4 + c + 1)
                    nc.scalar.activation(oaS[:, j, half * HALF:(half + 1) * HALF], ps[:, 4 + c, :], ACT.Copy,
                                         scale=onorm_c[:, j:j + 1]).then_inc(oa_act, 1)

            with act.Fori(0, GH) as h:
                gla_head(h)

            with act.Fori(0, KD) as cb:
                for j, sg in enumerate((sg_a, sg_b)):
                    act.wait_ge(e_mm, cb * 4 + 2 * j + 1)
                    if j == 0:
                        act.wait_ge(e_dve, cb * 3 + CREDIT)
                    nc.scalar.activation(sg[:].rearrange("p (a c) -> p a c", a=2), ps[:, 4 * j:4 * j + 2, :],
                                         ACT.Sigmoid).then_inc(sg_ok, 1)
            for t in range(NT):
                g, j = divmod(t, 4)
                act.wait_ge(f_ev, g * 8 + 4 + j + 1)
                nc.scalar.activation(h2[:, t, :], x1[:, t, :], ACT.Square, accum_out=stat[:, 7, t:t + 1]) \
                    .then_inc(x1_sq, 1)
            for t in range(NT):
                act.wait_ge(h2_tr, 2 * t + 2)
                if t >= 2:
                    act.wait_ge(lg_mm, t - 1)
                nc.scalar.activation(h2T[:, t % 2, 4:8, :], ps[:, 2 * (t % 2) + 1, :].rearrange("p (a c) -> p a c", a=4),
                                     ACT.Copy).then_inc(h2T_act, 1)
            act.wait_ge(soft, 2)
            nc.scalar.activation(aff[:], aff[:], ACT.Exp).then_inc(soft_exp, 1)

            def split(n, turn=0):
                act.wait_ge(raw_in[n % RING], turn * 32 + 16 * (n // RING) + 16)
                if n >= RING:
                    act.wait_ge(w_used, turn * UNITS + n - RING + 1)
                nc.scalar.activation(w_hi[:, n % RING, :], w_raw[:, n % RING, :], ACT.Copy).then_inc(hi_ok, 1)

            def rows_in(e):
                for b in range(2):
                    act.wait_ge(xe_tr, e * 2 + b + 1)
                    nc.scalar.activation(xeT_hi[:, 4 * b:4 * b + 4, :], ps[:, b, :].rearrange("p (a c) -> p a c", a=4),
                                         ACT.Copy).then_inc(xeT_hi_ok, 1)

            def silu(e, j, used):
                act.wait_ge(w_used, used)
                nc.scalar.activation(silu_g[:, j, :], ps[:, 2 * j, :], ACT.Silu).then_inc(silu_e, 1)

            def act_in(e, j):
                act.wait_ge(a_tr, e * 2 + j + 1)
                nc.scalar.activation(act_T_hi[:, 4 * j:4 * j + 4, :], ps[:, 6 + j, :].rearrange("p (a c) -> p a c", a=4),
                                     ACT.Copy).then_inc(aT_hi_ok, 1)

            def results(e, used):
                act.wait_ge(w_used, used)
                act.wait_ge(ye_free, e + CREDIT)
                act.wait_ge(val_ok, e + 1)
                nc.scalar.activation(ye[:].rearrange("p (a c) -> p a c", a=2), ps[:, 4:6, :], ACT.Copy,
                                     scale=val_s[:, 0:1]).then_inc(ye_ok, 1)

            rows_in(0)
            for n in range(FIRST):
                split(n)
                if n == 8 + LEAD - 1:
                    silu(0, 0, 8)
            with act.Fori(0, NE - 1) as e:
                for u in range(UNITS):
                    split(FIRST + u, e)
                    if u == LEAD - 1:
                        act_in(e, 0)
                        silu(e, 1, e * UNITS + FIRST)
                        rows_in(e + 1)
                    if u == 4 + LEAD - 1:
                        act_in(e, 1)
                    if u == 12 + LEAD - 1:
                        silu(e + 1, 0, e * UNITS + FIRST + 12)
                    if u == 16 + LEAD - 1:
                        results(e, e * UNITS + FIRST + 16)
            end = FIRST + (NE - 1) * UNITS
            for u in range(8):
                split(end + u)
                if u == LEAD - 1:
                    act_in(NE - 1, 0)
                    silu(NE - 1, 1, end)
                if u == 4 + LEAD - 1:
                    act_in(NE - 1, 1)
            results(NE - 1, end + 8)


_INS = ["x", "positions", "g_mix", "w_in", "gla_wa2_f", "gla_ba_f", "gla_wa2_b", "gla_ba_b", "gla_onorm", "w_gla_out",
        "mla_q_norm", "w_uq", "mla_kv_norm", "w_ukv", "q_head_norm", "k_head_norm", "w_mla_out", "w_o", "g_ffn",
        "w_router", "w_gate_e", "w_up_e", "w_down_e"]


def kernel(**inputs):
    import concourse.bacc as bacc
    from concourse.bass_utils import run_bass_kernel_spmd

    nc = bacc.Bacc("TRN2", target_bir_lowering=False, num_devices=1)
    arrays, args = {}, []
    for name in _INS:
        a = np.ascontiguousarray(inputs[name])
        arrays[f"in_{name}"] = a
        args.append(nc.dram_tensor(f"in_{name}", a.shape, mybir.dt.from_np(a.dtype), kind="ExternalInput").ap())
    args.append(nc.dram_tensor("layer_out", (1, S, D), F32, kind="ExternalOutput").ap())
    hybrid_layer(nc, *args)
    r = run_bass_kernel_spmd(nc, [arrays], core_ids=[0])
    return r.results[0]["layer_out"]
```

```python
import math
from contextlib import ExitStack

import numpy as np

import concourse.bass as bass
from concourse import mybir

P = 128
F32 = mybir.dt.float32
F32R = mybir.dt.float32r
I32 = mybir.dt.int32
U32 = mybir.dt.uint32
ALU = mybir.AluOpType
ACT = mybir.ActivationFunctionType
AX = mybir.AxisListType.X

S = 1024
D = 1024
NT = S // P
KD = D // P
HALF = 512
GH, DK, DV, RANK, CH = 4, 128, 256, 16, 64
NCH = S // CH
GATE_DIV = 16.0
MH, NOPE, ROPE, MV = 8, 128, 64, 128
HQ = NOPE + ROPE
QR, KVR = 384, 256
RH = ROPE // 2
NE, CAP, FF = 16, 128, 1024
EPS = 1e-6
BIG = 3.0e38
UNIT = 1024
UNITS = 24
RING = 12
FIRST = 16
TURN = ([("d", 0, k) for k in range(4)] + [(m, 0, k) for k in range(4) for m in "gu"]
        + [("d", 1, k) for k in range(4)] + [(m, 1, k) for k in range(4) for m in "gu"])
LEAD = 3
GLA_UNITS = 6
MERGE0 = GH * GLA_UNITS
JOBS = 2 * KD
OUT0 = MERGE0 + 2 * JOBS
CREDIT = 1
PAIRS = 2
C_Q, C_K, C_V, C_R = 0, 512, 1024, 2048
C_LAT = 3072
LAT = 2 * RANK + QR + KVR + ROPE
LA = 2 * RANK + QR
LB = KVR + ROPE
C_GA = C_LAT + LAT
C_GB = C_GA + D


class Steps:

    def __init__(self, eng, sem, base=0, turn=0, per=0):
        self.eng, self.sem, self.base, self.turn, self.per, self.n = eng, sem, base, turn, per, 0

    def mark(self, ins):
        ins.then_inc(self.sem, 1)
        self.n += 1
        return self.n

    def wait(self, n=None):
        self.eng.wait_ge(self.sem, self.turn * self.per + self.base + (self.n if n is None else n))

    def link(self, ins):
        self.mark(ins)
        self.wait()

    def end(self):
        assert self.n == self.per, (self.n, self.per)


def rope_frequencies():
    return [float(np.float32(10000.0 ** (-j / RH))) for j in range(RH)]


def hybrid_layer(nc, x, positions, g_mix, w_in, gla_wa2_f, gla_ba_f, gla_wa2_b, gla_ba_b, gla_onorm,
                 w_gla_out, mla_q_norm, w_uq, mla_kv_norm, w_ukv, q_head_norm, k_head_norm,
                 w_mla_out, w_o, g_ffn, w_router, w_gate_e, w_up_e, w_down_e, out):
    x_rows = x[0]
    out_rows = out[0]
    h2_dram = nc.dram_tensor("h2_rows", (S, D), F32, kind="Internal").ap()
    oa_dram = nc.dram_tensor("gla_out_T", (KD, P, S), F32, kind="Internal").ap()
    ob_dram = nc.dram_tensor("mla_out_T", (KD, P, S), F32, kind="Internal").ap()

    def col(v, n):
        return v.rearrange("(k p) -> p k", p=P) if n > 1 else v.rearrange("(p a) -> p a", a=1)

    def spread(v, n):
        return v.rearrange("(a n) -> a n", a=1).broadcast_to((P, n))

    w_in_k = w_in.rearrange("(k p) n -> p k n", p=P)
    w_uq_k = w_uq.rearrange("(k p) n -> p k n", p=P)
    w_ukv_k = w_ukv.rearrange("(k p) n -> p k n", p=P)
    w_go_k = w_gla_out.rearrange("(k p) n -> p k n", p=P)
    w_mo_k = w_mla_out.rearrange("(k p) n -> p k n", p=P)
    w_o_k = w_o.rearrange("(k p) n -> p k n", p=P)

    with ExitStack() as ctx:
        def sb_in(stack, name, shape, dt=F32):
            return stack.enter_context(nc.sbuf_tensor(name, shape, dt))

        def sb(name, shape, dt=F32):
            return sb_in(ctx, name, shape, dt)

        def sem(name):
            return ctx.enter_context(nc.semaphore(name))

        ps = ctx.enter_context(nc.psum_tensor("ps", [P, 8, HALF], F32))

        ident = sb("ident", [P, P])
        g_mix_c = sb("g_mix_c", [P, KD])
        qn_c = sb("qn_c", [P, QR // P])
        kvn_c = sb("kvn_c", [P, KVR // P])
        onorm_c = sb("onorm_c", [P, DV // P])
        qhn_c = sb("qhn_c", [P, 1])
        khn_c = sb("khn_c", [P, 1])
        qhr_b = sb("qhr_b", [P, ROPE])
        khr_b = sb("khr_b", [P, ROPE])
        minus_half = sb("minus_half", [P, NT])
        stat = sb("stat", [P, 16, NT])
        idx_c = sb("idx_c", [P, NE], U32)
        val_c = sb("val_c", [P, NE])
        w_router_s = sb("w_router_s", [P, KD, NE])

        mix_mem = ExitStack()
        with mix_mem:
            stage = sb_in(mix_mem, "stage", [P, 2, S])
            gateT = stage[0:RANK]
            w_a2 = sb_in(mix_mem, "w_a2", [RANK, 2, DK])
            b_a2 = sb_in(mix_mem, "b_a2", [P, 2])
            d_raw = sb_in(mix_mem, "d_raw", [P, 2, UNIT])
            d_hi = sb_in(mix_mem, "d_hi", [P, 2, UNIT], F32R)
            d_lo = sb_in(mix_mem, "d_lo", [P, 2, UNIT], F32R)

            early_mem = ExitStack()
            with early_mem:
                hT = sb_in(early_mem, "hT", [P, KD, S])
                mla_mem = ExitStack()
                with mla_mem:
                    cqT = sb_in(mla_mem, "cqT", [P, QR // P, S])
                    ckvT = sb_in(mla_mem, "ckvT", [P, KVR // P, S])
                    k_rot = sb_in(mla_mem, "k_rot", [P, NT, ROPE])
                    cos_t = sb_in(mla_mem, "cos_t", [P, NT, RH])
                    sin_t = sb_in(mla_mem, "sin_t", [P, NT, RH])
                    freq = sb_in(mla_mem, "freq", [P, RH])
                    w_uq_h = sb_in(mla_mem, "w_uq_h", [P, QR // P, HQ])
                    w_ukv_h = sb_in(mla_mem, "w_ukv_h", [P, KVR // P, NOPE + MV])
                    lat_mem = ExitStack()
                    with lat_mem:
                        xs = sb_in(lat_mem, "xs", [P, NT, D])
                        w_lat = sb_in(lat_mem, "w_lat", [P, KD, LAT])
                        lat_r = sb_in(lat_mem, "lat_r", [P, NT, LAT])
                        sq_a = sb_in(lat_mem, "sq_a", [P, D])
                        pos_i = sb_in(lat_mem, "pos_i", [P, NT], I32)
                        pos_f = sb_in(lat_mem, "pos_f", [P, NT])
                        ang = sb_in(lat_mem, "ang", [P, NT, RH])
                        turns_f = sb_in(lat_mem, "turns_f", [P, 2, NT, RH])
                        turns_i = sb_in(lat_mem, "turns_i", [P, 2, NT, RH], I32)
                        k_tmp = sb_in(lat_mem, "k_tmp", [P, 3, NT, RH])
                    head_mem = ExitStack()
                    with head_mem:
                        qR = sb_in(head_mem, "qR", [P, NT, HQ])
                        kvR = sb_in(head_mem, "kvR", [P, NT, NOPE + MV])
                        kRr = sb_in(head_mem, "kRr", [P, NT, ROPE])
                        sq_q = sb_in(head_mem, "sq_q", [P, NT, HQ])
                        r_tmp = sb_in(head_mem, "r_tmp", [P, 4, NT, RH])
                        qT = sb_in(head_mem, "qT", [P, S])
                        kT = sb_in(head_mem, "kT", [P, S])
                        qTr = sb_in(head_mem, "qTr", [ROPE, S])
                        kTr = sb_in(head_mem, "kTr", [ROPE, S])
                        vS = sb_in(head_mem, "vS", [P, NT, MV])
                        probs = sb_in(head_mem, "probs", [P, 3, S])
                        probsT = sb_in(head_mem, "probsT", [P, 2, NT, HALF])
                        obS = sb_in(head_mem, "obS", [P, S])
                        row_max = sb_in(head_mem, "row_max", [P, NT])
                        row_sum = sb_in(head_mem, "row_sum", [P, NT])
                        row_inv = sb_in(head_mem, "row_inv", [P, NT])

            late_mem = ExitStack()
            with late_mem:
                carry = sb_in(late_mem, "carry", [P, KD * S])
                hT_hi = sb_in(late_mem, "hT_hi", [P, KD, S], F32R)
                hT_lo = sb_in(late_mem, "hT_lo", [P, KD, S], F32R)
                state = carry[:, :].rearrange("p (d n v) -> p d n v", d=2, n=NCH)
                mT = carry[:, :].rearrange("p (k s) -> p k s", k=KD)
                h2 = carry[:, :].rearrange("p (t d) -> p t d", t=NT)
                mT_hi, mT_lo = hT_hi, hT_lo
                gla_tmp = ExitStack()
                with gla_tmp:
                    out_mem = ExitStack()
                    with out_mem:
                        oaS = sb_in(out_mem, "oaS", [P, 2, S])
                    vr = sb_in(gla_tmp, "vr", [P, NT, 2 * DV])
                    qk_T = sb_in(gla_tmp, "qk_T", [P, 2, S])
                    qt = sb_in(gla_tmp, "qt", [P, 2, S])
                    kt = sb_in(gla_tmp, "kt", [P, 2, S])
                    kd = sb_in(gla_tmp, "kd", [P, 2, S])
                    zT = sb_in(gla_tmp, "zT", [P, S])
                    eT = sb_in(gla_tmp, "eT", [P, S])
                    bT = sb_in(gla_tmp, "bT", [P, S])
                    decay = sb_in(gla_tmp, "decay", [P, 2, NCH])
                    keep_hi = sb_in(gla_tmp, "keep_hi", [P, 2, P])
                    keep_lo = sb_in(gla_tmp, "keep_lo", [P, 2, P])
                    scan_m = sb_in(gla_tmp, "scan_m", [P, S])
                    kdR = qk_T[:, :, :].rearrange("p d (t c) -> p d t c", t=NT)
                    oR = kd[:, :, :].rearrange("p a (t c) -> p (a t) c", c=DV)
                    o_sqr = kt[:, :, :].rearrange("p a (t c) -> p (a t) c", c=DV)
                    att = bT[:, :].rearrange("p (t c) -> p t c", t=NT)
                    att_f = zT[:, :].rearrange("p (t c) -> p t c", t=NT)
                    att_b = eT[:, :].rearrange("p (t c) -> p t c", t=NT)
                merge_mem = ExitStack()
                with merge_mem:
                    sg = sb_in(merge_mem, "sg", [P, 2, S])
                    branch_mem = ExitStack()
                    with branch_mem:
                        oT_hi = sb_in(branch_mem, "oT_hi", [P, KD, S], F32R)
                        oT_lo = sb_in(branch_mem, "oT_lo", [P, KD, S], F32R)
                    ffn_mem = ExitStack()
                    with ffn_mem:
                        x1 = sb_in(ffn_mem, "x1", [P, NT, D])
                        h2T = sb_in(ffn_mem, "h2T", [P, 2, KD, P])
                        g_ffn_b = sb_in(ffn_mem, "g_ffn_b", [P, D])
        route_mem = ExitStack()
        with route_mem:
            w_raw = sb_in(route_mem, "w_raw", [P, RING, UNIT])
            w_hi = sb_in(route_mem, "w_hi", [P, RING, UNIT], F32R)
            w_lo = sb_in(route_mem, "w_lo", [P, RING, UNIT], F32R)
            aff = sb_in(route_mem, "aff", [P, NT, NE])
            affT = sb_in(route_mem, "affT", [NE, 2, S])
            top_v = sb_in(route_mem, "top_v", [NE, CAP])
            top_i = sb_in(route_mem, "top_i", [NE, CAP], U32)
            top_f = sb_in(route_mem, "top_f", [NE, CAP])
            xe = sb_in(route_mem, "xe", [P, D])
            xeT_hi = sb_in(route_mem, "xeT_hi", [P, KD, CAP], F32R)
            xeT_lo = sb_in(route_mem, "xeT_lo", [P, KD, CAP], F32R)
            silu_g = sb_in(route_mem, "silu_g", [P, 2, HALF])
            act_r = sb_in(route_mem, "act_r", [P, 2, HALF])
            act_T_hi = sb_in(route_mem, "act_T_hi", [P, KD, CAP], F32R)
            act_T_lo = sb_in(route_mem, "act_T_lo", [P, KD, CAP], F32R)
            ye = sb_in(route_mem, "ye", [P, D])
            val_s = sb_in(route_mem, "val_s", [P, 1])

        x_in = [sem(f"x_in{t}") for t in range(NT)]
        small_in = sem("small_in")
        wlat_in = [sem(f"wlat_in{j}") for j in range(2)]
        consts = sem("consts")
        pool_step = sem("pool_step")
        gate_consts = sem("gate_consts")
        dve_a = sem("dve_a")
        act_a = sem("act_a")
        ssq_x = sem("ssq_x")
        ms_x = sem("ms_x")
        rstd_x = sem("rstd_x")
        xn = sem("xn")
        hT_tr = sem("hT_tr")
        hT_dve = sem("hT_dve")
        hT_act = sem("hT_act")
        lat_mm = sem("lat_mm")
        lat_ev = sem("lat_ev")
        lat_sq = sem("lat_sq")
        lat_ms = sem("lat_ms")
        lat_rs = sem("lat_rs")
        lat_n = sem("lat_n")
        lat_tr = sem("lat_tr")
        latT_dve = sem("latT_dve")
        latT_act = sem("latT_act")
        trig_arg = sem("trig_arg")
        trig = sem("trig")
        k_rot_ok = sem("k_rot_ok")

        wu_in = sem("wu_in")
        prj_mm = sem("prj_mm")
        prj_ev = sem("prj_ev")
        head_sq = sem("head_sq")
        head_ms = sem("head_ms")
        head_rs = sem("head_rs")
        head_n = sem("head_n")
        head_step = sem("head_step")
        seam_tr = sem("seam_tr")
        seam_dve = sem("seam_dve")
        seam_act = sem("seam_act")
        v_ok = sem("v_ok")
        s_mm = sem("s_mm")
        max_ok = sem("max_ok")
        exp_ok = sem("exp_ok")
        inv_ok = sem("inv_ok")
        p_ok = sem("p_ok")
        p_tr = sem("p_tr")
        pt_dve = sem("pt_dve")
        pt_act = sem("pt_act")
        pv_mm = sem("pv_mm")
        ob_ev = sem("ob_ev")
        ob_out = sem("ob_out")

        d_in = [sem(f"d_in{j}") for j in range(2)]
        d_hi_ok = sem("d_hi_ok")
        d_lo_ok = sem("d_lo_ok")
        d_used = sem("d_used")
        hT_hi_ok = sem("hT_hi_ok")
        hT_lo_ok = sem("hT_lo_ok")
        wa_in = sem("wa_in")
        qk_mm = sem("qk_mm")
        qk_ev = sem("qk_ev")
        z_mm = sem("z_mm")
        z_dve = sem("z_dve")
        z_act = sem("z_act")
        gla_step = sem("gla_step")
        ls_ok = sem("ls_ok")
        b_ok = sem("b_ok")
        e_ok = sem("e_ok")
        tail_ok = sem("tail_ok")
        ed_ok = sem("ed_ok")
        mats_ok = sem("mats_ok")
        vr_mm = sem("vr_mm")
        vr_ev = sem("vr_ev")
        silu_ok = sem("silu_ok")
        att_mm = sem("att_mm")
        att_ok = sem("att_ok")
        kd_tr = sem("kd_tr")
        kd_ev = sem("kd_ev")
        ds_mm = sem("ds_mm")
        st_ok = sem("st_ok")
        o_mm = sem("o_mm")
        o_ev = sem("o_ev")
        o_sq = sem("o_sq")
        o_ms = sem("o_ms")
        o_rs = sem("o_rs")
        o_n = sem("o_n")
        o_tr = sem("o_tr")
        oa_dve = sem("oa_dve")
        oa_act = sem("oa_act")
        oa_out = sem("oa_out")

        stage_in = [sem(f"stage_in{j}") for j in range(2)]
        oT_hi_ok = sem("oT_hi_ok")
        oT_lo_ok = sem("oT_lo_ok")
        g_ev = sem("g_ev")
        y_ev = sem("y_ev")
        m_ok = sem("m_ok")
        mT_hi_ok = sem("mT_hi_ok")
        mT_lo_ok = sem("mT_lo_ok")
        x1_in = sem("x1_in")
        gf_in = sem("gf_in")
        f_mm = sem("f_mm")
        f_ev = sem("f_ev")
        x1_sq = sem("x1_sq")
        x1_ms = sem("x1_ms")
        x1_rs = sem("x1_rs")
        h2_ok = sem("h2_ok")
        rows_out = sem("rows_out")
        h2_tr = sem("h2_tr")
        h2T_dve = sem("h2T_dve")
        h2T_act = sem("h2T_act")
        lg_mm = sem("lg_mm")
        soft = sem("soft")
        soft_exp = sem("soft_exp")
        aff_tr = sem("aff_tr")
        affT_ok = sem("affT_ok")
        top_ok = sem("top_ok")
        top_tr = sem("top_tr")
        idx_ok = sem("idx_ok")

        raw_in = [sem(f"raw_in{j}") for j in range(RING)]
        hi_ok = sem("hi_ok")
        lo_ok = sem("lo_ok")
        w_used = sem("w_used")
        xe_in = sem("xe_in")
        xe_tr = sem("xe_tr")
        xeT_hi_ok = sem("xeT_hi_ok")
        xeT_lo_ok = sem("xeT_lo_ok")
        silu_e = sem("silu_e")
        act_ok = sem("act_ok")
        a_tr = sem("a_tr")
        aT_hi_ok = sem("aT_hi_ok")
        aT_lo_ok = sem("aT_lo_ok")
        val_ok = sem("val_ok")
        ye_ok = sem("ye_ok")
        ye_out = sem("ye_out")
        ye_free = sem("ye_free")

        block = ctx.enter_context(nc.Block())
        small_loads = 10

        @block.sync
        def _(sp):
            for t in range(NT):
                sp.dma_start(xs[:, t, :], x_rows[t * P:(t + 1) * P, :]).then_inc(x_in[t], 16)
            for j in range(2):
                k0, k1 = j * KD // 2, (j + 1) * KD // 2
                sp.dma_start(w_lat[:, k0:k1, :], w_in_k[:, k0:k1, C_LAT:C_LAT + LAT]).then_inc(wlat_in[j], 16)

            def load_up(h):
                sp.dma_start(w_uq_h[:], w_uq_k[:, :, bass.ds(h * HQ, HQ)]).then_inc(wu_in, 16)
                sp.dma_start(w_ukv_h[:], w_ukv_k[:, :, bass.ds(h * (NOPE + MV), NOPE + MV)]).then_inc(wu_in, 16)

            def load_dense(pieces, k, before=0):
                if not isinstance(before, int) or before + k >= 2:
                    sp.wait_ge(d_lo_ok, before + k - 1)
                for dst, src in pieces:
                    sp.dma_start(dst, src).then_inc(d_in[k % 2], 16)

            def load_gla(h, u, before=0):
                slot = d_raw[:, u % 2, :]
                if u < 2:
                    slot = slot.rearrange("p (a c) -> p a c", a=4)
                    load_dense([(slot[:, :, j * DK:(j + 1) * DK], w_in_k[:, 4 * u:4 * u + 4, bass.ds(c + h * DK, DK)])
                                for j, c in enumerate((C_Q, C_K))], u, before)
                else:
                    slot, k = slot.rearrange("p (a c) -> p a c", a=2), 2 * (u - 2)
                    load_dense([(slot[:, :, j * DV:(j + 1) * DV], w_in_k[:, k:k + 2, bass.ds(c + h * DV, DV)])
                                for j, c in enumerate((C_V, C_R))], u, before)

            def load_job(b, kind, cb, k, before=0):
                w = ((w_in_k[:, :, C_GA:C_GB], w_go_k), (w_in_k[:, :, C_GB:C_GB + D], w_mo_k))[b][kind]
                slot = d_raw[:, k % 2, :].rearrange("p (a c) -> p a c", a=KD)
                load_dense([(slot[:, i:i + 4, :], w[:, i:i + 4, bass.ds(cb * P, P)]) for i in (0, 4)], k, before)

            def load_out(u):
                n, cols = OUT0 + u, (slice(0, HALF), slice(HALF, D))
                load_dense([(d_raw[:, n % 2, c], w_o_k[:, u % KD, c]) for c in cols], n)

            def load_a2(h):
                sp.dma_start(w_a2[:, 0, :], gla_wa2_f[:, bass.ds(h * DK, DK)]).then_inc(wa_in, 16)
                sp.dma_start(w_a2[:, 1, :], gla_wa2_b[:, bass.ds(h * DK, DK)]).then_inc(wa_in, 16)
                for d, b in enumerate((gla_ba_f, gla_ba_b)):
                    sp.dma_start(b_a2[:, d:d + 1], b[bass.ds(h * DK, DK)].rearrange("(p a) -> p a", a=1),
                                 allow_slow_non_contiguous=True).then_inc(wa_in, 16)

            load_up(0)
            load_gla(0, 0)
            load_gla(0, 1)
            load_a2(0)

            def mla_turn(h, last):
                if not last:
                    sp.wait_ge(prj_mm, h * 8 + 8)
                    load_up(h + 1)
                for j in range(2):
                    cols = slice(j * HALF, (j + 1) * HALF)
                    sp.wait_ge(ob_ev, h * 2 + j + 1 + CREDIT)
                    sp.dma_start(ob_dram[bass.ds(h, 1), :, cols].rearrange("a p s -> p (a s)"),
                                 obS[:, cols]).then_inc(ob_out, 16)

            with sp.Fori(0, MH - 1) as h:
                mla_turn(h, False)
            mla_turn(MH - 1, True)

            def store_oa(h):
                sp.wait_ge(oa_dve, h * 2 + 2)
                sp.wait_ge(oa_act, h * 2 + 2)
                sp.dma_start(oa_dram[bass.ds(h * 2, 2)].rearrange("a p s -> p a s"), oaS[:]).then_inc(oa_out, 16)

            def gla_turn(h, first=False, last=False):
                load_gla(h, 2, h * GLA_UNITS)
                load_gla(h, 3, h * GLA_UNITS)
                if not first:
                    store_oa(h - 1)
                load_gla(h, 4, h * GLA_UNITS)
                load_gla(h, 5, h * GLA_UNITS)
                if not last:
                    sp.wait_ge(z_dve, h * 2 + 2)
                    load_a2(h + 1)
                    load_gla(h + 1, 0, (h + 1) * GLA_UNITS)
                    load_gla(h + 1, 1, (h + 1) * GLA_UNITS)

            gla_turn(0, first=True)
            with sp.Fori(1, GH - 1) as h:
                gla_turn(h)
            gla_turn(GH - 1, last=True)

            def load_branch(b):
                src = (oa_dram, ob_dram)[b]
                for k in range(KD):
                    if b or k >= 2:
                        sp.wait_ge(oT_lo_ok, b * KD + k - 1)
                    sp.dma_start(stage[:, k % 2, :], src[k]).then_inc(stage_in[k % 2], 16)

            def load_turn(b, r):
                before = MERGE0 + b * JOBS + r * 4
                for i in range(2):
                    load_job(b, 1, r * 2 + i, 2 + 2 * i, before)
                    load_job(b, 0, r * 2 + i + 2, 3 + 2 * i, before)

            for b in range(2):
                n = MERGE0 + b * JOBS
                load_job(b, 0, 0, n)
                load_job(b, 0, 1, n + 1)
                if b == 0:
                    store_oa(GH - 1)
                    sp.wait_ge(oa_out, 16 * GH)
                    sp.wait_ge(ob_out, 32 * MH + CREDIT)
                load_branch(b)
                with sp.Fori(0, 3) as r:
                    load_turn(b, r)
                load_job(b, 1, 6, n + 14)
                load_job(b, 1, 7, n + 15)
            load_out(0)
            load_out(1)
            sp.wait_ge(d_used, OUT0)
            sp.dma_start(g_ffn_b[:], spread(g_ffn, D)).then_inc(gf_in, 16)
            for t in range(NT):
                sp.dma_start(x1[:, t, :], x_rows[t * P:(t + 1) * P, :]).then_inc(x1_in, 16)
            for u in range(2, 2 * KD):
                load_out(u)
            for t in range(NT):
                sp.wait_ge(h2_ok, t + 1)
                sp.dma_start(h2_dram[t * P:(t + 1) * P, :], h2[:, t, :]).then_inc(rows_out, 16)
                sp.dma_start(out_rows[t * P:(t + 1) * P, :], x1[:, t, :]).then_inc(rows_out, 16)
            sp.wait_ge(rows_out, 32 * NT)

            def load_unit(e, unit, n, turn=0):
                m, j, k = unit
                if n >= RING:
                    sp.wait_ge(lo_ok, turn * UNITS + n - RING + 1)
                w = {"g": w_gate_e, "u": w_up_e, "d": w_down_e}[m]
                src = w[bass.ds(e, 1)].rearrange("a (k p) f -> p (a k) f", p=P)
                if m == "d":
                    src = src[:, 4 * j + k, :]
                    dst = w_raw[:, n % RING, :]
                else:
                    src = src[:, 2 * k:2 * k + 2, j * HALF:(j + 1) * HALF]
                    dst = w_raw[:, n % RING, :].rearrange("p (a c) -> p a c", a=2)
                sp.dma_start(dst, src).then_inc(raw_in[n % RING], 16)

            sp.wait_ge(lg_mm, NT)
            first = TURN[4:12] + TURN[16:24]
            for n in range(FIRST):
                load_unit(0, first[n], n)
            with sp.Fori(0, NE - 1) as e:
                for u, unit in enumerate(TURN):
                    load_unit(e if unit[0] == "d" else e + 1, unit, FIRST + u, e)
            for u, unit in enumerate(TURN[0:4] + TURN[12:16]):
                load_unit(NE - 1, unit, FIRST + (NE - 1) * UNITS + u)

        @block.gpsimd
        def _(pool):
            for s in (ob_ev, pt_dve, pt_act, ye_ok, ob_out, ye_free):
                pool.sem_inc(s, CREDIT)
            pool.sem_inc(y_ev, PAIRS)
            st = Steps(pool, pool_step)
            pool.memset(minus_half[:], -0.5).then_inc(consts, 1)
            st.link(pool.memset(ident[:], 0.0))
            pool.affine_select(out=ident[:], in_=ident[:], compare_op=ALU.not_equal, fill=1.0, base=0,
                               pattern=[[-1, P]], channel_multiplier=1).then_inc(consts, 1)
            for j, f in enumerate(rope_frequencies()):
                ins = pool.memset(freq[:, j:j + 1], f)
            ins.then_inc(consts, 1)

            def rsqrt(dst, ready, count, done):
                pool.wait_ge(ready, count)
                pool.tensor_tensor(dst, dst, minus_half[:, 0:dst.shape[1]], ALU.pow).then_inc(done, 1)

            pool.wait_ge(consts, 3)
            for t in range(NT):
                rsqrt(stat[:, 0, t:t + 1], ms_x, t + 1, rstd_x)
            for t in range(NT):
                rsqrt(stat[:, 1:3, t], lat_ms, t + 1, lat_rs)
            for h in range(MH):
                rsqrt(stat[:, 4, :], head_ms, 2 * h + 1, head_rs)
                rsqrt(stat[:, 5, :], head_ms, 2 * h + 2, head_rs)
            pool.wait_ge(pv_mm, 2 * MH)
            pool.wait_ge(ob_out, 32 * MH + CREDIT)
            st.mark(pool.memset(keep_hi[:], BIG))
            st.link(pool.memset(scan_m[:], 1.0))
            st.mark(pool.memset(scan_m[:, 0:S:CH], 0.0))
            st.mark(pool.affine_select(out=keep_hi[:, 0, :], in_=keep_hi[:, 0, :], compare_op=ALU.is_ge, fill=0.0,
                                       base=0, pattern=[[1, P]], channel_multiplier=-1))
            st.link(pool.affine_select(out=keep_hi[:, 1, :], in_=keep_hi[:, 1, :], compare_op=ALU.is_gt, fill=0.0,
                                       base=0, pattern=[[-1, P]], channel_multiplier=1))
            st.mark(pool.memset(keep_hi[0:CH, 0, CH:P], 0.0))
            st.link(pool.memset(keep_hi[CH:P, 1, 0:CH], 0.0))
            pool.tensor_scalar(keep_lo[:], keep_hi[:], -1.0, 0.0, ALU.mult, ALU.add).then_inc(gate_consts, 1)
            for h in range(GH):
                for j in range(2):
                    rsqrt(stat[:, 6, 4 * j:4 * j + 4], o_ms, 2 * h + j + 1, o_rs)
            for t in range(NT):
                rsqrt(stat[:, 7, t:t + 1], x1_ms, t + 1, x1_rs)

            pool.wait_ge(idx_ok, 2)
            pool.wait_ge(rows_out, 32 * NT)

            def gather(e):
                if e:
                    pool.wait_ge(xe_tr, 2 * e)
                pool.indirect_dma_start(xe[:], None, h2_dram,
                                        bass.IndirectOffsetOnAxis(ap=idx_c[:, e:e + 1], axis=0)).then_inc(xe_in, 16)

            gather(0)
            for e in range(NE):
                if e + 1 < NE:
                    gather(e + 1)
                if e:
                    pool.wait_ge(ye_out, 16 * e)
                    pool.sem_inc(ye_free, 1)
                pool.wait_ge(ye_ok, e + 1 + CREDIT)
                pool.indirect_dma_start(out_rows, bass.IndirectOffsetOnAxis(ap=idx_c[:, e:e + 1], axis=0),
                                        ye[:], None, compute_op=ALU.add).then_inc(ye_out, 16)
            pool.wait_ge(ye_out, 16 * NE)

        @block.tensor
        def _(pe):
            def transpose4(bank, rows, srcs):
                for j, src in enumerate(srcs):
                    ins = pe.transpose(ps[0:rows, bank, j * P:(j + 1) * P], src, ident[:])
                return ins

            pe.wait_ge(consts, 3)
            for c in range(2 * KD):
                half, k = divmod(c, KD)
                pe.wait_ge(xn, 4 * half + 4)
                if c >= 4:
                    pe.wait_ge(hT_dve if c % 2 == 0 else hT_act, (c - 4) // 2 + 1)
                transpose4(c % 4, P, [xs[:, 4 * half + j, k * P:(k + 1) * P] for j in range(4)]).then_inc(hT_tr, 1)

            for t in range(NT):
                pe.wait_ge(hT_dve, 4 * (t // 4) + 4)
                pe.wait_ge(hT_act, 4 * (t // 4) + 4)
                if t >= 2:
                    pe.wait_ge(lat_ev, t - 1)
                a, b = 4 + 2 * (t % 2), 5 + 2 * (t % 2)
                for k in range(KD):
                    if t == 0 and k % 4 == 0:
                        pe.wait_ge(wlat_in[k // 4], 16)
                    lhs = hT[:, k, t * P:(t + 1) * P]
                    pe.matmul(ps[:, a, 0:LA], lhs, w_lat[:, k, 0:LA], start=k == 0, stop=k == KD - 1)
                    mm = pe.matmul(ps[:, b, 0:LB], lhs, w_lat[:, k, LA:LAT], start=k == 0, stop=k == KD - 1)
                mm.then_inc(lat_mm, 1)
            for c in range(14):
                half, j = divmod(c, 7)
                pe.wait_ge(lat_n, 4 * half + 4)
                if c >= 4:
                    pe.wait_ge(latT_dve if c % 2 == 0 else latT_act, (c - 4) // 2 + 1)
                lo = (0, RANK)[j] if j < 2 else 2 * RANK + (j - 2) * P
                w = RANK if j < 2 else P
                transpose4(c % 4, w, [lat_r[:, 4 * half + t, lo:lo + w] for t in range(4)]).then_inc(lat_tr, 1)

            pe.wait_ge(latT_dve, 7)
            pe.wait_ge(latT_act, 7)
            pe.wait_ge(lat_ev, NT)

            def project(n, g):
                if g == 0:
                    pe.wait_ge(wu_in, n * 32 + 32)
                pe.wait_ge(prj_ev, n * 8 + g)
                width = HQ if g < 4 else NOPE + MV
                src, w, kc = (cqT, w_uq_h, QR // P) if g < 4 else (ckvT, w_ukv_h, KVR // P)
                for j in range(2):
                    t = 2 * (g % 4) + j
                    for k in range(kc):
                        mm = pe.matmul(ps[:, 7, j * width:(j + 1) * width], src[:, k, t * P:(t + 1) * P], w[:, k, :],
                                       start=k == 0, stop=k == kc - 1)
                mm.then_inc(prj_mm, 1)

            for g in range(8):
                project(0, g)

            def mla_head(i, last):
                pe.wait_ge(prj_ev, i * 8 + 8)
                pe.wait_ge(ob_ev, i * 2 + CREDIT)
                for c in range(8):
                    what, half = divmod(c, 2)
                    if c in (0, 4):
                        pe.wait_ge(head_n, i * 2 + c // 4 + 1)
                    srcs = []
                    for j in range(4):
                        t = 4 * half + j
                        srcs.append((qR[:, t, 0:NOPE], qR[:, t, NOPE:HQ], kvR[:, t, 0:NOPE], kRr[:, t, :])[what])
                    transpose4((4 + c) % 8, NOPE if what % 2 == 0 else ROPE, srcs).then_inc(seam_tr, 1)
                pe.wait_ge(seam_dve, i * 4 + 4)
                pe.wait_ge(seam_act, i * 4 + 4)
                for n in range(10):
                    if n < 8:
                        if n >= 2:
                            pe.wait_ge(exp_ok, i * 8 + n - 1)
                        for j in range(2):
                            cols = slice(j * HALF, (j + 1) * HALF)
                            bank = ps[:, 2 * (n % 2) + j, :]
                            pe.matmul(bank, qT[:, n * P:(n + 1) * P], kT[:, cols], start=True, stop=False)
                            mm = pe.matmul(bank, qTr[:, n * P:(n + 1) * P], kTr[:, cols], start=False, stop=True)
                        mm.then_inc(s_mm, 1)
                        if not last:
                            project(i + 1, n)
                    if n >= 2:
                        q = n - 2
                        pe.wait_ge(p_ok, i * 8 + q + 1)
                        pe.wait_ge(pt_dve, i * 8 + q + CREDIT)
                        pe.wait_ge(pt_act, i * 8 + q + CREDIT)
                        for b in range(2):
                            transpose4(4 + b, P, [probs[:, q % 3, (4 * b + j) * P:(4 * b + j + 1) * P]
                                                  for j in range(4)]).then_inc(p_tr, 1)
                    if n in (5, 9):
                        j = (n - 5) // 4
                        pe.wait_ge(pt_dve, i * 8 + 4 * j + 4 + CREDIT)
                        pe.wait_ge(pt_act, i * 8 + 4 * j + 4 + CREDIT)
                        if j == 0:
                            pe.wait_ge(v_ok, i + 1)
                        else:
                            pe.wait_ge(ob_ev, i * 2 + 1 + CREDIT)
                        for k in range(NT):
                            mm = pe.matmul(ps[:, 6, :], vS[:, k, :], probsT[:, j, k, :], start=k == 0, stop=k == NT - 1)
                        mm.then_inc(pv_mm, 1)

            with pe.Fori(0, MH - 1) as i:
                mla_head(i, False)
            mla_head(MH - 1, True)

            pe.wait_ge(ob_ev, 2 * MH + CREDIT)

            def three(out_ap, a_hi, a_lo, b_hi, b_lo, start, stop):
                pe.matmul(out_ap, a_hi, b_hi, start=start, stop=False)
                pe.matmul(out_ap, a_hi, b_lo, start=False, stop=False)
                return pe.matmul(out_ap, a_lo, b_hi, start=False, stop=stop)

            def gate_logits(h, d):
                for half in range(2):
                    mm = pe.matmul(ps[:, 4 + 2 * d + half, :], w_a2[:, d, :],
                                   gateT[:, d, half * HALF:(half + 1) * HALF], start=True, stop=True)
                mm.then_inc(z_mm, 1)

            def project_qk(h, u, first):
                pe.wait_ge(d_lo_ok, h * GLA_UNITS + u + 1)
                for i in range(4):
                    k = 4 * u + i
                    if first:
                        pe.wait_ge(hT_lo_ok, k + 1)
                    for j in range(2):
                        cols = slice((2 * i + j) * P, (2 * i + j + 1) * P)
                        for half in range(2):
                            toks = slice(half * HALF, (half + 1) * HALF)
                            mm = three(ps[:, 2 * j + half, :], d_hi[:, u, cols], d_lo[:, u, cols],
                                       hT_hi[:, k, toks], hT_lo[:, k, toks], k == 0, k == KD - 1)
                mm.then_inc(d_used, 1)

            def project_vr(h, u):
                pe.wait_ge(d_lo_ok, h * GLA_UNITS + u + 1)
                for i in range(2):
                    k = 2 * (u - 2) + i
                    cols = slice(i * HALF, (i + 1) * HALF)
                    for t in (4, 5, 0, 1, 2, 3, 6, 7) if k == 0 else range(NT):
                        if k == 0 and t < 4:
                            pe.wait_ge(qk_ev, h * 4 + t + 1)
                        if k == 0 and t == 6:
                            pe.wait_ge(z_dve, h * 2 + 2)
                        toks = slice(t * P, (t + 1) * P)
                        mm = three(ps[:, t, :], hT_hi[:, k, toks], hT_lo[:, k, toks],
                                   d_hi[:, u % 2, cols], d_lo[:, u % 2, cols], k == 0, k == KD - 1)
                        if k == KD - 1 and t < NT - 1:
                            mm.then_inc(vr_mm, 1)
                mm.then_inc(d_used, 1)

            def outputs_T(h):
                for c in range(4):
                    half, j = divmod(c, 2)
                    pe.wait_ge(o_n, h * 2 + half + 1)
                    transpose4(4 + c, P, [oR[:, 4 * half + t, j * P:(j + 1) * P] for t in range(4)]).then_inc(o_tr, 1)

            def gla_head(h, first=False):
                pe.wait_ge(wa_in, h * 64 + 64)
                gate_logits(h, 0)
                if not first:
                    pe.wait_ge(o_ev, h * NT)
                project_qk(h, 0, first)
                if not first:
                    pe.wait_ge(z_dve, h * 2 + 1)
                    outputs_T(h - 1)
                project_qk(h, 1, first)
                if not first:
                    pe.wait_ge(oa_dve, h * 2)
                    pe.wait_ge(oa_act, h * 2)
                gate_logits(h, 1)
                pe.wait_ge(z_dve, h * 2 + 1)
                for u in range(2, GLA_UNITS):
                    project_vr(h, u)
                for d in range(2):
                    pe.wait_ge(mats_ok, h * 6 + 3 * d + 3)
                    for half in range(2):
                        c = 2 * d + half
                        pe.wait_ge(vr_ev, h * NT + c + 1)
                        transpose4(c, P, [kd[:, d, (4 * half + j) * P:(4 * half + j + 1) * P]
                                          for j in range(4)]).then_inc(kd_tr, 1)
                for half in range(2):
                    for d in range(2):
                        pe.wait_ge(vr_ev, h * NT + 2 * half + d + 5)
                        for j in range(4):
                            cols = slice((4 * half + j) * P, (4 * half + j + 1) * P)
                            mm = pe.matmul(ps[:, 4 + 2 * half + d, j * P:(j + 1) * P], kt[:, d, cols], qt[:, d, cols],
                                           start=True, stop=True)
                        mm.then_inc(att_mm, 1)
                pe.wait_ge(kd_ev, h * 4 + 4)
                pe.wait_ge(att_ok, h * 10 + 10)
                for n in range(30):
                    d, c = (1, NCH - 1 - n) if n < 15 else (0, n - 15)
                    if n >= 4:
                        pe.wait_ge(st_ok, h * 32 + n - 1)
                    r0 = CH * (c % 2)
                    mm = pe.matmul(ps[:, 4 + n % 4, 0:DV],
                                   kdR[r0:r0 + CH, d, c // 2, :], vr[r0:r0 + CH, c // 2, 0:DV], start=True, stop=True)
                    mm.then_inc(ds_mm, 1)
                for t in range(NT):
                    pe.wait_ge(st_ok, h * 32 + 17 + min(2 * t + 1, NCH - 1))
                    if t >= 4:
                        pe.wait_ge(o_ev, h * NT + t - 3)
                    pe.matmul(ps[:, t % 4, 0:DV], att[:, t, :], vr[:, t, 0:DV], start=True, stop=False,
                              skip_group_check=True)
                    for c in (2 * t, 2 * t + 1):
                        r0 = CH * (c % 2)
                        for d in range(2):
                            mm = pe.matmul(ps[r0:r0 + CH, t % 4, 0:DV], qt[:, d, c * CH:(c + 1) * CH],
                                           state[:, d, c, :], start=False, stop=True, skip_group_check=True)
                    mm.then_inc(o_mm, 1)

            gla_head(0, first=True)
            with pe.Fori(1, GH) as h:
                gla_head(h)
            outputs_T(GH - 1)

            def job(b, kind, i, n, turns=0):
                k = n % 2
                pe.wait_ge(d_lo_ok, turns * 4 + n + 1)
                before = b * KD + i - 1
                if kind:
                    pe.wait_ge(y_ev, turns * 2 + before + PAIRS)
                elif before >= 1:
                    pe.wait_ge(g_ev, turns * 2 + before)
                bank = 4 * kind + 2 * (i % 2)
                rhs_hi, rhs_lo = ((hT_hi, hT_lo), (oT_hi, oT_lo))[kind]
                for half in range(2):
                    toks = slice(half * HALF, (half + 1) * HALF)
                    for c in range(KD):
                        cols = slice(c * P, (c + 1) * P)
                        mm = three(ps[:, bank + half, :], d_hi[:, k, cols], d_lo[:, k, cols],
                                   rhs_hi[:, c, toks], rhs_lo[:, c, toks], c == 0, c == KD - 1)
                mm.then_inc(d_used, 1)

            pe.wait_ge(o_ev, GH * NT)
            for b in range(2):
                n = MERGE0 + b * JOBS
                job(b, 0, 0, n)
                job(b, 0, 1, n + 1)
                if b == 0:
                    pe.wait_ge(oa_dve, 2 * GH)
                    pe.wait_ge(oa_act, 2 * GH)
                pe.wait_ge(oT_lo_ok, KD * b + KD)
                with pe.Fori(0, 3) as r:
                    for i in range(2):
                        job(b, 1, i, n + 2 + 2 * i, r)
                        job(b, 0, i + 2, n + 3 + 2 * i, r)
                job(b, 1, 6, n + 14)
                job(b, 1, 7, n + 15)

            pe.wait_ge(g_ev, 2 * KD)
            for g in range(2):
                for k in range(KD):
                    n = OUT0 + g * KD + k
                    pe.wait_ge(d_lo_ok, n + 1)
                    if g == 0:
                        pe.wait_ge(mT_lo_ok, k + 1)
                    for half, j in [(a, b) for a in range(2) for b in range(4)] if g == k == 0 else                             [(a, b) for b in range(4) for a in range(2)]:
                        if g == k == half == 0 or k > 0:
                            pass
                        elif g == 0:
                            pe.wait_ge(y_ev, 2 * KD - (j < 2) + PAIRS)
                        else:
                            pe.wait_ge(f_ev, 2 * j + half + 1)
                        toks = slice((4 * g + j) * P, (4 * g + j + 1) * P)
                        cols = slice(half * HALF, (half + 1) * HALF)
                        mm = three(ps[:, 4 * half + j, :], mT_hi[:, k, toks], mT_lo[:, k, toks],
                                   d_hi[:, n % 2, cols], d_lo[:, n % 2, cols], k == 0, k == KD - 1)
                        if k == KD - 1 and 2 * j + half < 7:
                            mm.then_inc(f_mm, 1)
                    mm.then_inc(d_used, 1)

            pe.wait_ge(f_ev, 16)

            def rows_T(t):
                pe.wait_ge(h2_ok, t + 1)
                if t >= 2:
                    pe.wait_ge(h2T_dve, t - 1)
                    pe.wait_ge(h2T_act, t - 1)
                for b in range(2):
                    transpose4(2 * (t % 2) + b, P, [h2[:, t, (4 * b + j) * P:(4 * b + j + 1) * P]
                                                    for j in range(4)]).then_inc(h2_tr, 1)

            def logits(t):
                pe.wait_ge(h2T_dve, t + 1)
                pe.wait_ge(h2T_act, t + 1)
                for k in range(KD):
                    mm = pe.matmul(ps[:, 7, t * NE:(t + 1) * NE], h2T[:, t % 2, k, :], w_router_s[:, k, :],
                                   start=k == 0, stop=k == KD - 1)
                mm.then_inc(lg_mm, 1)

            for t in range(NT + 1):
                if t < NT:
                    rows_T(t)
                if t:
                    logits(t - 1)
            pe.wait_ge(soft, 5)
            for t in range(NT):
                mm = pe.transpose(ps[0:NE, t // 4, (t % 4) * P:(t % 4 + 1) * P], aff[:, t, :], ident[:])
            mm.then_inc(aff_tr, 1)
            pe.wait_ge(top_ok, 1)
            pe.transpose(ps[:, 2, 0:NE], top_v[:], ident[0:NE, 0:NE])
            pe.transpose(ps[:, 2, NE:2 * NE], top_f[:], ident[0:NE, 0:NE]).then_inc(top_tr, 1)

            def expert_rows_T(e):
                pe.wait_ge(xe_in, e * 16 + 16)
                if not isinstance(e, int):
                    pe.wait_ge(act_ok, e * 2 - 1)
                for b in range(2):
                    transpose4(b, P, [xe[:, (4 * b + j) * P:(4 * b + j + 1) * P] for j in range(4)]).then_inc(xe_tr, 1)

            def gate_up(e, j, n, turn=0):
                pe.wait_ge(xeT_lo_ok, e * 2 + 2)
                for u in range(8):
                    pe.wait_ge(lo_ok, turn * UNITS + n + u + 1)
                    for i in range(2):
                        k = u // 2 * 2 + i
                        w = (n + u) % RING, slice(i * HALF, (i + 1) * HALF)
                        mm = three(ps[:, 2 * j + u % 2, :], xeT_hi[:, k, :], xeT_lo[:, k, :],
                                   w_hi[:, w[0], w[1]], w_lo[:, w[0], w[1]], k == 0, k == KD - 1)
                    mm.then_inc(w_used, 1)

            def act_rows_T(e, j):
                pe.wait_ge(act_ok, e * 2 + j + 1)
                transpose4(6 + j, P, [act_r[:, j, c * P:(c + 1) * P] for c in range(4)]).then_inc(a_tr, 1)

            def down(e, j, n, turn=0):
                pe.wait_ge(aT_lo_ok, e * 2 + j + 1)
                if j == 0:
                    pe.wait_ge(ye_ok, e + CREDIT)
                for k in range(4):
                    pe.wait_ge(lo_ok, turn * UNITS + n + k + 1)
                    for half in range(2):
                        w = (n + k) % RING, slice(half * HALF, (half + 1) * HALF)
                        mm = three(ps[:, 4 + half, :], act_T_hi[:, 4 * j + k, :], act_T_lo[:, 4 * j + k, :],
                                   w_hi[:, w[0], w[1]], w_lo[:, w[0], w[1]], j == 0 and k == 0, j == 1 and k == 3)
                    mm.then_inc(w_used, 1)

            expert_rows_T(0)
            gate_up(0, 0, 0)
            gate_up(0, 1, 8)
            with pe.Fori(0, NE - 1) as e:
                act_rows_T(e, 0)
                expert_rows_T(e + 1)
                down(e, 0, FIRST, e)
                act_rows_T(e, 1)
                gate_up(e + 1, 0, FIRST + 4, e)
                down(e, 1, FIRST + 12, e)
                gate_up(e + 1, 1, FIRST + 16, e)
            end = FIRST + (NE - 1) * UNITS
            act_rows_T(NE - 1, 0)
            down(NE - 1, 0, end)
            act_rows_T(NE - 1, 1)
            down(NE - 1, 1, end + 4)

        @block.vector
        def _(dve):
            st = Steps(dve, dve_a)

            def mean_eps(dst, src, n):
                return dve.tensor_scalar(dst, src, 1.0 / n, EPS, ALU.mult, ALU.add)

            def low_part(dst, whole, high):
                return dve.tensor_tensor(dst, whole, high.bitcast(F32), ALU.subtract)

            dve.wait_ge(small_in, 16 * small_loads)
            scale = 1.0 / math.sqrt(HQ)
            st.mark(dve.tensor_scalar(qhn_c[:], qhn_c[:], scale, None, ALU.mult))
            st.mark(dve.tensor_scalar(qhr_b[:], qhr_b[:], scale, None, ALU.mult))

            def x_scale(t):
                dve.wait_ge(rstd_x, t + 1)
                dve.tensor_scalar(xs[:, t, :], xs[:, t, :], stat[:, 0, t:t + 1], None, ALU.mult).then_inc(xn, 1)

            for t in range(NT):
                dve.wait_ge(ssq_x, t + 1)
                mean_eps(stat[:, 0, t:t + 1], stat[:, 0, t:t + 1], D).then_inc(ms_x, 1)
                if t:
                    x_scale(t - 1)
            x_scale(NT - 1)
            dve.wait_ge(consts, 3)
            st.link(dve.tensor_copy(pos_f[:], pos_i[:]))
            st.link(dve.tensor_tensor(ang[:], pos_f[:].unsqueeze(2).broadcast_to((P, NT, RH)),
                                      freq[:].unsqueeze(1).broadcast_to((P, NT, RH)), ALU.mult))
            two_pi = 2 * math.pi
            part1 = 6.25
            part2 = float(np.float32(round((two_pi - part1) * 2 ** 14) / 2 ** 14))
            part3 = two_pi - part1 - part2
            for j, shift in enumerate((0.0, 0.25)):
                st.mark(dve.tensor_scalar(turns_f[:, j], ang[:], 1 / two_pi, shift, ALU.mult, ALU.add))
            st.wait()
            st.link(dve.tensor_copy(turns_i[:], turns_f[:]))
            st.link(dve.tensor_copy(turns_f[:], turns_i[:]))
            for j, (dst, shift) in enumerate(((sin_t, 0.0), (cos_t, math.pi / 2))):
                st.link(dve.scalar_tensor_tensor(out=dst[:], in0=turns_f[:, j], scalar=-part1, in1=ang[:],
                                                 op0=ALU.mult, op1=ALU.add))
                for part in (part2, part3):
                    st.link(dve.scalar_tensor_tensor(out=dst[:], in0=turns_f[:, j], scalar=-part, in1=dst[:],
                                                     op0=ALU.mult, op1=ALU.add))
                st.link(dve.tensor_scalar(dst[:], dst[:], shift, 3.1415925, ALU.add, ALU.min))
                dve.tensor_scalar(dst[:], dst[:], -3.1415925, None, ALU.max).then_inc(trig_arg, 1)

            for c in range(0, 2 * KD, 2):
                half, k = divmod(c, KD)
                dve.wait_ge(hT_tr, c + 1)
                dve.tensor_scalar(hT[:, k, half * HALF:(half + 1) * HALF], ps[:, c % 4, :], g_mix_c[:, k:k + 1], None,
                                  ALU.mult).then_inc(hT_dve, 1)

            def lat_scale(t):
                dve.wait_ge(lat_rs, t + 1)
                st.mark(dve.tensor_scalar(lat_r[:, t, 2 * RANK:LA], lat_r[:, t, 2 * RANK:LA], stat[:, 1, t:t + 1], None,
                                          ALU.mult))
                dve.tensor_scalar(lat_r[:, t, LA:LA + KVR], lat_r[:, t, LA:LA + KVR], stat[:, 2, t:t + 1], None,
                                  ALU.mult).then_inc(lat_n, 1)

            for t in range(NT):
                a, b = 4 + 2 * (t % 2), 5 + 2 * (t % 2)
                dve.wait_ge(lat_mm, t + 1)
                dve.tensor_copy(lat_r[:, t, 0:LA], ps[:, a, 0:LA])
                dve.tensor_copy(lat_r[:, t, LA:LAT], ps[:, b, 0:LB]).then_inc(lat_ev, 1)
                if t:
                    lat_scale(t - 1)
                dve.wait_ge(lat_sq, t + 1)
                st.mark(mean_eps(stat[:, 1, t:t + 1], stat[:, 1, t:t + 1], QR))
                mean_eps(stat[:, 2, t:t + 1], stat[:, 2, t:t + 1], KVR).then_inc(lat_ms, 1)
            lat_scale(NT - 1)

            def lat_out(c):
                half, j = divmod(c, 7)
                cols = slice(half * HALF, (half + 1) * HALF)
                if j < 2:
                    return gateT[:, j, cols], ps[0:RANK, c % 4, :], 1.0
                if j < 5:
                    return cqT[:, j - 2, cols], ps[:, c % 4, :], qn_c[:, j - 2:j - 1]
                return ckvT[:, j - 5, cols], ps[:, c % 4, :], kvn_c[:, j - 5:j - 4]

            for c in range(0, 14, 2):
                dve.wait_ge(lat_tr, c + 1)
                dst, src, gain = lat_out(c)
                dve.tensor_scalar(dst, src, gain, None, ALU.mult).then_inc(latT_dve, 1)

            def rotate(dst, src, tmp, steps):
                x1r, x2r = src[:, :, 0:RH], src[:, :, RH:ROPE]
                steps.mark(dve.tensor_tensor(tmp[:, 0], x1r, cos_t[:], ALU.mult))
                steps.mark(dve.tensor_tensor(tmp[:, 1], x2r, sin_t[:], ALU.mult))
                steps.mark(dve.tensor_tensor(tmp[:, 2], x2r, cos_t[:], ALU.mult))
                steps.mark(dve.tensor_tensor(tmp[:, 3], x1r, sin_t[:], ALU.mult))
                steps.wait()
                steps.mark(dve.tensor_tensor(dst[:, :, 0:RH], tmp[:, 0], tmp[:, 1], ALU.subtract))
                return dve.tensor_tensor(dst[:, :, RH:ROPE], tmp[:, 2], tmp[:, 3], ALU.add)

            st.link(dve.tensor_tensor(k_rot[:], lat_r[:, :, LA + KVR:LAT],
                                      khr_b[:].unsqueeze(1).broadcast_to((P, NT, ROPE)), ALU.mult))
            dve.wait_ge(trig, 2)
            rotate(k_rot[:], k_rot[:], lat_r[:, 0:4, 0:NT * RH].rearrange("p a (t r) -> p a t r", t=NT), st) \
                .then_inc(k_rot_ok, 1)

            dve.wait_ge(latT_act, 7)

            def q_stats(n, s):
                dve.wait_ge(head_sq, n * 2 + 1)
                s.link(dve.tensor_reduce(stat[:, 4, :], sq_q[:], AX, ALU.add))
                mean_eps(stat[:, 4, :], stat[:, 4, :], HQ).then_inc(head_ms, 1)

            def q_norm(n, s):
                dve.wait_ge(head_rs, n * 2 + 1)
                s.link(dve.tensor_tensor(qR[:], qR[:], stat[:, 4, :].unsqueeze(2).broadcast_to((P, NT, HQ)), ALU.mult))
                s.link(dve.tensor_tensor(qR[:, :, NOPE:HQ], qR[:, :, NOPE:HQ],
                                         qhr_b[:].unsqueeze(1).broadcast_to((P, NT, ROPE)), ALU.mult))
                rotate(qR[:, :, NOPE:HQ], qR[:, :, NOPE:HQ], r_tmp, s).then_inc(head_n, 1)

            def k_stats(n, s):
                dve.wait_ge(head_sq, n * 2 + 2)
                s.link(dve.tensor_reduce(stat[:, 5, :], sq_q[:, :, 0:NOPE], AX, ALU.add))
                s.link(dve.tensor_tensor(stat[:, 5, :], stat[:, 5, :], stat[:, 3, :], ALU.add))
                mean_eps(stat[:, 5, :], stat[:, 5, :], HQ).then_inc(head_ms, 1)

            def k_norm(n, s):
                dve.wait_ge(head_rs, n * 2 + 2)
                s.mark(dve.tensor_tensor(kvR[:, :, 0:NOPE], kvR[:, :, 0:NOPE],
                                         stat[:, 5, :].unsqueeze(2).broadcast_to((P, NT, NOPE)), ALU.mult))
                dve.tensor_tensor(kRr[:], k_rot[:], stat[:, 5, :].unsqueeze(2).broadcast_to((P, NT, ROPE)),
                                  ALU.mult).then_inc(head_n, 1)

            prep = 1 + 1 + 1 + 5 + 1 + 1 + 1
            s0 = Steps(dve, head_step, per=prep)
            dve.wait_ge(lat_sq, NT)
            dve.wait_ge(k_rot_ok, 1)
            q_stats(0, s0)
            q_norm(0, s0)
            k_stats(0, s0)
            k_norm(0, s0)
            s0.end()

            def mla_head(i, last):
                s = Steps(dve, head_step, base=prep, turn=i, per=prep)
                for c in range(0, 8, 2):
                    what = c // 2
                    dve.wait_ge(seam_tr, i * 8 + c + 1)
                    if what == 0:
                        ins = dve.tensor_scalar(qT[:, 0:HALF], ps[:, 4, :], qhn_c[:, 0:1], None, ALU.mult)
                    elif what == 1:
                        ins = dve.tensor_copy(qTr[:, 0:HALF], ps[0:ROPE, 6, :])
                    elif what == 2:
                        ins = dve.tensor_scalar(kT[:, 0:HALF], ps[:, 0, :], khn_c[:, 0:1], None, ALU.mult)
                    else:
                        ins = dve.tensor_copy(kTr[:, 0:HALF], ps[0:ROPE, 2, :])
                    ins.then_inc(seam_dve, 1)
                dve.tensor_copy(vS[:], kvR[:, :, NOPE:NOPE + MV]).then_inc(v_ok, 1)

                def normalise(q):
                    dve.wait_ge(exp_ok, i * 8 + q + 1)
                    dve.reciprocal(row_inv[:, q:q + 1], row_sum[:, q:q + 1]).then_inc(inv_ok, 1)
                    dve.wait_ge(inv_ok, i * 8 + q + 1)
                    dve.tensor_scalar(probs[:, q % 3, :], probs[:, q % 3, :], row_inv[:, q:q + 1], None,
                                      ALU.mult).then_inc(p_ok, 1)

                def head_out(j):
                    dve.wait_ge(pv_mm, i * 2 + j + 1)
                    dve.wait_ge(ob_out, i * 32 + CREDIT)
                    cols = slice(j * HALF, (j + 1) * HALF)
                    dve.tensor_copy(obS[:, cols], ps[:, 6, :]).then_inc(ob_ev, 1)

                for n in range(10):
                    if n < 8:
                        dve.wait_ge(s_mm, i * 8 + n + 1)
                        dve.tensor_reduce(row_max[:, n:n + 1], ps[:, 2 * (n % 2):2 * (n % 2) + 2, :],
                                          mybir.AxisListType.XY, ALU.max, negate=True).then_inc(max_ok, 1)
                    if 1 <= n <= 8:
                        normalise(n - 1)
                    if n >= 2:
                        q = n - 2
                        dve.wait_ge(p_tr, i * 16 + 2 * q + 1)
                        dve.tensor_copy(probsT[:, q // 4, 0:4, (q % 4) * P:(q % 4 + 1) * P],
                                        ps[:, 4, :].rearrange("p (a c) -> p a c", a=4)).then_inc(pt_dve, 1)
                    if not last:
                        if n == 4:
                            q_stats(i + 1, s)
                        if n == 5:
                            q_norm(i + 1, s)
                        if n == 8:
                            k_stats(i + 1, s)
                        if n == 9:
                            k_norm(i + 1, s)
                    if n == 6:
                        head_out(0)
                head_out(1)
                if not last:
                    s.end()

            with dve.Fori(0, MH - 1) as i:
                mla_head(i, False)
            mla_head(MH - 1, True)

            def dense_lo(n, before=0):
                dve.wait_ge(d_hi_ok, before + n + 1)
                low_part(d_lo[:, n % 2, :], d_raw[:, n % 2, :], d_hi[:, n % 2, :]).then_inc(d_lo_ok, 1)

            dense_lo(0)
            dense_lo(1)
            dve.wait_ge(gate_consts, 1)
            dve.wait_ge(ob_out, 32 * MH + CREDIT)
            for k in range(KD):
                dve.wait_ge(hT_hi_ok, k + 1)
                low_part(hT_lo[:, k, :], hT[:, k, :], hT_hi[:, k, :]).then_inc(hT_lo_ok, 1)

            def outputs_even(h):
                for c in (0, 2):
                    half, j = divmod(c, 2)
                    dve.wait_ge(o_tr, h * 4 + c + 1)
                    dve.tensor_scalar(oaS[:, j, half * HALF:(half + 1) * HALF], ps[:, 4 + c, :], onorm_c[:, j:j + 1],
                                      None, ALU.mult).then_inc(oa_dve, 1)

            def gla_head(h, first=False):
                s = Steps(dve, gla_step, turn=h, per=2)
                mine = h * GLA_UNITS
                for d in range(2):
                    dve.wait_ge(z_mm, h * 2 + d + 1)
                    if d == 0:
                        dve.wait_ge(wa_in, h * 64 + 64)
                    zb = ps[:, 4 + 2 * d:6 + 2 * d, :]
                    z3 = zT[:].rearrange("p (a c) -> p a c", a=2)
                    if d == 1:
                        dve.wait_ge(ed_ok, h * 2 + 1)
                    dve.tensor_scalar(z3, zb, b_a2[:, d:d + 1], None, ALU.add).then_inc(z_dve, 1)
                    dve.wait_ge(z_act, h * 6 + 3 * d + 3)
                    dve.scalar_tensor_tensor(out=eT[:], in0=zT[:], scalar=0.0, in1=eT[:], op0=ALU.min,
                                             op1=ALU.subtract).then_inc(ls_ok, 1)
                    dve.wait_ge(ls_ok, h * 2 + d + 1)
                    rev = slice(None, None, -1) if d else slice(None)
                    if d == 1:
                        dve.wait_ge(e_ok, h * 4 + 2)
                    dve.tensor_tensor_scan(bT[:, rev], scan_m[:], eT[:, rev], 0.0, ALU.mult,
                                           ALU.add).then_inc(b_ok, 1)
                    dve.wait_ge(b_ok, h * 2 + d + 1)
                    b3 = bT[:].rearrange("p (n c) -> p n c", c=CH)
                    last = b3[:, :, 0:1] if d else b3[:, :, CH - 1:CH]
                    if d == 1:
                        dense_lo(4, mine)
                    dve.tensor_tensor(zT[:].rearrange("p (n c) -> p n c", c=CH), last.broadcast_to((P, NCH, CH)), b3,
                                      ALU.subtract).then_inc(tail_ok, 1)
                    dve.wait_ge(e_ok, h * 4 + 2 * d + 1)
                    e3 = qt[:, d, :].rearrange("p (n c) -> p n c", c=CH)
                    s.link(dve.tensor_copy(decay[:, d, :].unsqueeze(2), e3[:, :, 0:1] if d else e3[:, :, CH - 1:CH]))
                    if d == 0:
                        if not first:
                            outputs_even(h - 1)
                        dense_lo(2, mine)
                        dense_lo(3, mine)
                        dve.wait_ge(qk_ev, h * 4 + 4)
                    else:
                        dense_lo(5, mine)
                    dve.tensor_tensor(qt[:, d, :], qt[:, d, :], qk_T[:, 0, :], ALU.mult).then_inc(mats_ok, 1)
                    dve.wait_ge(e_ok, h * 4 + 2 * d + 2)
                    dve.tensor_tensor(kt[:, d, :], kt[:, d, :], qk_T[:, 1, :], ALU.mult).then_inc(mats_ok, 1)
                    dve.wait_ge(ed_ok, h * 2 + d + 1)
                    dve.tensor_tensor(kd[:, d, :], kd[:, d, :], qk_T[:, 1, :], ALU.mult).then_inc(mats_ok, 1)
                dense_lo(6, mine)
                dve.wait_ge(mats_ok, h * 6 + 6)
                for c in range(4):
                    d, half = divmod(c, 2)
                    dve.wait_ge(kd_tr, h * 4 + c + 1)
                    dve.tensor_copy(kdR[:, d, 4 * half:4 * half + 4, :],
                                    ps[:, c, :].rearrange("p (a c) -> p a c", a=4)).then_inc(kd_ev, 1)
                for half in range(2):
                    t4 = slice(4 * half, 4 * half + 4)
                    for d in range(2):
                        dve.wait_ge(att_mm, h * 4 + 2 * half + d + 1)
                        dst = (att_f, att_b)[d][:, t4, :]
                        src = ps[:, 4 + 2 * half + d, :].rearrange("p (a c) -> p a c", a=4)
                        dve.tensor_tensor(dst, src, keep_hi[:, d, :].unsqueeze(1).broadcast_to((P, 4, P)),
                                          ALU.min).then_inc(att_ok, 1)
                        dve.wait_ge(att_ok, h * 10 + half * 5 + 2 * d + 1)
                        dve.tensor_tensor(dst, dst, keep_lo[:, d, :].unsqueeze(1).broadcast_to((P, 4, P)),
                                          ALU.max).then_inc(att_ok, 1)
                    dve.wait_ge(att_ok, h * 10 + half * 5 + 4)
                    dve.tensor_tensor(att[:, t4, :], att_f[:, t4, :], att_b[:, t4, :], ALU.add).then_inc(att_ok, 1)
                dense_lo(7, mine)
                dve.memset(state[:, 1, NCH - 1, :], 0.0).then_inc(st_ok, 1)
                dve.memset(state[:, 0, 0, :], 0.0).then_inc(st_ok, 1)
                for n in range(30):
                    d, c = (1, NCH - 1 - n) if n < 15 else (0, n - 15)
                    to = c - 1 if d else c + 1
                    dve.wait_ge(ds_mm, h * 30 + n + 1)
                    dve.wait_ge(st_ok, h * 32 + n + 2)
                    dve.scalar_tensor_tensor(out=state[:, d, to, :], in0=state[:, d, c, :], scalar=decay[:, d, c:c + 1],
                                             in1=ps[:, 4 + n % 4, 0:DV],
                                             op0=ALU.mult, op1=ALU.add).then_inc(st_ok, 1)

                def o_scale(half):
                    dve.wait_ge(o_sq, h * NT + 4 * half + 4)
                    mean_eps(stat[:, 6, 4 * half:4 * half + 4], stat[:, 6, 4 * half:4 * half + 4], DV).then_inc(o_ms, 1)
                    dve.wait_ge(o_rs, h * 2 + half + 1)
                    if half == 0:
                        dve.wait_ge(silu_ok, h + 1)
                    for t in range(4 * half, 4 * half + 4):
                        ins = dve.scalar_tensor_tensor(out=oR[:, t, :], in0=oR[:, t, :], scalar=stat[:, 6, t:t + 1],
                                                       in1=vr[:, t, DV:2 * DV], op0=ALU.mult, op1=ALU.mult)
                    ins.then_inc(o_n, 1)

                for t in range(NT):
                    dve.wait_ge(o_mm, h * NT + t + 1)
                    dve.tensor_copy(oR[:, t, :], ps[:, t % 4, 0:DV]).then_inc(o_ev, 1)
                    if t == 5:
                        o_scale(0)
                o_scale(1)
                s.end()

            gla_head(0, first=True)
            with dve.Fori(1, GH) as h:
                gla_head(h)
            outputs_even(GH - 1)

            def product(b, i, n, turns=0):
                dve.wait_ge(d_used, turns * 4 + n + 1)
                dve.wait_ge(g_ev, turns * 2 + b * KD + i + 1)
                banks = ps[:, 4 + 2 * (i % 2):6 + 2 * (i % 2), :]
                gate = sg[:, i % 2, :]
                gate3 = gate.rearrange("p (a c) -> p a c", a=2)
                m = mT[:, bass.ds(turns * 2 + i, 1), :].rearrange("p a s -> p (a s)")
                if b == 0:
                    dve.tensor_tensor(m.rearrange("p (a c) -> p a c", a=2), banks, gate3, ALU.mult).then_inc(y_ev, 1)
                else:
                    dve.tensor_tensor(gate3, banks, gate3, ALU.mult).then_inc(y_ev, 1)
                    dve.wait_ge(y_ev, turns * 2 + b * KD + i + 1 + PAIRS)
                    dve.tensor_tensor(m, m, gate, ALU.add).then_inc(m_ok, 1)

            def merged_lo(k):
                dve.wait_ge(mT_hi_ok, k + 1)
                low_part(mT_lo[:, k, :], mT[:, k, :], mT_hi[:, k, :]).then_inc(mT_lo_ok, 1)

            for b in range(2):
                n = MERGE0 + b * JOBS
                for k in range(KD):
                    dve.wait_ge(oT_hi_ok, b * KD + k + 1)
                    low_part(oT_lo[:, k, :], stage[:, k % 2, :], oT_hi[:, k, :]).then_inc(oT_lo_ok, 1)
                dense_lo(n + 2)
                dense_lo(n + 3)
                with dve.Fori(0, 3) as r:
                    for i in range(2):
                        dense_lo(n + 4 + 2 * i, r * 4)
                        product(b, i, n + 2 + 2 * i, r)
                        dense_lo(n + 5 + 2 * i, r * 4)
                if b:
                    for k in range(6):
                        merged_lo(k)
                for i in (6, 7):
                    dense_lo(n + 10 + i)
                    product(b, i, n + 8 + i)
                    if b:
                        merged_lo(i)

            dve.wait_ge(x1_in, 16 * NT)
            dve.wait_ge(gf_in, 16)

            def ffn_norm(t):
                dve.wait_ge(x1_sq, t + 1)
                mean_eps(stat[:, 7, t:t + 1], stat[:, 7, t:t + 1], D).then_inc(x1_ms, 1)
                dve.wait_ge(x1_rs, t + 1)
                dve.scalar_tensor_tensor(out=h2[:, t, :], in0=x1[:, t, :], scalar=stat[:, 7, t:t + 1], in1=g_ffn_b[:],
                                         op0=ALU.mult, op1=ALU.mult).then_inc(h2_ok, 1)

            for g in range(2):
                for k in range(KD):
                    if k < KD - 1 and g * KD + k + 2 < 2 * KD:
                        dense_lo(OUT0 + g * KD + k + 2)
                    if g == 1 and 2 <= k < 6:
                        ffn_norm(k - 2)
                for j in range(4):
                    for half in range(2):
                        if 2 * j + half < 7:
                            dve.wait_ge(f_mm, g * 7 + 2 * j + half + 1)
                        else:
                            dve.wait_ge(d_used, OUT0 + (g + 1) * KD)
                        x = x1[:, 4 * g + j, half * HALF:(half + 1) * HALF]
                        dve.tensor_tensor(x, ps[:, 4 * half + j, :], x, ALU.add).then_inc(f_ev, 1)
                if g == 0:
                    dense_lo(OUT0 + KD + 1)
                else:
                    for j in range(4):
                        ffn_norm(4 + j)
            for t in range(NT):
                dve.wait_ge(h2_tr, 2 * t + 1)
                if t >= 2:
                    dve.wait_ge(lg_mm, t - 1)
                dve.tensor_copy(h2T[:, t % 2, 0:4, :], ps[:, 2 * (t % 2), :].rearrange("p (a c) -> p a c", a=4)) \
                    .then_inc(h2T_dve, 1)

            dve.wait_ge(lg_mm, NT)
            dve.wait_ge(rows_out, 32 * NT)
            lg = ps[:, 7, 0:NT * NE].rearrange("p (t e) -> p t e", t=NT)
            s = Steps(dve, soft)
            s.link(dve.tensor_reduce(stat[:, 8, :], lg, AX, ALU.max))
            s.mark(dve.tensor_tensor(aff[:], lg, stat[:, 8, :].unsqueeze(2).broadcast_to((P, NT, NE)), ALU.subtract))
            dve.wait_ge(soft_exp, 1)
            s.link(dve.tensor_reduce(stat[:, 9, :], aff[:], AX, ALU.add))
            s.link(dve.reciprocal(stat[:, 10, :], stat[:, 9, :]))
            s.mark(dve.tensor_tensor(aff[:], aff[:], stat[:, 10, :].unsqueeze(2).broadcast_to((P, NT, NE)), ALU.mult))
            dve.wait_ge(aff_tr, 1)
            t = Steps(dve, affT_ok)
            t.link(dve.tensor_copy(affT[:, 0, :].rearrange("p (a c) -> p a c", a=2), ps[0:NE, 0:2, :]))
            for r in range(CAP // 8):
                src, v8 = affT[:, r % 2, :], top_v[:, 8 * r:8 * r + 8]
                t.link(dve.max(v8, src))
                t.mark(dve.max_index(top_i[:, 8 * r:8 * r + 8], v8, src))
                t.link(dve.match_replace(affT[:, (r + 1) % 2, :], v8, src, -1.0))
            dve.tensor_copy(top_f[:], top_i[:]).then_inc(top_ok, 1)
            dve.wait_ge(top_tr, 1)
            dve.tensor_copy(val_c[:], ps[:, 2, 0:NE]).then_inc(idx_ok, 1)
            dve.tensor_copy(idx_c[:], ps[:, 2, NE:2 * NE]).then_inc(idx_ok, 1)
            dve.wait_ge(idx_ok, 2)

            def split(n, turn=0):
                dve.wait_ge(hi_ok, turn * UNITS + n + 1)
                low_part(w_lo[:, n % RING, :], w_raw[:, n % RING, :], w_hi[:, n % RING, :]).then_inc(lo_ok, 1)

            def rows_in(e):
                for b in range(2):
                    dve.wait_ge(xeT_hi_ok, e * 2 + b + 1)
                    rows = slice(4 * b, 4 * b + 4)
                    low_part(xeT_lo[:, rows, :], ps[:, b, :].rearrange("p (a c) -> p a c", a=4),
                             xeT_hi[:, rows, :]).then_inc(xeT_lo_ok, 1)

            def activate(e, j):
                dve.wait_ge(silu_e, e * 2 + j + 1)
                dve.tensor_tensor(act_r[:, j, :], ps[:, 2 * j + 1, :], silu_g[:, j, :], ALU.mult).then_inc(act_ok, 1)

            def act_in(e, j):
                dve.wait_ge(aT_hi_ok, e * 2 + j + 1)
                rows = slice(4 * j, 4 * j + 4)
                low_part(act_T_lo[:, rows, :], ps[:, 6 + j, :].rearrange("p (a c) -> p a c", a=4),
                         act_T_hi[:, rows, :]).then_inc(aT_lo_ok, 1)

            def affinity(e):
                dve.tensor_copy(val_s[:], val_c[:, bass.ds(e, 1)]).then_inc(val_ok, 1)

            rows_in(0)
            for n in range(FIRST):
                split(n)
                if n == 8 + LEAD - 1:
                    activate(0, 0)
            with dve.Fori(0, NE - 1) as e:
                for u in range(UNITS):
                    split(FIRST + u, e)
                    if u == LEAD - 1:
                        act_in(e, 0)
                        activate(e, 1)
                        rows_in(e + 1)
                    if u == 4 + LEAD - 1:
                        act_in(e, 1)
                    if u == 12 + LEAD - 1:
                        activate(e + 1, 0)
                        dve.wait_ge(ye_ok, e + CREDIT)
                        affinity(e)
            for u in range(8):
                split(FIRST + (NE - 1) * UNITS + u)
                if u == LEAD - 1:
                    act_in(NE - 1, 0)
                    activate(NE - 1, 1)
                if u == 4 + LEAD - 1:
                    act_in(NE - 1, 1)
            dve.wait_ge(ye_ok, NE - 1 + CREDIT)
            affinity(NE - 1)

        @block.scalar
        def _(act):
            nc.scalar.preload_act_table_set("natural_log_exp_and_others")
            loads = [(g_mix_c[:], col(g_mix, KD)), (qn_c[:], col(mla_q_norm, QR // P)),
                     (kvn_c[:], col(mla_kv_norm, KVR // P)), (onorm_c[:], col(gla_onorm, DV // P)),
                     (qhn_c[:], col(q_head_norm[0:NOPE], 1)), (khn_c[:], col(k_head_norm[0:NOPE], 1)),
                     (qhr_b[:], spread(q_head_norm[NOPE:HQ], ROPE)), (khr_b[:], spread(k_head_norm[NOPE:HQ], ROPE)),
                     (pos_i[:], positions.rearrange("b (t p) -> p (b t)", p=P)),
                     (w_router_s[:], w_router.rearrange("(k p) e -> p k e", p=P))]
            for dst, src in loads:
                act.dma_start(dst, src, allow_slow_non_contiguous=True).then_inc(small_in, 16)
            assert len(loads) == small_loads

            a_st = Steps(act, act_a)
            for t in range(NT):
                act.wait_ge(x_in[t], 16)
                nc.scalar.activation(sq_a[:], xs[:, t, :], ACT.Square, accum_out=stat[:, 0, t:t + 1]).then_inc(ssq_x, 1)
                act.wait_ge(ssq_x, t + 1)
            act.wait_ge(small_in, 16 * small_loads)
            for c in range(1, 2 * KD, 2):
                half, k = divmod(c, KD)
                act.wait_ge(hT_tr, c + 1)
                nc.scalar.activation(hT[:, k, half * HALF:(half + 1) * HALF], ps[:, c % 4, :], ACT.Copy,
                                     scale=g_mix_c[:, k:k + 1]).then_inc(hT_act, 1)
            for j, tbl in enumerate((sin_t, cos_t)):
                act.wait_ge(trig_arg, j + 1)
                nc.scalar.activation(tbl[:], tbl[:], ACT.Sin).then_inc(trig, 1)
            for t in range(NT):
                act.wait_ge(lat_ev, t + 1)
                a_st.link(nc.scalar.activation(sq_a[:, 0:QR], lat_r[:, t, 2 * RANK:LA], ACT.Square,
                                               accum_out=stat[:, 1, t:t + 1]))
                a_st.link(nc.scalar.activation(sq_a[:, 0:KVR], lat_r[:, t, LA:LA + KVR], ACT.Square,
                                               accum_out=stat[:, 2, t:t + 1]))
                nc.scalar.activation(sq_a[:, 0:ROPE], lat_r[:, t, LA + KVR:LAT], ACT.Square,
                                     accum_out=stat[:, 3, t:t + 1]).then_inc(lat_sq, 1)
                act.wait_ge(lat_sq, t + 1)
            for c in range(1, 14, 2):
                half, j = divmod(c, 7)
                cols = slice(half * HALF, (half + 1) * HALF)
                act.wait_ge(lat_tr, c + 1)
                if j < 2:
                    ins = nc.scalar.activation(gateT[:, j, cols], ps[0:RANK, c % 4, :], ACT.Copy)
                elif j < 5:
                    ins = nc.scalar.activation(cqT[:, j - 2, cols], ps[:, c % 4, :], ACT.Copy,
                                               scale=qn_c[:, j - 2:j - 1])
                else:
                    ins = nc.scalar.activation(ckvT[:, j - 5, cols], ps[:, c % 4, :], ACT.Copy,
                                               scale=kvn_c[:, j - 5:j - 4])
                ins.then_inc(latT_act, 1)

            act.wait_ge(k_rot_ok, 1)
            act.wait_ge(lat_tr, 14)

            def take(n, g):
                act.wait_ge(prj_mm, n * 8 + g + 1)
                width = HQ if g < 4 else NOPE + MV
                dst = (qR if g < 4 else kvR)[:, 2 * (g % 4):2 * (g % 4) + 2, :]
                if g == 4:
                    act.wait_ge(v_ok, n)
                nc.scalar.activation(dst, ps[:, 7, 0:2 * width].rearrange("p (a c) -> p a c", a=2),
                                     ACT.Copy).then_inc(prj_ev, 1)
                if g == 3:
                    act.wait_ge(prj_ev, n * 8 + 4)
                    act.wait_ge(head_ms, n * 2)
                    nc.scalar.activation(sq_q[:], qR[:], ACT.Square).then_inc(head_sq, 1)
                if g == 7:
                    act.wait_ge(prj_ev, n * 8 + 8)
                    act.wait_ge(head_ms, n * 2 + 1)
                    nc.scalar.activation(sq_q[:, :, 0:NOPE], kvR[:, :, 0:NOPE], ACT.Square).then_inc(head_sq, 1)

            for g in range(8):
                take(0, g)

            def mla_head(i, last):
                for c in range(1, 8, 2):
                    what = c // 2
                    act.wait_ge(seam_tr, i * 8 + c + 1)
                    if what == 0:
                        ins = nc.scalar.activation(qT[:, HALF:S], ps[:, 5, :], ACT.Copy, scale=qhn_c[:, 0:1])
                    elif what == 1:
                        ins = nc.scalar.activation(qTr[:, HALF:S], ps[0:ROPE, 7, :], ACT.Copy)
                    elif what == 2:
                        ins = nc.scalar.activation(kT[:, HALF:S], ps[:, 1, :], ACT.Copy, scale=khn_c[:, 0:1])
                    else:
                        ins = nc.scalar.activation(kTr[:, HALF:S], ps[0:ROPE, 3, :], ACT.Copy)
                    ins.then_inc(seam_act, 1)
                for n in range(10):
                    if n < 8:
                        act.wait_ge(max_ok, i * 8 + n + 1)
                        if n >= 3:
                            act.wait_ge(p_tr, i * 16 + 2 * (n - 3) + 2)
                        nc.scalar.activation(probs[:, n % 3, :].rearrange("p (a c) -> p a c", a=2),
                                             ps[:, 2 * (n % 2):2 * (n % 2) + 2, :], ACT.Exp, bias=row_max[:, n:n + 1],
                                             accum_out=row_sum[:, n:n + 1]).then_inc(exp_ok, 1)
                        if not last:
                            take(i + 1, n)
                    if n >= 2:
                        q = n - 2
                        act.wait_ge(p_tr, i * 16 + 2 * q + 2)
                        nc.scalar.activation(probsT[:, q // 4, 4:8, (q % 4) * P:(q % 4 + 1) * P],
                                             ps[:, 5, :].rearrange("p (a c) -> p a c", a=4), ACT.Copy).then_inc(pt_act, 1)

            with act.Fori(0, MH - 1) as i:
                mla_head(i, False)
            mla_head(MH - 1, True)

            def dense_hi(n, before=0):
                act.wait_ge(d_in[n % 2], before * 16 + 32 * (n // 2) + 32)
                if not isinstance(before, int) or before + n >= 2:
                    act.wait_ge(d_used, before + n - 1)
                nc.scalar.activation(d_hi[:, n % 2, :], d_raw[:, n % 2, :], ACT.Copy).then_inc(d_hi_ok, 1)

            dense_hi(0)
            dense_hi(1)
            act.wait_ge(gate_consts, 1)
            for k in range(KD):
                nc.scalar.activation(hT_hi[:, k, :], hT[:, k, :], ACT.Copy).then_inc(hT_hi_ok, 1)

            def outputs_odd(h):
                for c in (1, 3):
                    half, j = divmod(c, 2)
                    act.wait_ge(o_tr, h * 4 + c + 1)
                    nc.scalar.activation(oaS[:, j, half * HALF:(half + 1) * HALF], ps[:, 4 + c, :], ACT.Copy,
                                         scale=onorm_c[:, j:j + 1]).then_inc(oa_act, 1)

            def gla_head(h, first=False):
                mine = h * GLA_UNITS

                def take_qk():
                    act.wait_ge(d_used, mine + 2)
                    for c in range(4):
                        j, half = divmod(c, 2)
                        nc.scalar.activation(qk_T[:, j, half * HALF:(half + 1) * HALF], ps[:, c, :], ACT.Copy,
                                             scale=DK ** -0.5 if j == 0 else 1.0).then_inc(qk_ev, 1)

                def take_vr(t):
                    if t < NT - 1:
                        act.wait_ge(vr_mm, h * (NT - 1) + t + 1)
                    else:
                        act.wait_ge(d_used, mine + GLA_UNITS)
                    nc.scalar.activation(vr[:, t, :], ps[:, t, :], ACT.Copy).then_inc(vr_ev, 1)

                for d in range(2):
                    act.wait_ge(z_dve, h * 2 + d + 1)
                    if d == 1:
                        act.wait_ge(b_ok, h * 2 + 1)
                    nc.scalar.activation(eT[:], zT[:], ACT.Abs).then_inc(z_act, 1)
                    act.wait_ge(z_act, h * 6 + 3 * d + 1)
                    nc.scalar.activation(eT[:], eT[:], ACT.Exp, scale=-1.0).then_inc(z_act, 1)
                    act.wait_ge(z_act, h * 6 + 3 * d + 2)
                    nc.scalar.activation(eT[:], eT[:], ACT.Ln, bias=1.0).then_inc(z_act, 1)
                    if d == 1:
                        dense_hi(4, mine)
                    act.wait_ge(b_ok, h * 2 + d + 1)
                    nc.scalar.activation(qt[:, d, :], bT[:], ACT.Exp, scale=1 / GATE_DIV).then_inc(e_ok, 1)
                    nc.scalar.activation(kt[:, d, :], bT[:], ACT.Exp, scale=-1 / GATE_DIV).then_inc(e_ok, 1)
                    if d == 0 and not first:
                        outputs_odd(h - 1)
                    act.wait_ge(tail_ok, h * 2 + d + 1)
                    nc.scalar.activation(kd[:, d, :], zT[:], ACT.Exp, scale=1 / GATE_DIV).then_inc(ed_ok, 1)
                    if d == 0:
                        dense_hi(2, mine)
                        dense_hi(3, mine)
                        take_qk()
                    else:
                        dense_hi(5, mine)
                        dense_hi(6, mine)
                if not first:
                    act.wait_ge(oa_out, h * 16)
                for t in range(NT):
                    take_vr(t)
                act.wait_ge(vr_ev, h * NT + NT)
                nc.scalar.activation(vr[:, :, DV:2 * DV], vr[:, :, DV:2 * DV], ACT.Silu).then_inc(silu_ok, 1)
                dense_hi(7, mine)
                act.wait_ge(att_mm, h * 4 + 4)
                for t in range(NT):
                    act.wait_ge(o_ev, h * NT + t + 1)
                    nc.scalar.activation(o_sqr[:, t, :], oR[:, t, :], ACT.Square,
                                         accum_out=stat[:, 6, t:t + 1]).then_inc(o_sq, 1)

            gla_head(0, first=True)
            with act.Fori(1, GH) as h:
                gla_head(h)
            outputs_odd(GH - 1)

            def gate(b, i, n, turns=0):
                act.wait_ge(d_used, turns * 4 + n + 1)
                if not isinstance(turns, int) or b * KD + i >= 2:
                    act.wait_ge(y_ev, turns * 2 + b * KD + i - 1 + PAIRS)
                if b and i >= 2:
                    act.wait_ge(m_ok, turns * 2 + i - 1)
                k = i % 2
                nc.scalar.activation(sg[:, k, :].rearrange("p (a c) -> p a c", a=2), ps[:, 2 * k:2 * k + 2, :],
                                     ACT.Sigmoid).then_inc(g_ev, 1)

            def merged_hi(k):
                act.wait_ge(m_ok, k + 1)
                nc.scalar.activation(mT_hi[:, k, :], mT[:, k, :], ACT.Copy).then_inc(mT_hi_ok, 1)

            for b in range(2):
                n = MERGE0 + b * JOBS
                act.wait_ge(d_used, n)
                for k in range(KD):
                    act.wait_ge(stage_in[k % 2], b * 64 + 16 * (k // 2) + 16)
                    nc.scalar.activation(oT_hi[:, k, :], stage[:, k % 2, :], ACT.Copy).then_inc(oT_hi_ok, 1)
                dense_hi(n + 2)
                gate(b, 0, n)
                dense_hi(n + 3)
                gate(b, 1, n + 1)
                with act.Fori(0, 3) as r:
                    for i in range(2):
                        dense_hi(n + 4 + 2 * i, r * 4)
                        dense_hi(n + 5 + 2 * i, r * 4)
                        gate(b, i + 2, n + 3 + 2 * i, r)
                if b:
                    act.wait_ge(d_used, OUT0 - 2)
                    for k in range(6):
                        merged_hi(k)
                for i in (6, 7):
                    dense_hi(n + 10 + i)
                    if b:
                        merged_hi(i)
            for g in range(2):
                for k in range(KD):
                    if g * KD + k + 2 < 2 * KD:
                        dense_hi(OUT0 + g * KD + k + 2)
                for j in range(4):
                    t = 4 * g + j
                    act.wait_ge(f_ev, g * 8 + 2 * j + 2)
                    nc.scalar.activation(h2[:, t, :], x1[:, t, :], ACT.Square, accum_out=stat[:, 7, t:t + 1]) \
                        .then_inc(x1_sq, 1)
            for t in range(NT):
                act.wait_ge(h2_tr, 2 * t + 2)
                if t >= 2:
                    act.wait_ge(lg_mm, t - 1)
                nc.scalar.activation(h2T[:, t % 2, 4:8, :], ps[:, 2 * (t % 2) + 1, :].rearrange("p (a c) -> p a c", a=4),
                                     ACT.Copy).then_inc(h2T_act, 1)
            act.wait_ge(soft, 2)
            nc.scalar.activation(aff[:], aff[:], ACT.Exp).then_inc(soft_exp, 1)

            def split(n, turn=0):
                act.wait_ge(raw_in[n % RING], turn * 32 + 16 * (n // RING) + 16)
                if n >= RING:
                    act.wait_ge(w_used, turn * UNITS + n - RING + 1)
                nc.scalar.activation(w_hi[:, n % RING, :], w_raw[:, n % RING, :], ACT.Copy).then_inc(hi_ok, 1)

            def rows_in(e):
                for b in range(2):
                    act.wait_ge(xe_tr, e * 2 + b + 1)
                    nc.scalar.activation(xeT_hi[:, 4 * b:4 * b + 4, :], ps[:, b, :].rearrange("p (a c) -> p a c", a=4),
                                         ACT.Copy).then_inc(xeT_hi_ok, 1)

            def silu(e, j, used):
                act.wait_ge(w_used, used)
                nc.scalar.activation(silu_g[:, j, :], ps[:, 2 * j, :], ACT.Silu).then_inc(silu_e, 1)

            def act_in(e, j):
                act.wait_ge(a_tr, e * 2 + j + 1)
                nc.scalar.activation(act_T_hi[:, 4 * j:4 * j + 4, :], ps[:, 6 + j, :].rearrange("p (a c) -> p a c", a=4),
                                     ACT.Copy).then_inc(aT_hi_ok, 1)

            def results(e, used):
                act.wait_ge(w_used, used)
                act.wait_ge(ye_free, e + CREDIT)
                act.wait_ge(val_ok, e + 1)
                nc.scalar.activation(ye[:].rearrange("p (a c) -> p a c", a=2), ps[:, 4:6, :], ACT.Copy,
                                     scale=val_s[:, 0:1]).then_inc(ye_ok, 1)

            rows_in(0)
            for n in range(FIRST):
                split(n)
                if n == 8 + LEAD - 1:
                    silu(0, 0, 8)
            with act.Fori(0, NE - 1) as e:
                for u in range(UNITS):
                    split(FIRST + u, e)
                    if u == LEAD - 1:
                        act_in(e, 0)
                        silu(e, 1, e * UNITS + FIRST)
                        rows_in(e + 1)
                    if u == 4 + LEAD - 1:
                        act_in(e, 1)
                    if u == 12 + LEAD - 1:
                        silu(e + 1, 0, e * UNITS + FIRST + 12)
                    if u == 16 + LEAD - 1:
                        results(e, e * UNITS + FIRST + 16)
            end = FIRST + (NE - 1) * UNITS
            for u in range(8):
                split(end + u)
                if u == LEAD - 1:
                    act_in(NE - 1, 0)
                    silu(NE - 1, 1, end)
                if u == 4 + LEAD - 1:
                    act_in(NE - 1, 1)
            results(NE - 1, end + 8)


_INS = ["x", "positions", "g_mix", "w_in", "gla_wa2_f", "gla_ba_f", "gla_wa2_b", "gla_ba_b", "gla_onorm", "w_gla_out",
        "mla_q_norm", "w_uq", "mla_kv_norm", "w_ukv", "q_head_norm", "k_head_norm", "w_mla_out", "w_o", "g_ffn",
        "w_router", "w_gate_e", "w_up_e", "w_down_e"]


def kernel(**inputs):
    import concourse.bacc as bacc
    from concourse.bass_utils import run_bass_kernel_spmd

    nc = bacc.Bacc("TRN2", target_bir_lowering=False, num_devices=1)
    arrays, args = {}, []
    for name in _INS:
        a = np.ascontiguousarray(inputs[name])
        arrays[f"in_{name}"] = a
        args.append(nc.dram_tensor(f"in_{name}", a.shape, mybir.dt.from_np(a.dtype), kind="ExternalInput").ap())
    args.append(nc.dram_tensor("layer_out", (1, S, D), F32, kind="ExternalOutput").ap())
    hybrid_layer(nc, *args)
    r = run_bass_kernel_spmd(nc, [arrays], core_ids=[0])
    return r.results[0]["layer_out"]
```

```python
import math
from contextlib import ExitStack

import numpy as np

import concourse.bass as bass
from concourse import mybir

P = 128
F32 = mybir.dt.float32
F32R = mybir.dt.float32r
I32 = mybir.dt.int32
U32 = mybir.dt.uint32
ALU = mybir.AluOpType
ACT = mybir.ActivationFunctionType
AX = mybir.AxisListType.X

S = 1024
D = 1024
NT = S // P
KD = D // P
HALF = 512
GH, DK, DV, RANK, CH = 4, 128, 256, 16, 64
NCH = S // CH
GATE_DIV = 16.0
MH, NOPE, ROPE, MV = 8, 128, 64, 128
HQ = NOPE + ROPE
QR, KVR = 384, 256
RH = ROPE // 2
NE, CAP, FF = 16, 128, 1024
EPS = 1e-6
BIG = 3.0e38
UNIT = 1024
UNITS = 24
RING = 12
FIRST = 16
TURN = ([("d", 0, k) for k in range(4)] + [(m, 0, k) for k in range(4) for m in "gu"]
        + [("d", 1, k) for k in range(4)] + [(m, 1, k) for k in range(4) for m in "gu"])
LEAD = 3
GLA_UNITS = 6
MERGE0 = GH * GLA_UNITS
JOBS = 2 * KD
OUT0 = MERGE0 + 2 * JOBS
CREDIT = 1
PAIRS = 2
C_Q, C_K, C_V, C_R = 0, 512, 1024, 2048
C_LAT = 3072
LAT = 2 * RANK + QR + KVR + ROPE
LA = 2 * RANK + QR
LB = KVR + ROPE
C_GA = C_LAT + LAT
C_GB = C_GA + D


SEAM_BANKS = (7, 0, 1, 2, 3, 7, 0, 1)
def project_bank(head, group):
    return 6 + (group + 1) % 2 if isinstance(head, int) else 7


O_BANKS = (6, 7, 4, 5)
AFTER_SCORES = (0, 1, 2, 4, 6, 7)
AFTER_TRANSPOSES = {2: 3, 3: 5}

class Steps:

    def __init__(self, eng, sem, base=0, turn=0, per=0):
        self.eng, self.sem, self.base, self.turn, self.per, self.n = eng, sem, base, turn, per, 0

    def mark(self, ins):
        ins.then_inc(self.sem, 1)
        self.n += 1
        return self.n

    def wait(self, n=None):
        self.eng.wait_ge(self.sem, self.turn * self.per + self.base + (self.n if n is None else n))

    def link(self, ins):
        self.mark(ins)
        self.wait()

    def end(self):
        assert self.n == self.per, (self.n, self.per)


def rope_frequencies():
    return [float(np.float32(10000.0 ** (-j / RH))) for j in range(RH)]


def hybrid_layer(nc, x, positions, g_mix, w_in, gla_wa2_f, gla_ba_f, gla_wa2_b, gla_ba_b, gla_onorm,
                 w_gla_out, mla_q_norm, w_uq, mla_kv_norm, w_ukv, q_head_norm, k_head_norm,
                 w_mla_out, w_o, g_ffn, w_router, w_gate_e, w_up_e, w_down_e, out):
    x_rows = x[0]
    out_rows = out[0]
    h2_dram = nc.dram_tensor("h2_rows", (S, D), F32, kind="Internal").ap()
    h_dram = nc.dram_tensor("rows_T", (KD, P, S), F32, kind="Internal").ap()
    oa_dram = nc.dram_tensor("gla_out_T", (KD, P, S), F32, kind="Internal").ap()
    ob_dram = nc.dram_tensor("mla_out_T", (KD, P, S), F32, kind="Internal").ap()

    def col(v, n):
        return v.rearrange("(k p) -> p k", p=P) if n > 1 else v.rearrange("(p a) -> p a", a=1)

    def spread(v, n):
        return v.rearrange("(a n) -> a n", a=1).broadcast_to((P, n))

    w_in_k = w_in.rearrange("(k p) n -> p k n", p=P)
    w_uq_k = w_uq.rearrange("(k p) n -> p k n", p=P)
    w_ukv_k = w_ukv.rearrange("(k p) n -> p k n", p=P)
    w_go_k = w_gla_out.rearrange("(k p) n -> p k n", p=P)
    w_mo_k = w_mla_out.rearrange("(k p) n -> p k n", p=P)
    w_o_k = w_o.rearrange("(k p) n -> p k n", p=P)

    with ExitStack() as ctx:
        def sb_in(stack, name, shape, dt=F32):
            return stack.enter_context(nc.sbuf_tensor(name, shape, dt))

        def sb(name, shape, dt=F32):
            return sb_in(ctx, name, shape, dt)

        def sem(name):
            return ctx.enter_context(nc.semaphore(name))

        ps = ctx.enter_context(nc.psum_tensor("ps", [P, 8, HALF], F32))

        ident = sb("ident", [P, P])
        g_mix_c = sb("g_mix_c", [P, KD])
        qn_c = sb("qn_c", [P, QR // P])
        kvn_c = sb("kvn_c", [P, KVR // P])
        onorm_c = sb("onorm_c", [P, DV // P])
        qhn_c = sb("qhn_c", [P, 1])
        khn_c = sb("khn_c", [P, 1])
        qhr_b = sb("qhr_b", [P, ROPE])
        khr_b = sb("khr_b", [P, ROPE])
        minus_half = sb("minus_half", [P, NT])
        stat = sb("stat", [P, 16, NT])
        idx_c = sb("idx_c", [P, NE], U32)
        val_c = sb("val_c", [P, NE])
        w_router_s = sb("w_router_s", [P, KD, NE])

        mix_mem = ExitStack()
        with mix_mem:
            stage = sb_in(mix_mem, "stage", [P, 2, S])
            gateT = stage[0:RANK]
            w_a2 = sb_in(mix_mem, "w_a2", [RANK, 2, DK])
            b_a2 = sb_in(mix_mem, "b_a2", [P, 2])
            d_raw = sb_in(mix_mem, "d_raw", [P, 2, UNIT])
            d_hi = sb_in(mix_mem, "d_hi", [P, 2, UNIT], F32R)
            d_lo = sb_in(mix_mem, "d_lo", [P, 2, UNIT], F32R)

            early_mem = ExitStack()
            with early_mem:
                mla_mem = ExitStack()
                with mla_mem:
                    cqT = sb_in(mla_mem, "cqT", [P, QR // P, S])
                    ckvT = sb_in(mla_mem, "ckvT", [P, KVR // P, S])
                    k_rot = sb_in(mla_mem, "k_rot", [P, NT, ROPE])
                    cos_t = sb_in(mla_mem, "cos_t", [P, NT, RH])
                    sin_t = sb_in(mla_mem, "sin_t", [P, NT, RH])
                    freq = sb_in(mla_mem, "freq", [P, RH])
                    w_uq_h = sb_in(mla_mem, "w_uq_h", [P, QR // P, HQ])
                    w_ukv_h = sb_in(mla_mem, "w_ukv_h", [P, KVR // P, NOPE + MV])
                    lat_mem = ExitStack()
                    with lat_mem:
                        hT = sb_in(lat_mem, "hT", [P, KD, S])
                        xs = sb_in(lat_mem, "xs", [P, NT, D])
                        w_lat = sb_in(lat_mem, "w_lat", [P, KD, LAT])
                        lat_r = sb_in(lat_mem, "lat_r", [P, NT, LAT])
                        sq_a = sb_in(lat_mem, "sq_a", [P, D])
                        pos_i = sb_in(lat_mem, "pos_i", [P, NT], I32)
                        pos_f = sb_in(lat_mem, "pos_f", [P, NT])
                        ang = sb_in(lat_mem, "ang", [P, NT, RH])
                        turns_f = sb_in(lat_mem, "turns_f", [P, 2, NT, RH])
                        turns_i = sb_in(lat_mem, "turns_i", [P, 2, NT, RH], I32)
                        k_tmp = sb_in(lat_mem, "k_tmp", [P, 3, NT, RH])
                    head_mem = ExitStack()
                    with head_mem:
                        qR = sb_in(head_mem, "qR", [P, NT, HQ + ROPE])
                        kvR = sb_in(head_mem, "kvR", [P, NT, NOPE + MV])
                        kRr = sb_in(head_mem, "kRr", [P, NT, 2 * ROPE])
                        sq_q = sb_in(head_mem, "sq_q", [P, NT, HQ])
                        r_tmp = sq_q[:, :, :].rearrange("p t c -> p (t c)")[:, 0:4 * NT * RH] \
                            .rearrange("p (a t r) -> p a t r", a=4, t=NT)
                        qT_hi = sb_in(head_mem, "qT_hi", [P, S], F32R)
                        qT_lo = sb_in(head_mem, "qT_lo", [P, S], F32R)
                        kT_hi = sb_in(head_mem, "kT_hi", [P, S], F32R)
                        kT_lo = sb_in(head_mem, "kT_lo", [P, S], F32R)
                        qr_T = sb_in(head_mem, "qr_T", [P, S], F32R)
                        kr_T = sb_in(head_mem, "kr_T", [P, S], F32R)
                        kr_lo = sb_in(head_mem, "kr_lo", [ROPE, S], F32R)
                        v_hi = sb_in(head_mem, "v_hi", [P, NT, MV], F32R)
                        v_lo = sb_in(head_mem, "v_lo", [P, NT, MV], F32R)
                        probs = sb_in(head_mem, "probs", [P, 3, S])
                        pT_hi = sb_in(head_mem, "pT_hi", [P, 2, NT, HALF], F32R)
                        pT_lo = sb_in(head_mem, "pT_lo", [P, 2, NT, HALF], F32R)
                        obS = sb_in(head_mem, "obS", [P, S])
                        row_max = sb_in(head_mem, "row_max", [P, NT])
                        row_sum = sb_in(head_mem, "row_sum", [P, NT])
                        row_inv = sb_in(head_mem, "row_inv", [P, NT])

            late_mem = ExitStack()
            with late_mem:
                carry = sb_in(late_mem, "carry", [P, KD * S])
                hT_hi = sb_in(late_mem, "hT_hi", [P, KD, S], F32R)
                hT_lo = sb_in(late_mem, "hT_lo", [P, KD, S], F32R)
                state = carry[:, :].rearrange("p (d n v) -> p d n v", d=2, n=NCH)
                hT_again = carry[:, :].rearrange("p (k s) -> p k s", k=KD)
                mT = carry[:, :].rearrange("p (k s) -> p k s", k=KD)
                h2 = carry[:, :].rearrange("p (t d) -> p t d", t=NT)
                mT_hi, mT_lo = hT_hi, hT_lo
                gla_tmp = ExitStack()
                with gla_tmp:
                    out_mem = ExitStack()
                    with out_mem:
                        oaS = sb_in(out_mem, "oaS", [P, 2, S])
                    vr = sb_in(gla_tmp, "vr", [P, NT, 2 * DV])
                    qk_T = sb_in(gla_tmp, "qk_T", [P, 2, S])
                    qt = sb_in(gla_tmp, "qt", [P, 2, S])
                    kt = sb_in(gla_tmp, "kt", [P, 2, S])
                    kd = sb_in(gla_tmp, "kd", [P, 2, S])
                    zT = sb_in(gla_tmp, "zT", [P, S])
                    eT = sb_in(gla_tmp, "eT", [P, S])
                    bT = sb_in(gla_tmp, "bT", [P, S])
                    decay = sb_in(gla_tmp, "decay", [P, 2, NCH])
                    keep_hi = sb_in(gla_tmp, "keep_hi", [P, 2, P])
                    keep_lo = sb_in(gla_tmp, "keep_lo", [P, 2, P])
                    scan_m = sb_in(gla_tmp, "scan_m", [P, S])
                    kdR = qk_T[:, :, :].rearrange("p d (t c) -> p d t c", t=NT)
                    oR = kd[:, :, :].rearrange("p a (t c) -> p (a t) c", c=DV)
                    o_sqr = kt[:, :, :].rearrange("p a (t c) -> p (a t) c", c=DV)
                    att = bT[:, :].rearrange("p (t c) -> p t c", t=NT)
                    att_f = zT[:, :].rearrange("p (t c) -> p t c", t=NT)
                    att_b = eT[:, :].rearrange("p (t c) -> p t c", t=NT)
                merge_mem = ExitStack()
                with merge_mem:
                    sg = sb_in(merge_mem, "sg", [P, 2, S])
                    branch_mem = ExitStack()
                    with branch_mem:
                        oT_hi = sb_in(branch_mem, "oT_hi", [P, KD, S], F32R)
                        oT_lo = sb_in(branch_mem, "oT_lo", [P, KD, S], F32R)
                    ffn_mem = ExitStack()
                    with ffn_mem:
                        x1 = sb_in(ffn_mem, "x1", [P, NT, D])
                        h2T = sb_in(ffn_mem, "h2T", [P, 2, KD, P])
                        g_ffn_b = sb_in(ffn_mem, "g_ffn_b", [P, D])
        route_mem = ExitStack()
        with route_mem:
            w_raw = sb_in(route_mem, "w_raw", [P, RING, UNIT])
            w_hi = sb_in(route_mem, "w_hi", [P, RING, UNIT], F32R)
            w_lo = sb_in(route_mem, "w_lo", [P, RING, UNIT], F32R)
            aff = sb_in(route_mem, "aff", [P, NT, NE])
            affT = sb_in(route_mem, "affT", [2 * NE, 2, S // 2])
            top_v = sb_in(route_mem, "top_v", [2 * NE, CAP])
            top_i = sb_in(route_mem, "top_i", [2 * NE, CAP], U32)
            top_f = sb_in(route_mem, "top_f", [2 * NE, CAP])
            top_rev = sb_in(route_mem, "top_rev", [2 * NE, 2, CAP])
            halves = sb_in(route_mem, "halves", [P, 8, NE])
            xe = sb_in(route_mem, "xe", [P, D])
            xeT_hi = sb_in(route_mem, "xeT_hi", [P, KD, CAP], F32R)
            xeT_lo = sb_in(route_mem, "xeT_lo", [P, KD, CAP], F32R)
            silu_g = sb_in(route_mem, "silu_g", [P, 2, HALF])
            act_r = sb_in(route_mem, "act_r", [P, 2, HALF])
            act_T_hi = sb_in(route_mem, "act_T_hi", [P, KD, CAP], F32R)
            act_T_lo = sb_in(route_mem, "act_T_lo", [P, KD, CAP], F32R)
            ye = sb_in(route_mem, "ye", [P, D])
            val_s = sb_in(route_mem, "val_s", [P, 1])

        x_in = [sem(f"x_in{t}") for t in range(NT)]
        small_in = sem("small_in")
        wlat_in = sem("wlat_in")
        g_mix_in = sem("g_mix_in")
        consts = sem("consts")
        pool_step = sem("pool_step")
        gate_consts = sem("gate_consts")
        dve_a = sem("dve_a")
        act_a = sem("act_a")
        ssq_x = sem("ssq_x")
        ms_x = sem("ms_x")
        rstd_x = sem("rstd_x")
        xn = sem("xn")
        hT_tr = sem("hT_tr")
        hT_dve = sem("hT_dve")
        hT_act = sem("hT_act")
        lat_mm = sem("lat_mm")
        lat_ev = sem("lat_ev")
        lat_sq = sem("lat_sq")
        lat_ms = sem("lat_ms")
        lat_rs = sem("lat_rs")
        lat_n = sem("lat_n")
        lat_tr = sem("lat_tr")
        latT_dve = sem("latT_dve")
        latT_act = sem("latT_act")
        trig_arg = sem("trig_arg")
        trig = sem("trig")
        k_rot_ok = sem("k_rot_ok")

        wu_in = sem("wu_in")
        prj_mm = sem("prj_mm")
        prj_ev = sem("prj_ev")
        head_sq = sem("head_sq")
        head_ms = sem("head_ms")
        head_rs = sem("head_rs")
        head_n = sem("head_n")
        head_step = sem("head_step")
        seam_tr = sem("seam_tr")
        seam_hi = sem("seam_hi")
        seam_lo = sem("seam_lo")
        v_hi_ok = sem("v_hi_ok")
        v_ok = sem("v_ok")
        h_out = sem("h_out")
        hT_in = sem("hT_in")
        s_mm = sem("s_mm")
        max_ok = sem("max_ok")
        exp_ok = sem("exp_ok")
        inv_ok = sem("inv_ok")
        p_ok = sem("p_ok")
        p_tr = sem("p_tr")
        pt_hi = sem("pt_hi")
        pt_lo = sem("pt_lo")
        pv_mm = sem("pv_mm")
        ob_ev = sem("ob_ev")
        ob_out = sem("ob_out")

        d_in = [sem(f"d_in{j}") for j in range(2)]
        d_hi_ok = sem("d_hi_ok")
        d_lo_ok = sem("d_lo_ok")
        d_used = sem("d_used")
        hT_hi_ok = sem("hT_hi_ok")
        hT_lo_ok = sem("hT_lo_ok")
        wa_in = sem("wa_in")
        qk_ev = sem("qk_ev")
        z_mm = sem("z_mm")
        z_dve = sem("z_dve")
        z_act = sem("z_act")
        gla_step = sem("gla_step")
        ls_ok = sem("ls_ok")
        b_ok = sem("b_ok")
        e_ok = sem("e_ok")
        tail_ok = sem("tail_ok")
        ed_ok = sem("ed_ok")
        mats_ok = sem("mats_ok")
        vr_mm = sem("vr_mm")
        vr_ev = sem("vr_ev")
        silu_ok = sem("silu_ok")
        att_mm = sem("att_mm")
        att_ok = sem("att_ok")
        kd_tr = sem("kd_tr")
        kd_ev = sem("kd_ev")
        ds_mm = sem("ds_mm")
        st_ok = sem("st_ok")
        o_mm = sem("o_mm")
        o_ev = sem("o_ev")
        o_sq = sem("o_sq")
        o_ms = sem("o_ms")
        o_rs = sem("o_rs")
        o_n = sem("o_n")
        o_tr = sem("o_tr")
        oa_dve = sem("oa_dve")
        oa_act = sem("oa_act")
        oa_out = sem("oa_out")

        oa_back = sem("oa_back")
        stage_in = [sem(f"stage_in{j}") for j in range(2)]
        oT_hi_ok = sem("oT_hi_ok")
        oT_lo_ok = sem("oT_lo_ok")
        g_ev = sem("g_ev")
        y_ev = sem("y_ev")
        m_ok = sem("m_ok")
        mT_hi_ok = sem("mT_hi_ok")
        mT_lo_ok = sem("mT_lo_ok")
        x1_in = sem("x1_in")
        gf_in = sem("gf_in")
        f_mm = sem("f_mm")
        f_ev = sem("f_ev")
        x1_sq = sem("x1_sq")
        x1_ms = sem("x1_ms")
        x1_rs = sem("x1_rs")
        h2_ok = sem("h2_ok")
        rows_out = sem("rows_out")
        h2_tr = sem("h2_tr")
        h2T_dve = sem("h2T_dve")
        h2T_act = sem("h2T_act")
        lg_mm = sem("lg_mm")
        soft = sem("soft")
        soft_exp = sem("soft_exp")
        aff_tr = sem("aff_tr")
        affT_ok = sem("affT_ok")
        top_ok = sem("top_ok")
        top_tr = sem("top_tr")
        idx_ok = sem("idx_ok")

        raw_in = [sem(f"raw_in{j}") for j in range(RING)]
        hi_ok = sem("hi_ok")
        lo_ok = sem("lo_ok")
        w_used = sem("w_used")
        xe_in = sem("xe_in")
        xe_tr = sem("xe_tr")
        xeT_hi_ok = sem("xeT_hi_ok")
        xeT_lo_ok = sem("xeT_lo_ok")
        silu_e = sem("silu_e")
        act_ok = sem("act_ok")
        a_tr = sem("a_tr")
        aT_hi_ok = sem("aT_hi_ok")
        aT_lo_ok = sem("aT_lo_ok")
        val_ok = sem("val_ok")
        ye_ok = sem("ye_ok")
        ye_out = sem("ye_out")
        ye_free = sem("ye_free")

        block = ctx.enter_context(nc.Block())
        small_loads = 9

        @block.sync
        def _(sp):
            for t in range(NT):
                sp.dma_start(xs[:, t, :], x_rows[t * P:(t + 1) * P, :]).then_inc(x_in[t], 16)
                if t == 3:
                    sp.dma_start(g_mix_c[:], col(g_mix, KD), allow_slow_non_contiguous=True).then_inc(g_mix_in, 16)
            for j in range(2):
                k0, k1 = j * KD // 2, (j + 1) * KD // 2
                sp.dma_start(w_lat[:, k0:k1, :], w_in_k[:, k0:k1, C_LAT:C_LAT + LAT]).then_inc(wlat_in, 16)
            loads = [(qn_c[:], col(mla_q_norm, QR // P)),
                     (kvn_c[:], col(mla_kv_norm, KVR // P)), (onorm_c[:], col(gla_onorm, DV // P)),
                     (qhn_c[:], col(q_head_norm[0:NOPE], 1)), (khn_c[:], col(k_head_norm[0:NOPE], 1)),
                     (qhr_b[:], spread(q_head_norm[NOPE:HQ], ROPE)), (khr_b[:], spread(k_head_norm[NOPE:HQ], ROPE)),
                     (pos_i[:], positions.rearrange("b (t p) -> p (b t)", p=P)),
                     (w_router_s[:], w_router.rearrange("(k p) e -> p k e", p=P))]
            for dst, src in loads:
                sp.dma_start(dst, src, allow_slow_non_contiguous=True).then_inc(small_in, 16)
            assert len(loads) == small_loads

            def load_up(h):
                sp.dma_start(w_uq_h[:], w_uq_k[:, :, bass.ds(h * HQ, HQ)]).then_inc(wu_in, 16)
                sp.dma_start(w_ukv_h[:], w_ukv_k[:, :, bass.ds(h * (NOPE + MV), NOPE + MV)]).then_inc(wu_in, 16)

            def load_dense(pieces, k, before=0):
                if not isinstance(before, int) or before + k >= 2:
                    sp.wait_ge(d_lo_ok, before + k - 1)
                for dst, src in pieces:
                    sp.dma_start(dst, src).then_inc(d_in[k % 2], 16)

            def load_gla(h, u, before=0):
                slot = d_raw[:, u % 2, :]
                if u < 2:
                    slot = slot.rearrange("p (a c) -> p a c", a=4)
                    load_dense([(slot[:, :, j * DK:(j + 1) * DK], w_in_k[:, 4 * u:4 * u + 4, bass.ds(c + h * DK, DK)])
                                for j, c in enumerate((C_Q, C_K))], u, before)
                else:
                    slot, k = slot.rearrange("p (a c) -> p a c", a=2), 2 * (u - 2)
                    load_dense([(slot[:, :, j * DV:(j + 1) * DV], w_in_k[:, k:k + 2, bass.ds(c + h * DV, DV)])
                                for j, c in enumerate((C_V, C_R))], u, before)

            def load_job(b, kind, cb, k, before=0):
                w = ((w_in_k[:, :, C_GA:C_GB], w_go_k), (w_in_k[:, :, C_GB:C_GB + D], w_mo_k))[b][kind]
                slot = d_raw[:, k % 2, :].rearrange("p (a c) -> p a c", a=KD)
                load_dense([(slot[:, i:i + 4, :], w[:, i:i + 4, bass.ds(cb * P, P)]) for i in (0, 4)], k, before)

            def load_out(u):
                n, cols = OUT0 + u, (slice(0, HALF), slice(HALF, D))
                load_dense([(d_raw[:, n % 2, c], w_o_k[:, u % KD, c]) for c in cols], n)

            def load_a2(h):
                sp.dma_start(w_a2[:, 0, :], gla_wa2_f[:, bass.ds(h * DK, DK)]).then_inc(wa_in, 16)
                sp.dma_start(w_a2[:, 1, :], gla_wa2_b[:, bass.ds(h * DK, DK)]).then_inc(wa_in, 16)
                for d, b in enumerate((gla_ba_f, gla_ba_b)):
                    sp.dma_start(b_a2[:, d:d + 1], b[bass.ds(h * DK, DK)].rearrange("(p a) -> p a", a=1),
                                 allow_slow_non_contiguous=True).then_inc(wa_in, 16)

            load_up(0)
            sp.wait_ge(hT_dve, KD)
            sp.wait_ge(hT_act, KD)
            sp.dma_start(h_dram.rearrange("k p s -> p k s"), hT[:]).then_inc(h_out, 16)
            load_gla(0, 0)
            load_gla(0, 1)
            load_a2(0)
            sp.wait_ge(prj_mm, 8)
            load_up(1)

            def store_ob(h, j):
                cols = slice(j * HALF, (j + 1) * HALF)
                sp.wait_ge(ob_ev, h * 2 + j + 1 + CREDIT)
                sp.dma_start(ob_dram[bass.ds(h, 1), :, cols].rearrange("a p s -> p (a s)"),
                             obS[:, cols]).then_inc(ob_out, 16)

            with sp.Fori(0, MH - 2) as h:
                store_ob(h, 0)
                sp.wait_ge(prj_mm, h * 8 + 16)
                load_up(h + 2)
                store_ob(h, 1)
            store_ob(MH - 2, 0)
            store_ob(MH - 2, 1)
            sp.wait_ge(h_out, 16)
            sp.wait_ge(seam_tr, MH * 8)
            sp.dma_start(hT_again, h_dram.rearrange("k p s -> p k s")).then_inc(hT_in, 16)
            store_ob(MH - 1, 0)
            store_ob(MH - 1, 1)

            def store_oa(h):
                sp.wait_ge(oa_dve, h * 2 + 2)
                sp.wait_ge(oa_act, h * 2 + 2)
                sp.dma_start(oa_dram[bass.ds(h * 2, 2)].rearrange("a p s -> p a s"), oaS[:]).then_inc(oa_out, 16)

            def gla_turn(h, first=False, last=False):
                load_gla(h, 2, h * GLA_UNITS)
                load_gla(h, 3, h * GLA_UNITS)
                if not first:
                    store_oa(h - 1)
                load_gla(h, 4, h * GLA_UNITS)
                load_gla(h, 5, h * GLA_UNITS)
                if not last:
                    sp.wait_ge(z_dve, h * 2 + 2)
                    load_a2(h + 1)
                    load_gla(h + 1, 0, (h + 1) * GLA_UNITS)
                    load_gla(h + 1, 1, (h + 1) * GLA_UNITS)

            gla_turn(0, first=True)
            with sp.Fori(1, GH - 1) as h:
                gla_turn(h)
            gla_turn(GH - 1, last=True)

            def load_branch(b):
                src = (oa_dram, ob_dram)[b]
                if b == 0:
                    sp.wait_ge(oa_out, 16 * (GH - 1))
                    sp.wait_ge(o_ev, GH * NT)
                    sp.dma_start(mT[:, 0:6, :], src[0:6].rearrange("k p s -> p k s")).then_inc(oa_back, 16)
                    store_oa(GH - 1)
                    sp.wait_ge(oa_out, 16 * GH)
                    sp.dma_start(mT[:, 6:8, :], src[6:8].rearrange("k p s -> p k s")).then_inc(oa_back, 16)
                    return
                for k in range(KD):
                    if k >= 2:
                        sp.wait_ge(oT_lo_ok, KD + k - 1)
                    sp.dma_start(stage[:, k % 2, :], src[k]).then_inc(stage_in[k % 2], 16)

            def load_turn(b, r):
                before = MERGE0 + b * JOBS + r * 4
                for i in range(2):
                    load_job(b, 1, r * 2 + i, 2 + 2 * i, before)
                    load_job(b, 0, r * 2 + i + 2, 3 + 2 * i, before)

            for b in range(2):
                n = MERGE0 + b * JOBS
                load_job(b, 0, 0, n)
                load_job(b, 0, 1, n + 1)
                if b:
                    sp.wait_ge(ob_out, 32 * MH + CREDIT)
                load_branch(b)
                with sp.Fori(0, 3) as r:
                    load_turn(b, r)
                load_job(b, 1, 6, n + 14)
                load_job(b, 1, 7, n + 15)
            load_out(0)
            load_out(1)
            sp.wait_ge(d_used, OUT0)
            sp.dma_start(g_ffn_b[:], spread(g_ffn, D)).then_inc(gf_in, 16)
            for u in range(2, 2 * KD):
                load_out(u)
                if u < 2 + NT:
                    sp.dma_start(x1[:, u - 2, :], x_rows[(u - 2) * P:(u - 1) * P, :]).then_inc(x1_in, 16)
            for t in range(NT):
                sp.wait_ge(h2_ok, t + 1)
                sp.dma_start(h2_dram[t * P:(t + 1) * P, :], h2[:, t, :]).then_inc(rows_out, 16)
                sp.dma_start(out_rows[t * P:(t + 1) * P, :], x1[:, t, :]).then_inc(rows_out, 16)
            sp.wait_ge(rows_out, 32 * NT)

            def load_unit(e, unit, n, turn=0):
                m, j, k = unit
                if n >= RING:
                    sp.wait_ge(lo_ok, turn * UNITS + n - RING + 1)
                w = {"g": w_gate_e, "u": w_up_e, "d": w_down_e}[m]
                src = w[bass.ds(e, 1)].rearrange("a (k p) f -> p (a k) f", p=P)
                if m == "d":
                    src = src[:, 4 * j + k, :]
                    dst = w_raw[:, n % RING, :]
                else:
                    src = src[:, 2 * k:2 * k + 2, j * HALF:(j + 1) * HALF]
                    dst = w_raw[:, n % RING, :].rearrange("p (a c) -> p a c", a=2)
                sp.dma_start(dst, src).then_inc(raw_in[n % RING], 16)

            sp.wait_ge(lg_mm, NT)
            first = TURN[4:12] + TURN[16:24]
            for n in range(FIRST):
                load_unit(0, first[n], n)
            with sp.Fori(0, NE - 1) as e:
                for u, unit in enumerate(TURN):
                    load_unit(e if unit[0] == "d" else e + 1, unit, FIRST + u, e)
            for u, unit in enumerate(TURN[0:4] + TURN[12:16]):
                load_unit(NE - 1, unit, FIRST + (NE - 1) * UNITS + u)

        @block.gpsimd
        def _(pool):
            for s in (ob_ev, ye_ok, ob_out, ye_free, pv_mm):
                pool.sem_inc(s, CREDIT)
            pool.sem_inc(y_ev, PAIRS)
            st = Steps(pool, pool_step)
            pool.memset(minus_half[:], -0.5).then_inc(consts, 1)
            st.link(pool.memset(ident[:], 0.0))
            pool.affine_select(out=ident[:], in_=ident[:], compare_op=ALU.not_equal, fill=1.0, base=0,
                               pattern=[[-1, P]], channel_multiplier=1).then_inc(consts, 1)
            for j, f in enumerate(rope_frequencies()):
                ins = pool.memset(freq[:, j:j + 1], f)
            ins.then_inc(consts, 1)

            def rsqrt(dst, ready, count, done):
                pool.wait_ge(ready, count)
                pool.tensor_tensor(dst, dst, minus_half[:, 0:dst.shape[1]], ALU.pow).then_inc(done, 1)

            pool.wait_ge(consts, 3)
            for t in range(NT):
                rsqrt(stat[:, 0, t:t + 1], ms_x, t + 1, rstd_x)
            for t in range(NT):
                rsqrt(stat[:, 1:3, t], lat_ms, t + 1, lat_rs)
            for h in range(MH):
                rsqrt(stat[:, 4, :], head_ms, 2 * h + 1, head_rs)
                rsqrt(stat[:, 5, :], head_ms, 2 * h + 2, head_rs)
            pool.wait_ge(pv_mm, 2 * MH + CREDIT)
            pool.wait_ge(ob_out, 32 * MH + CREDIT)
            st.mark(pool.memset(keep_hi[:], BIG))
            st.link(pool.memset(scan_m[:], 1.0))
            st.mark(pool.memset(scan_m[:, 0:S:CH], 0.0))
            st.mark(pool.affine_select(out=keep_hi[:, 0, :], in_=keep_hi[:, 0, :], compare_op=ALU.is_ge, fill=0.0,
                                       base=0, pattern=[[1, P]], channel_multiplier=-1))
            st.link(pool.affine_select(out=keep_hi[:, 1, :], in_=keep_hi[:, 1, :], compare_op=ALU.is_gt, fill=0.0,
                                       base=0, pattern=[[-1, P]], channel_multiplier=1))
            st.mark(pool.memset(keep_hi[0:CH, 0, CH:P], 0.0))
            st.link(pool.memset(keep_hi[CH:P, 1, 0:CH], 0.0))
            pool.tensor_scalar(keep_lo[:], keep_hi[:], -1.0, 0.0, ALU.mult, ALU.add).then_inc(gate_consts, 1)
            for h in range(GH):
                for j in range(2):
                    rsqrt(stat[:, 6, 4 * j:4 * j + 4], o_ms, 2 * h + j + 1, o_rs)
            for t in range(NT):
                rsqrt(stat[:, 7, t:t + 1], x1_ms, t + 1, x1_rs)

            pool.wait_ge(idx_ok, 2)
            pool.wait_ge(rows_out, 32 * NT)

            def gather(e):
                if e:
                    pool.wait_ge(xe_tr, 2 * e)
                pool.indirect_dma_start(xe[:], None, h2_dram,
                                        bass.IndirectOffsetOnAxis(ap=idx_c[:, e:e + 1], axis=0)).then_inc(xe_in, 16)

            gather(0)
            for e in range(NE):
                if e + 1 < NE:
                    gather(e + 1)
                if e:
                    pool.wait_ge(ye_out, 16 * e)
                    pool.sem_inc(ye_free, 1)
                pool.wait_ge(ye_ok, e + 1 + CREDIT)
                pool.indirect_dma_start(out_rows, bass.IndirectOffsetOnAxis(ap=idx_c[:, e:e + 1], axis=0),
                                        ye[:], None, compute_op=ALU.add).then_inc(ye_out, 16)
            pool.wait_ge(ye_out, 16 * NE)

        @block.tensor
        def _(pe):
            def transpose4(bank, rows, srcs):
                for j, src in enumerate(srcs):
                    ins = pe.transpose(ps[0:rows, bank, j * P:(j + 1) * P], src, ident[:])
                return ins

            pe.wait_ge(consts, 3)
            for c in range(2 * KD):
                half, k = divmod(c, KD)
                pe.wait_ge(xn, 4 * half + 4)
                if c >= 4:
                    pe.wait_ge(hT_dve if c % 2 == 0 else hT_act, (c - 4) // 2 + 1)
                transpose4(c % 4, P, [xs[:, 4 * half + j, k * P:(k + 1) * P] for j in range(4)]).then_inc(hT_tr, 1)

            for t in range(NT):
                pe.wait_ge(hT_dve, 4 * (t // 4) + 4)
                pe.wait_ge(hT_act, 4 * (t // 4) + 4)
                if t >= 2:
                    pe.wait_ge(lat_ev, t - 1)
                a, b = 4 + 2 * (t % 2), 5 + 2 * (t % 2)
                for k in range(KD):
                    if t == 0 and k == 0:
                        pe.wait_ge(wlat_in, 32)
                    lhs = hT[:, k, t * P:(t + 1) * P]
                    pe.matmul(ps[:, a, 0:LA], lhs, w_lat[:, k, 0:LA], start=k == 0, stop=k == KD - 1)
                    mm = pe.matmul(ps[:, b, 0:LB], lhs, w_lat[:, k, LA:LAT], start=k == 0, stop=k == KD - 1)
                mm.then_inc(lat_mm, 1)
            for c in range(14):
                half, j = divmod(c, 7)
                pe.wait_ge(lat_n, 4 * half + 4)
                if c >= 4:
                    pe.wait_ge(latT_dve if c % 2 == 0 else latT_act, (c - 4) // 2 + 1)
                lo = (0, RANK)[j] if j < 2 else 2 * RANK + (j - 2) * P
                w = RANK if j < 2 else P
                transpose4(c % 4, w, [lat_r[:, 4 * half + t, lo:lo + w] for t in range(4)]).then_inc(lat_tr, 1)

            def three(out_ap, a_hi, a_lo, b_hi, b_lo, start, stop):
                pe.matmul(out_ap, a_hi, b_hi, start=start, stop=False)
                pe.matmul(out_ap, a_hi, b_lo, start=False, stop=False)
                return pe.matmul(out_ap, a_lo, b_hi, start=False, stop=stop)

            pe.wait_ge(latT_dve, 7)
            pe.wait_ge(latT_act, 7)
            pe.wait_ge(lat_ev, NT)

            def project(n, g):
                bank = project_bank(n, g)
                if g == 0:
                    pe.wait_ge(wu_in, n * 32 + 32)
                if bank == project_bank(n, g - 1) and g:
                    pe.wait_ge(prj_ev, n * 8 + g)
                elif g >= 2:
                    pe.wait_ge(prj_ev, n * 8 + g - 1)
                width = HQ if g < 4 else NOPE + MV
                src, w, kc = (cqT, w_uq_h, QR // P) if g < 4 else (ckvT, w_ukv_h, KVR // P)
                for j in range(2):
                    t = 2 * (g % 4) + j
                    for k in range(kc):
                        mm = pe.matmul(ps[:, bank, j * width:(j + 1) * width], src[:, k, t * P:(t + 1) * P], w[:, k, :],
                                       start=k == 0, stop=k == kc - 1)
                mm.then_inc(prj_mm, 1)

            for g in range(8):
                project(0, g)

            def seam(h, c, first=False):
                what, half = divmod(c, 2)
                if c == 0:
                    pe.wait_ge(prj_ev, h * 8 + 8)
                if c in (0, 4):
                    pe.wait_ge(head_n, h * 2 + c // 4 + 1)
                if c in (1, 3) and not first:
                    pe.wait_ge(exp_ok, (h - 1) * 8 + 7 + c // 2)
                if c >= 5:
                    pe.wait_ge(seam_lo, h * 8 + c - 4)
                srcs = []
                for j in range(4):
                    t = 4 * half + j
                    srcs.append((qR[:, t, 0:NOPE], qR[:, t, NOPE:NOPE + 2 * ROPE], kvR[:, t, 0:NOPE],
                                 kRr[:, t, :])[what])
                transpose4(SEAM_BANKS[c], P, srcs).then_inc(seam_tr, 1)

            for c in range(8):
                seam(0, c, first=True)

            def mla_head(i, last):
                pe.wait_ge(seam_lo, i * 8 + 8)
                for n in range(10):
                    if n < 8:
                        if n >= 2:
                            pe.wait_ge(exp_ok, i * 8 + n - 1)
                        for j in range(2):
                            cols = slice(j * HALF, (j + 1) * HALF)
                            bank = ps[:, 2 * (n % 2) + j, :]
                            q = slice(n * P, (n + 1) * P)
                            three(bank, qT_hi[:, q], qT_lo[:, q], kT_hi[:, cols], kT_lo[:, cols], True, False)
                            pe.matmul(bank, qr_T[:, q], kr_T[:, cols], start=False, stop=False)
                            mm = pe.matmul(bank, qr_T[0:ROPE, q], kr_lo[:, cols], start=False, stop=True)
                        mm.then_inc(s_mm, 1)
                        if not last and n < 6:
                            project(i + 1, AFTER_SCORES[n])
                    if n == 8 and not last:
                        seam(i + 1, 0)
                    if n == 9 and not last:
                        seam(i + 1, 1)
                        seam(i + 1, 2)
                    if n >= 2:
                        q = n - 2
                        pe.wait_ge(p_ok, i * 8 + q + 1)
                        for b in range(2):
                            if q:
                                pe.wait_ge(pt_lo, i * 16 + 2 * q + b - 1)
                            transpose4(4 + b, P, [probs[:, q % 3, (4 * b + j) * P:(4 * b + j + 1) * P]
                                                  for j in range(4)]).then_inc(p_tr, 1)
                        if not last and n in AFTER_TRANSPOSES:
                            project(i + 1, AFTER_TRANSPOSES[n])
                    if n == 9 and not last:
                        for c in range(3, 8):
                            seam(i + 1, c)
                    if n in (6, 7, 9):
                        j = n // 9
                        if n == 6:
                            pe.wait_ge(pt_lo, i * 16 + 8)
                            pe.wait_ge(v_ok, i + 1)
                        if n == 9:
                            pe.wait_ge(pt_lo, i * 16 + 16)
                            pe.wait_ge(ob_ev, i * 2 + 1 + CREDIT)
                        for k in {6: range(4), 7: range(4, NT), 9: range(NT)}[n]:
                            mm = three(ps[:, 6, :], v_hi[:, k, :], v_lo[:, k, :], pT_hi[:, j, k, :], pT_lo[:, j, k, :],
                                       k == 0, k == NT - 1)
                        if n > 6:
                            mm.then_inc(pv_mm, 1)

            with pe.Fori(0, MH - 1) as i:
                mla_head(i, False)
            mla_head(MH - 1, True)

            pe.wait_ge(ob_ev, 2 * MH + CREDIT)

            def gate_logits(h, d):
                for half in range(2):
                    mm = pe.matmul(ps[:, 6 - 2 * d + half, :], w_a2[:, d, :],
                                   gateT[:, d, half * HALF:(half + 1) * HALF], start=True, stop=True)
                mm.then_inc(z_mm, 1)

            def project_qk(h, u, first=False):
                pe.wait_ge(d_lo_ok, h * GLA_UNITS + u + 1)
                for i in range(4):
                    k = 4 * u + i
                    if first:
                        pe.wait_ge(hT_lo_ok, k + 1)
                    for j in range(2):
                        cols = slice((2 * i + j) * P, (2 * i + j + 1) * P)
                        for half in range(2):
                            toks = slice(half * HALF, (half + 1) * HALF)
                            mm = three(ps[:, 2 * j + half, :], d_hi[:, u, cols], d_lo[:, u, cols],
                                       hT_hi[:, k, toks], hT_lo[:, k, toks], k == 0, k == KD - 1)
                mm.then_inc(d_used, 1)

            def project_vr(h, u):
                pe.wait_ge(d_lo_ok, h * GLA_UNITS + u + 1)
                for i in range(2):
                    k = 2 * (u - 2) + i
                    cols = slice(i * HALF, (i + 1) * HALF)
                    for t in (6, 7, 0, 1, 2, 3, 4, 5) if k == 0 else range(NT):
                        if k == 0 and t < 4:
                            pe.wait_ge(qk_ev, h * 4 + t + 1)
                        if k == 0 and t == 4:
                            pe.wait_ge(z_dve, h * 2 + 2)
                        toks = slice(t * P, (t + 1) * P)
                        mm = three(ps[:, t, :], hT_hi[:, k, toks], hT_lo[:, k, toks],
                                   d_hi[:, u % 2, cols], d_lo[:, u % 2, cols], k == 0, k == KD - 1)
                        if k == KD - 1 and t < NT - 1:
                            mm.then_inc(vr_mm, 1)
                mm.then_inc(d_used, 1)

            def outputs_T(h):
                for c in range(4):
                    half, j = divmod(c, 2)
                    pe.wait_ge(o_n, h * 2 + half + 1)
                    transpose4(4 + c, P, [oR[:, 4 * half + t, j * P:(j + 1) * P] for t in range(4)]).then_inc(o_tr, 1)

            def gla_head(h, first=False, last=False):
                pe.wait_ge(wa_in, h * 64 + 64)
                if not first:
                    pe.wait_ge(o_ev, h * NT - 2)
                gate_logits(h, 0)
                project_qk(h, 1, first)
                pe.wait_ge(z_dve, h * 2 + 1)
                if not first:
                    pe.wait_ge(o_ev, h * NT)
                    outputs_T(h - 1)
                    pe.wait_ge(oa_dve, h * 2)
                    pe.wait_ge(oa_act, h * 2)
                gate_logits(h, 1)
                for u in range(2, GLA_UNITS):
                    project_vr(h, u)
                for d in range(2):
                    pe.wait_ge(mats_ok, h * 6 + 3 * d + 3)
                    for half in range(2):
                        c = 2 * d + half
                        pe.wait_ge(vr_ev, h * NT + c + 1)
                        transpose4(c, P, [kd[:, d, (4 * half + j) * P:(4 * half + j + 1) * P]
                                          for j in range(4)]).then_inc(kd_tr, 1)
                for half in range(2):
                    for d in range(2):
                        pe.wait_ge(vr_ev, h * NT + 2 * half + d + 5)
                        for j in range(4):
                            cols = slice((4 * half + j) * P, (4 * half + j + 1) * P)
                            mm = pe.matmul(ps[:, 4 + 2 * half + d, j * P:(j + 1) * P], kt[:, d, cols], qt[:, d, cols],
                                           start=True, stop=True)
                        mm.then_inc(att_mm, 1)
                pe.wait_ge(kd_ev, h * 4 + 4)
                if not last:
                    project_qk(h + 1, 0)
                pe.wait_ge(att_ok, h * 10 + 10)
                for n in range(30):
                    d, c = (1, NCH - 1 - n) if n < 15 else (0, n - 15)
                    if n >= 4:
                        pe.wait_ge(st_ok, h * 32 + n - 1)
                    r0 = CH * (c % 2)
                    mm = pe.matmul(ps[:, 4 + n % 4, 0:DV],
                                   kdR[r0:r0 + CH, d, c // 2, :], vr[r0:r0 + CH, c // 2, 0:DV], start=True, stop=True)
                    mm.then_inc(ds_mm, 1)
                for t in range(NT):
                    bank = O_BANKS[t % 4]
                    if t < 4:
                        pe.wait_ge(st_ok, h * 32 + 29 + t)
                    else:
                        pe.wait_ge(o_ev, h * NT + t - 3)
                    pe.matmul(ps[:, bank, 0:DV], att[:, t, :], vr[:, t, 0:DV], start=True, stop=False,
                              skip_group_check=True)
                    for c in (2 * t, 2 * t + 1):
                        r0 = CH * (c % 2)
                        for d in range(2):
                            mm = pe.matmul(ps[r0:r0 + CH, bank, 0:DV], qt[:, d, c * CH:(c + 1) * CH],
                                           state[:, d, c, :], start=False, stop=True, skip_group_check=True)
                    mm.then_inc(o_mm, 1)

            project_qk(0, 0, first=True)
            gla_head(0, first=True)
            with pe.Fori(1, GH - 1) as h:
                gla_head(h)
            gla_head(GH - 1, last=True)
            pe.wait_ge(o_ev, GH * NT)
            outputs_T(GH - 1)

            def job(b, kind, i, n, turns=0):
                k = n % 2
                pe.wait_ge(d_lo_ok, turns * 4 + n + 1)
                before = b * KD + i - 1
                if kind:
                    pe.wait_ge(y_ev, turns * 2 + before + PAIRS)
                elif before >= 1:
                    pe.wait_ge(g_ev, turns * 2 + before)
                bank = 4 * kind + 2 * (i % 2)
                rhs_hi, rhs_lo = ((hT_hi, hT_lo), (oT_hi, oT_lo))[kind]
                for half in range(2):
                    toks = slice(half * HALF, (half + 1) * HALF)
                    for c in range(KD):
                        cols = slice(c * P, (c + 1) * P)
                        mm = three(ps[:, bank + half, :], d_hi[:, k, cols], d_lo[:, k, cols],
                                   rhs_hi[:, c, toks], rhs_lo[:, c, toks], c == 0, c == KD - 1)
                mm.then_inc(d_used, 1)

            for b in range(2):
                n = MERGE0 + b * JOBS
                job(b, 0, 0, n)
                job(b, 0, 1, n + 1)
                if b == 0:
                    pe.wait_ge(oa_dve, 2 * GH)
                    pe.wait_ge(oa_act, 2 * GH)
                pe.wait_ge(oT_lo_ok, KD * b + KD)
                with pe.Fori(0, 3) as r:
                    for i in range(2):
                        job(b, 1, i, n + 2 + 2 * i, r)
                        job(b, 0, i + 2, n + 3 + 2 * i, r)
                job(b, 1, 6, n + 14)
                job(b, 1, 7, n + 15)

            pe.wait_ge(g_ev, 2 * KD)
            halves_first = [(half, j) for half in range(2) for j in range(4)]
            tiles_first = [(half, j) for j in range(4) for half in range(2)]
            for g in range(2):
                for k in range(KD):
                    n = OUT0 + g * KD + k
                    pe.wait_ge(d_lo_ok, n + 1)
                    if g == 0:
                        pe.wait_ge(mT_lo_ok, k + 1)
                    for half, j in halves_first if g == k == 0 else tiles_first:
                        if k == 0 and g == 0 and half:
                            pe.wait_ge(y_ev, 2 * KD - (j < 2) + PAIRS)
                        if k == 0 and g:
                            pe.wait_ge(f_ev, 2 * j + half + 1)
                        toks = slice((4 * g + j) * P, (4 * g + j + 1) * P)
                        cols = slice(half * HALF, (half + 1) * HALF)
                        mm = three(ps[:, 4 * half + j, :], mT_hi[:, k, toks], mT_lo[:, k, toks],
                                   d_hi[:, n % 2, cols], d_lo[:, n % 2, cols], k == 0, k == KD - 1)
                        if k == KD - 1 and 2 * j + half < 7:
                            mm.then_inc(f_mm, 1)
                    mm.then_inc(d_used, 1)

            pe.wait_ge(f_ev, 16)

            def rows_T(t):
                pe.wait_ge(h2_ok, t + 1)
                if t >= 2:
                    pe.wait_ge(h2T_dve, t - 1)
                    pe.wait_ge(h2T_act, t - 1)
                for b in range(2):
                    transpose4(2 * (t % 2) + b, P, [h2[:, t, (4 * b + j) * P:(4 * b + j + 1) * P]
                                                    for j in range(4)]).then_inc(h2_tr, 1)

            def logits(t):
                pe.wait_ge(h2T_dve, t + 1)
                pe.wait_ge(h2T_act, t + 1)
                for k in range(KD):
                    at = (2 * (t % 4) + t // 4) * NE
                    mm = pe.matmul(ps[:, 7, at:at + NE], h2T[:, t % 2, k, :], w_router_s[:, k, :],
                                   start=k == 0, stop=k == KD - 1)
                mm.then_inc(lg_mm, 1)

            for t in range(NT + 1):
                if t < NT:
                    rows_T(t)
                if t:
                    logits(t - 1)
            pe.wait_ge(soft, 5)
            for j in range(4):
                mm = pe.transpose(ps[0:2 * NE, 0, j * P:(j + 1) * P],
                                  aff[:, 2 * j:2 * j + 2, :].rearrange("p a e -> p (a e)"), ident[:])
            mm.then_inc(aff_tr, 1)
            pe.wait_ge(top_ok, 3)
            for j, src in enumerate((top_v[:], top_f[:], top_rev[:, 0, :], top_rev[:, 1, :])):
                mm = pe.transpose(ps[:, 2, 2 * NE * j:2 * NE * (j + 1)], src, ident[0:2 * NE, 0:2 * NE])
            mm.then_inc(top_tr, 1)

            def expert_rows_T(e):
                pe.wait_ge(xe_in, e * 16 + 16)
                if not isinstance(e, int):
                    pe.wait_ge(act_ok, e * 2 - 1)
                for b in range(2):
                    transpose4(b, P, [xe[:, (4 * b + j) * P:(4 * b + j + 1) * P] for j in range(4)]).then_inc(xe_tr, 1)

            def gate_up(e, j, n, turn=0):
                pe.wait_ge(xeT_lo_ok, e * 2 + 2)
                for u in range(8):
                    pe.wait_ge(lo_ok, turn * UNITS + n + u + 1)
                    for i in range(2):
                        k = u // 2 * 2 + i
                        w = (n + u) % RING, slice(i * HALF, (i + 1) * HALF)
                        mm = three(ps[:, 2 * j + u % 2, :], xeT_hi[:, k, :], xeT_lo[:, k, :],
                                   w_hi[:, w[0], w[1]], w_lo[:, w[0], w[1]], k == 0, k == KD - 1)
                    mm.then_inc(w_used, 1)

            def act_rows_T(e, j):
                pe.wait_ge(act_ok, e * 2 + j + 1)
                transpose4(6 + j, P, [act_r[:, j, c * P:(c + 1) * P] for c in range(4)]).then_inc(a_tr, 1)

            def down(e, j, n, turn=0):
                pe.wait_ge(aT_lo_ok, e * 2 + j + 1)
                if j == 0:
                    pe.wait_ge(ye_ok, e + CREDIT)
                for k in range(4):
                    pe.wait_ge(lo_ok, turn * UNITS + n + k + 1)
                    for half in range(2):
                        w = (n + k) % RING, slice(half * HALF, (half + 1) * HALF)
                        mm = three(ps[:, 4 + half, :], act_T_hi[:, 4 * j + k, :], act_T_lo[:, 4 * j + k, :],
                                   w_hi[:, w[0], w[1]], w_lo[:, w[0], w[1]], j == 0 and k == 0, j == 1 and k == 3)
                    mm.then_inc(w_used, 1)

            expert_rows_T(0)
            gate_up(0, 0, 0)
            gate_up(0, 1, 8)
            with pe.Fori(0, NE - 1) as e:
                act_rows_T(e, 0)
                expert_rows_T(e + 1)
                down(e, 0, FIRST, e)
                act_rows_T(e, 1)
                gate_up(e + 1, 0, FIRST + 4, e)
                down(e, 1, FIRST + 12, e)
                gate_up(e + 1, 1, FIRST + 16, e)
            end = FIRST + (NE - 1) * UNITS
            act_rows_T(NE - 1, 0)
            down(NE - 1, 0, end)
            act_rows_T(NE - 1, 1)
            down(NE - 1, 1, end + 4)

        @block.vector
        def _(dve):
            st = Steps(dve, dve_a)

            def mean_eps(dst, src, n):
                return dve.tensor_scalar(dst, src, 1.0 / n, EPS, ALU.mult, ALU.add)

            def low_part(dst, whole, high):
                return dve.tensor_tensor(dst, whole, high.bitcast(F32), ALU.subtract)

            def x_scale(t):
                dve.wait_ge(rstd_x, t + 1)
                dve.tensor_scalar(xs[:, t, :], xs[:, t, :], stat[:, 0, t:t + 1], None, ALU.mult).then_inc(xn, 1)

            for t in range(NT):
                dve.wait_ge(ssq_x, t + 1)
                mean_eps(stat[:, 0, t:t + 1], stat[:, 0, t:t + 1], D).then_inc(ms_x, 1)
                if t:
                    x_scale(t - 1)
            x_scale(NT - 1)
            dve.wait_ge(g_mix_in, 16)
            for c in range(0, 2 * KD, 2):
                half, k = divmod(c, KD)
                dve.wait_ge(hT_tr, c + 1)
                dve.tensor_scalar(hT[:, k, half * HALF:(half + 1) * HALF], ps[:, c % 4, :], g_mix_c[:, k:k + 1], None,
                                  ALU.mult).then_inc(hT_dve, 1)
            dve.wait_ge(small_in, 16 * small_loads)
            scale = 1.0 / math.sqrt(HQ)
            st.mark(dve.tensor_scalar(qhn_c[:], qhn_c[:], scale, None, ALU.mult))
            st.mark(dve.tensor_scalar(qhr_b[:], qhr_b[:], scale, None, ALU.mult))

            dve.wait_ge(consts, 3)
            st.link(dve.tensor_copy(pos_f[:], pos_i[:]))
            st.link(dve.tensor_tensor(ang[:], pos_f[:].unsqueeze(2).broadcast_to((P, NT, RH)),
                                      freq[:].unsqueeze(1).broadcast_to((P, NT, RH)), ALU.mult))
            two_pi = 2 * math.pi
            part1 = 6.25
            part2 = float(np.float32(round((two_pi - part1) * 2 ** 14) / 2 ** 14))
            part3 = two_pi - part1 - part2
            for j, shift in enumerate((0.0, 0.25)):
                st.mark(dve.tensor_scalar(turns_f[:, j], ang[:], 1 / two_pi, shift, ALU.mult, ALU.add))
            st.wait()
            st.link(dve.tensor_copy(turns_i[:], turns_f[:]))
            st.link(dve.tensor_copy(turns_f[:], turns_i[:]))
            for j, (dst, shift) in enumerate(((sin_t, 0.0), (cos_t, math.pi / 2))):
                st.link(dve.scalar_tensor_tensor(out=dst[:], in0=turns_f[:, j], scalar=-part1, in1=ang[:],
                                                 op0=ALU.mult, op1=ALU.add))
                for part in (part2, part3):
                    st.link(dve.scalar_tensor_tensor(out=dst[:], in0=turns_f[:, j], scalar=-part, in1=dst[:],
                                                     op0=ALU.mult, op1=ALU.add))
                st.link(dve.tensor_scalar(dst[:], dst[:], shift, 3.1415925, ALU.add, ALU.min))
                dve.tensor_scalar(dst[:], dst[:], -3.1415925, None, ALU.max).then_inc(trig_arg, 1)


            def lat_scale(t):
                dve.wait_ge(lat_rs, t + 1)
                st.mark(dve.tensor_scalar(lat_r[:, t, 2 * RANK:LA], lat_r[:, t, 2 * RANK:LA], stat[:, 1, t:t + 1], None,
                                          ALU.mult))
                dve.tensor_scalar(lat_r[:, t, LA:LA + KVR], lat_r[:, t, LA:LA + KVR], stat[:, 2, t:t + 1], None,
                                  ALU.mult).then_inc(lat_n, 1)

            for t in range(NT):
                a, b = 4 + 2 * (t % 2), 5 + 2 * (t % 2)
                dve.wait_ge(lat_mm, t + 1)
                dve.tensor_copy(lat_r[:, t, 0:LA], ps[:, a, 0:LA])
                dve.tensor_copy(lat_r[:, t, LA:LAT], ps[:, b, 0:LB]).then_inc(lat_ev, 1)
                if t:
                    lat_scale(t - 1)
                dve.wait_ge(lat_sq, t + 1)
                st.mark(mean_eps(stat[:, 1, t:t + 1], stat[:, 1, t:t + 1], QR))
                mean_eps(stat[:, 2, t:t + 1], stat[:, 2, t:t + 1], KVR).then_inc(lat_ms, 1)
            lat_scale(NT - 1)

            def lat_out(c):
                half, j = divmod(c, 7)
                cols = slice(half * HALF, (half + 1) * HALF)
                if j < 2:
                    return gateT[:, j, cols], ps[0:RANK, c % 4, :], 1.0
                if j < 5:
                    return cqT[:, j - 2, cols], ps[:, c % 4, :], qn_c[:, j - 2:j - 1]
                return ckvT[:, j - 5, cols], ps[:, c % 4, :], kvn_c[:, j - 5:j - 4]

            for c in range(0, 14, 2):
                dve.wait_ge(lat_tr, c + 1)
                dst, src, gain = lat_out(c)
                dve.tensor_scalar(dst, src, gain, None, ALU.mult).then_inc(latT_dve, 1)

            def rotate(dst, src, tmp, steps, parts=(0, 1)):
                copies = dst.shape[2] // ROPE
                dst = dst.rearrange("p t (c r) -> p t c r", c=copies)
                tmp4 = [tmp[:, a].unsqueeze(2).broadcast_to((P, NT, copies, RH)) for a in range(4)]
                x1r, x2r = src[:, :, 0:RH], src[:, :, RH:ROPE]
                if 0 in parts:
                    steps.mark(dve.tensor_tensor(tmp[:, 0], x1r, cos_t[:], ALU.mult))
                    steps.mark(dve.tensor_tensor(tmp[:, 1], x2r, sin_t[:], ALU.mult))
                    steps.mark(dve.tensor_tensor(tmp[:, 2], x2r, cos_t[:], ALU.mult))
                    steps.mark(dve.tensor_tensor(tmp[:, 3], x1r, sin_t[:], ALU.mult))
                if 1 not in parts:
                    return None
                steps.wait()
                steps.mark(dve.tensor_tensor(dst[:, :, :, 0:RH], tmp4[0], tmp4[1], ALU.subtract))
                return dve.tensor_tensor(dst[:, :, :, RH:ROPE], tmp4[2], tmp4[3], ALU.add)

            st.link(dve.tensor_tensor(k_rot[:], lat_r[:, :, LA + KVR:LAT],
                                      khr_b[:].unsqueeze(1).broadcast_to((P, NT, ROPE)), ALU.mult))
            dve.wait_ge(trig, 2)
            rotate(k_rot[:], k_rot[:], lat_r[:, 0:4, 0:NT * RH].rearrange("p a (t r) -> p a t r", t=NT), st) \
                .then_inc(k_rot_ok, 1)

            dve.wait_ge(latT_act, 7)

            def q_stats(n, s):
                dve.wait_ge(head_sq, n * 2 + 1)
                s.link(dve.tensor_reduce(stat[:, 4, :], sq_q[:], AX, ALU.add))
                mean_eps(stat[:, 4, :], stat[:, 4, :], HQ).then_inc(head_ms, 1)

            def q_gain(n, s):
                dve.wait_ge(head_rs, n * 2 + 1)
                s.link(dve.tensor_tensor(qR[:, :, 0:HQ], qR[:, :, 0:HQ],
                                         stat[:, 4, :].unsqueeze(2).broadcast_to((P, NT, HQ)), ALU.mult))

            def q_products(n, s):
                s.link(dve.tensor_tensor(qR[:, :, NOPE:HQ], qR[:, :, NOPE:HQ],
                                         qhr_b[:].unsqueeze(1).broadcast_to((P, NT, ROPE)), ALU.mult))
                rotate(qR[:, :, NOPE:HQ + ROPE], qR[:, :, NOPE:HQ], r_tmp, s, parts=(0,))

            def q_rotate(n, s):
                rotate(qR[:, :, NOPE:HQ + ROPE], qR[:, :, NOPE:HQ], r_tmp, s, parts=(1,)).then_inc(head_n, 1)

            def k_stats(n, s):
                dve.wait_ge(head_sq, n * 2 + 2)
                s.link(dve.tensor_reduce(stat[:, 5, :], sq_q[:, :, 0:NOPE], AX, ALU.add))
                s.link(dve.tensor_tensor(stat[:, 5, :], stat[:, 5, :], stat[:, 3, :], ALU.add))
                mean_eps(stat[:, 5, :], stat[:, 5, :], HQ).then_inc(head_ms, 1)

            def k_norm(n, s):
                dve.wait_ge(head_rs, n * 2 + 2)
                s.mark(dve.tensor_tensor(kvR[:, :, 0:NOPE], kvR[:, :, 0:NOPE],
                                         stat[:, 5, :].unsqueeze(2).broadcast_to((P, NT, NOPE)), ALU.mult))
                dve.tensor_tensor(kRr[:].rearrange("p t (c r) -> p t c r", c=2),
                                  k_rot[:].unsqueeze(2).broadcast_to((P, NT, 2, ROPE)),
                                  stat[:, 5, :].unsqueeze(2).unsqueeze(3).broadcast_to((P, NT, 2, ROPE)),
                                  ALU.mult).then_inc(head_n, 1)

            prep = 1 + 1 + 1 + 5 + 1 + 1 + 1
            s0 = Steps(dve, head_step, per=prep)
            dve.wait_ge(lat_sq, NT)
            dve.wait_ge(k_rot_ok, 1)
            q_stats(0, s0)
            q_gain(0, s0)
            q_products(0, s0)
            q_rotate(0, s0)
            k_stats(0, s0)
            k_norm(0, s0)
            s0.end()

            def seam_low(i, c):
                what, half = divmod(c, 2)
                cols = slice(half * HALF, (half + 1) * HALF)
                dve.wait_ge(seam_hi, i * 8 + c + 1)
                if what % 2 == 0:
                    hi, lo = ((qT_hi, qT_lo), (kT_hi, kT_lo))[what // 2]
                    ins = dve.scalar_tensor_tensor(out=lo[:, cols], in0=ps[:, SEAM_BANKS[c], :],
                                               scalar=(qhn_c, khn_c)[what // 2][:, 0:1],
                                               in1=hi[:, cols].bitcast(F32), op0=ALU.mult, op1=ALU.subtract)
                elif what == 1:
                    ins = low_part(qr_T[ROPE:P, cols], ps[ROPE:P, SEAM_BANKS[c], :], qr_T[ROPE:P, cols])
                else:
                    ins = low_part(kr_lo[:, cols], ps[0:ROPE, SEAM_BANKS[c], :], kr_T[0:ROPE, cols])
                ins.then_inc(seam_lo, 1)

            for c in range(8):
                seam_low(0, c)

            def mla_head(i, last):
                s = Steps(dve, head_step, base=prep, turn=i, per=prep)
                dve.wait_ge(v_hi_ok, i + 1)
                low_part(v_lo[:], kvR[:, :, NOPE:NOPE + MV], v_hi[:]).then_inc(v_ok, 1)

                def normalise(q):
                    dve.wait_ge(exp_ok, i * 8 + q + 1)
                    dve.reciprocal(row_inv[:, q:q + 1], row_sum[:, q:q + 1]).then_inc(inv_ok, 1)
                    dve.wait_ge(inv_ok, i * 8 + q + 1)
                    dve.tensor_scalar(probs[:, q % 3, :], probs[:, q % 3, :], row_inv[:, q:q + 1], None,
                                      ALU.mult).then_inc(p_ok, 1)

                def head_out(j):
                    dve.wait_ge(pv_mm, i * 2 + j + 1 + CREDIT)
                    dve.wait_ge(ob_out, i * 32 + CREDIT)
                    cols = slice(j * HALF, (j + 1) * HALF)
                    dve.tensor_copy(obS[:, cols], ps[:, 6, :]).then_inc(ob_ev, 1)

                for n in range(10):
                    if n < 8:
                        dve.wait_ge(s_mm, i * 8 + n + 1)
                        dve.tensor_reduce(row_max[:, n:n + 1], ps[:, 2 * (n % 2):2 * (n % 2) + 2, :],
                                          mybir.AxisListType.XY, ALU.max, negate=True).then_inc(max_ok, 1)
                    if 1 <= n <= 8:
                        normalise(n - 1)
                    if n == 8 and not last:
                        seam_low(i + 1, 0)
                    if n == 9 and not last:
                        seam_low(i + 1, 1)
                        seam_low(i + 1, 2)
                    if n >= 2:
                        q = n - 2
                        for b in range(2):
                            dve.wait_ge(pt_hi, i * 16 + 2 * q + b + 1)
                            at = (slice(None), q // 4, slice(4 * b, 4 * b + 4), slice((q % 4) * P, (q % 4 + 1) * P))
                            low_part(pT_lo[at], ps[:, 4 + b, :].rearrange("p (a c) -> p a c", a=4),
                                     pT_hi[at]).then_inc(pt_lo, 1)
                    if not last:
                        if n == 3:
                            q_stats(i + 1, s)
                        if n == 4:
                            q_gain(i + 1, s)
                        if n == 5:
                            q_products(i + 1, s)
                        if n == 6:
                            q_rotate(i + 1, s)
                        if n == 7:
                            k_stats(i + 1, s)
                        if n == 8:
                            k_norm(i + 1, s)
                        if n == 9:
                            for c in range(3, 8):
                                seam_low(i + 1, c)
                    if n == 8:
                        head_out(0)
                head_out(1)
                if not last:
                    s.end()

            def dense_lo(n, before=0):
                dve.wait_ge(d_hi_ok, before + n + 1)
                low_part(d_lo[:, n % 2, :], d_raw[:, n % 2, :], d_hi[:, n % 2, :]).then_inc(d_lo_ok, 1)

            with dve.Fori(0, MH - 1) as i:
                mla_head(i, False)
            dense_lo(0)
            dense_lo(1)
            mla_head(MH - 1, True)


            for k in range(KD):
                dve.wait_ge(hT_hi_ok, k + 1)
                low_part(hT_lo[:, k, :], hT_again[:, k, :], hT_hi[:, k, :]).then_inc(hT_lo_ok, 1)
            dve.wait_ge(gate_consts, 1)
            dve.wait_ge(ob_out, 32 * MH + CREDIT)

            def outputs_even(h):
                for c in (0, 2):
                    half, j = divmod(c, 2)
                    dve.wait_ge(o_tr, h * 4 + c + 1)
                    dve.tensor_scalar(oaS[:, j, half * HALF:(half + 1) * HALF], ps[:, 4 + c, :], onorm_c[:, j:j + 1],
                                      None, ALU.mult).then_inc(oa_dve, 1)

            def gla_head(h, first=False):
                s = Steps(dve, gla_step, turn=h, per=2)
                mine = h * GLA_UNITS

                def gate_bias(d):
                    dve.wait_ge(z_mm, h * 2 + d + 1)
                    if d == 0:
                        dve.wait_ge(wa_in, h * 64 + 64)
                    else:
                        dve.wait_ge(ed_ok, h * 2 + 1)
                    dve.tensor_scalar(zT[:].rearrange("p (a c) -> p a c", a=2), ps[:, 6 - 2 * d:8 - 2 * d, :],
                                      b_a2[:, d:d + 1], None, ALU.add).then_inc(z_dve, 1)

                for d in range(2):
                    if d == 0:
                        gate_bias(0)
                    dve.wait_ge(z_act, h * 6 + 3 * d + 3)
                    dve.scalar_tensor_tensor(out=eT[:], in0=zT[:], scalar=0.0, in1=eT[:], op0=ALU.min,
                                             op1=ALU.subtract).then_inc(ls_ok, 1)
                    dve.wait_ge(ls_ok, h * 2 + d + 1)
                    rev = slice(None, None, -1) if d else slice(None)
                    if d == 1:
                        dve.wait_ge(e_ok, h * 4 + 2)
                    dve.tensor_tensor_scan(bT[:, rev], scan_m[:], eT[:, rev], 0.0, ALU.mult,
                                           ALU.add).then_inc(b_ok, 1)
                    dve.wait_ge(b_ok, h * 2 + d + 1)
                    b3 = bT[:].rearrange("p (n c) -> p n c", c=CH)
                    last = b3[:, :, 0:1] if d else b3[:, :, CH - 1:CH]
                    if d == 1:
                        dense_lo(4, mine)
                    dve.tensor_tensor(zT[:].rearrange("p (n c) -> p n c", c=CH), last.broadcast_to((P, NCH, CH)), b3,
                                      ALU.subtract).then_inc(tail_ok, 1)
                    dve.wait_ge(e_ok, h * 4 + 2 * d + 1)
                    e3 = qt[:, d, :].rearrange("p (n c) -> p n c", c=CH)
                    s.link(dve.tensor_copy(decay[:, d, :].unsqueeze(2), e3[:, :, 0:1] if d else e3[:, :, CH - 1:CH]))
                    if d == 0:
                        dense_lo(2, mine)
                        if not first:
                            outputs_even(h - 1)
                        gate_bias(1)
                        dense_lo(3, mine)
                        dve.wait_ge(qk_ev, h * 4 + 4)
                    else:
                        dense_lo(5, mine)
                    dve.tensor_tensor(qt[:, d, :], qt[:, d, :], qk_T[:, 0, :], ALU.mult).then_inc(mats_ok, 1)
                    dve.wait_ge(e_ok, h * 4 + 2 * d + 2)
                    dve.tensor_tensor(kt[:, d, :], kt[:, d, :], qk_T[:, 1, :], ALU.mult).then_inc(mats_ok, 1)
                    dve.wait_ge(ed_ok, h * 2 + d + 1)
                    dve.tensor_tensor(kd[:, d, :], kd[:, d, :], qk_T[:, 1, :], ALU.mult).then_inc(mats_ok, 1)
                dense_lo(6, mine)
                dve.wait_ge(mats_ok, h * 6 + 6)
                for c in range(4):
                    d, half = divmod(c, 2)
                    dve.wait_ge(kd_tr, h * 4 + c + 1)
                    dve.tensor_copy(kdR[:, d, 4 * half:4 * half + 4, :],
                                    ps[:, c, :].rearrange("p (a c) -> p a c", a=4)).then_inc(kd_ev, 1)
                for half in range(2):
                    t4 = slice(4 * half, 4 * half + 4)
                    for d in range(2):
                        dve.wait_ge(att_mm, h * 4 + 2 * half + d + 1)
                        dst = (att_f, att_b)[d][:, t4, :]
                        src = ps[:, 4 + 2 * half + d, :].rearrange("p (a c) -> p a c", a=4)
                        dve.tensor_tensor(dst, src, keep_hi[:, d, :].unsqueeze(1).broadcast_to((P, 4, P)),
                                          ALU.min).then_inc(att_ok, 1)
                        dve.wait_ge(att_ok, h * 10 + half * 5 + 2 * d + 1)
                        dve.tensor_tensor(dst, dst, keep_lo[:, d, :].unsqueeze(1).broadcast_to((P, 4, P)),
                                          ALU.max).then_inc(att_ok, 1)
                    dve.wait_ge(att_ok, h * 10 + half * 5 + 4)
                    dve.tensor_tensor(att[:, t4, :], att_f[:, t4, :], att_b[:, t4, :], ALU.add).then_inc(att_ok, 1)
                dense_lo(7, mine)
                dve.memset(state[:, 1, NCH - 1, :], 0.0).then_inc(st_ok, 1)
                dve.memset(state[:, 0, 0, :], 0.0).then_inc(st_ok, 1)
                for n in range(30):
                    d, c = (1, NCH - 1 - n) if n < 15 else (0, n - 15)
                    to = c - 1 if d else c + 1
                    dve.wait_ge(ds_mm, h * 30 + n + 1)
                    dve.wait_ge(st_ok, h * 32 + n + 2)
                    dve.scalar_tensor_tensor(out=state[:, d, to, :], in0=state[:, d, c, :], scalar=decay[:, d, c:c + 1],
                                             in1=ps[:, 4 + n % 4, 0:DV],
                                             op0=ALU.mult, op1=ALU.add).then_inc(st_ok, 1)

                def o_scale(half):
                    dve.wait_ge(o_sq, h * NT + 4 * half + 4)
                    mean_eps(stat[:, 6, 4 * half:4 * half + 4], stat[:, 6, 4 * half:4 * half + 4], DV).then_inc(o_ms, 1)
                    dve.wait_ge(o_rs, h * 2 + half + 1)
                    if half == 0:
                        dve.wait_ge(silu_ok, h + 1)
                    for t in range(4 * half, 4 * half + 4):
                        ins = dve.scalar_tensor_tensor(out=oR[:, t, :], in0=oR[:, t, :], scalar=stat[:, 6, t:t + 1],
                                                       in1=vr[:, t, DV:2 * DV], op0=ALU.mult, op1=ALU.mult)
                    ins.then_inc(o_n, 1)

                for t in range(NT):
                    dve.wait_ge(o_mm, h * NT + t + 1)
                    dve.tensor_copy(oR[:, t, :], ps[:, O_BANKS[t % 4], 0:DV]).then_inc(o_ev, 1)
                    if t == 5:
                        o_scale(0)
                o_scale(1)
                s.end()

            gla_head(0, first=True)
            with dve.Fori(1, GH) as h:
                gla_head(h)
            outputs_even(GH - 1)

            def product(b, i, n, turns=0):
                dve.wait_ge(d_used, turns * 4 + n + 1)
                dve.wait_ge(g_ev, turns * 2 + b * KD + i + 1)
                banks = ps[:, 4 + 2 * (i % 2):6 + 2 * (i % 2), :]
                gate = sg[:, i % 2, :]
                gate3 = gate.rearrange("p (a c) -> p a c", a=2)
                m = mT[:, bass.ds(turns * 2 + i, 1), :].rearrange("p a s -> p (a s)")
                if b == 0:
                    dve.tensor_tensor(m.rearrange("p (a c) -> p a c", a=2), banks, gate3, ALU.mult).then_inc(y_ev, 1)
                else:
                    dve.tensor_tensor(gate3, banks, gate3, ALU.mult).then_inc(y_ev, 1)
                    dve.wait_ge(y_ev, turns * 2 + b * KD + i + 1 + PAIRS)
                    dve.tensor_tensor(m, m, gate, ALU.add).then_inc(m_ok, 1)

            def merged_lo(k):
                dve.wait_ge(mT_hi_ok, k + 1)
                low_part(mT_lo[:, k, :], mT[:, k, :], mT_hi[:, k, :]).then_inc(mT_lo_ok, 1)

            for b in range(2):
                n = MERGE0 + b * JOBS
                for k in range(KD):
                    dve.wait_ge(oT_hi_ok, b * KD + k + 1)
                    src = stage[:, k % 2, :] if b else mT[:, k, :]
                    low_part(oT_lo[:, k, :], src, oT_hi[:, k, :]).then_inc(oT_lo_ok, 1)
                dense_lo(n + 2)
                dense_lo(n + 3)
                with dve.Fori(0, 3) as r:
                    for i in range(2):
                        dense_lo(n + 4 + 2 * i, r * 4)
                        product(b, i, n + 2 + 2 * i, r)
                        dense_lo(n + 5 + 2 * i, r * 4)
                if b:
                    for k in range(6):
                        merged_lo(k)
                for i in (6, 7):
                    dense_lo(n + 10 + i)
                    product(b, i, n + 8 + i)
                    if b:
                        merged_lo(i)


            def ffn_norm(t):
                dve.wait_ge(x1_sq, t + 1)
                mean_eps(stat[:, 7, t:t + 1], stat[:, 7, t:t + 1], D).then_inc(x1_ms, 1)
                dve.wait_ge(x1_rs, t + 1)
                dve.scalar_tensor_tensor(out=h2[:, t, :], in0=x1[:, t, :], scalar=stat[:, 7, t:t + 1], in1=g_ffn_b[:],
                                         op0=ALU.mult, op1=ALU.mult).then_inc(h2_ok, 1)

            for g in range(2):
                for k in range(KD):
                    if k < KD - 1 and g * KD + k + 2 < 2 * KD:
                        dense_lo(OUT0 + g * KD + k + 2)
                    if g == 1 and 2 <= k < 6:
                        ffn_norm(k - 2)
                if g == 0:
                    dve.wait_ge(x1_in, 16 * NT)
                    dve.wait_ge(gf_in, 16)
                for j in range(4):
                    for half in range(2):
                        if 2 * j + half < 7:
                            dve.wait_ge(f_mm, g * 7 + 2 * j + half + 1)
                        else:
                            dve.wait_ge(d_used, OUT0 + (g + 1) * KD)
                        x = x1[:, 4 * g + j, half * HALF:(half + 1) * HALF]
                        dve.tensor_tensor(x, ps[:, 4 * half + j, :], x, ALU.add).then_inc(f_ev, 1)
                if g == 0:
                    dense_lo(OUT0 + KD + 1)
                else:
                    for j in range(4):
                        ffn_norm(4 + j)
            for t in range(NT):
                dve.wait_ge(h2_tr, 2 * t + 1)
                if t >= 2:
                    dve.wait_ge(lg_mm, t - 1)
                dve.tensor_copy(h2T[:, t % 2, 0:4, :], ps[:, 2 * (t % 2), :].rearrange("p (a c) -> p a c", a=4)) \
                    .then_inc(h2T_dve, 1)

            dve.wait_ge(lg_mm, NT)
            dve.wait_ge(rows_out, 32 * NT)
            lg = ps[:, 7, 0:NT * NE].rearrange("p (t e) -> p t e", t=NT)
            s = Steps(dve, soft)
            s.link(dve.tensor_reduce(stat[:, 8, :], lg, AX, ALU.max))
            s.mark(dve.tensor_tensor(aff[:], lg, stat[:, 8, :].unsqueeze(2).broadcast_to((P, NT, NE)), ALU.subtract))
            dve.wait_ge(soft_exp, 1)
            s.link(dve.tensor_reduce(stat[:, 9, :], aff[:], AX, ALU.add))
            s.link(dve.reciprocal(stat[:, 10, :], stat[:, 9, :]))
            s.mark(dve.tensor_tensor(aff[:], aff[:], stat[:, 10, :].unsqueeze(2).broadcast_to((P, NT, NE)), ALU.mult))
            dve.wait_ge(aff_tr, 1)
            t = Steps(dve, affT_ok)
            t.link(dve.tensor_copy(affT[:, 0, :], ps[0:2 * NE, 0, :]))
            for r in range(CAP // 8):
                src, v8 = affT[:, r % 2, :], top_v[:, 8 * r:8 * r + 8]
                t.link(dve.max(v8, src))
                t.mark(dve.max_index(top_i[:, 8 * r:8 * r + 8], v8, src))
                t.link(dve.match_replace(affT[:, (r + 1) % 2, :], v8, src, -1.0))
            dve.tensor_copy(top_f[:], top_i[:]).then_inc(top_ok, 1)
            dve.tensor_copy(top_rev[:, 0, ::-1], top_v[:]).then_inc(top_ok, 1)
            dve.wait_ge(top_ok, 1)
            dve.tensor_copy(top_rev[:, 1, ::-1], top_f[:]).then_inc(top_ok, 1)
            dve.wait_ge(top_tr, 1)
            t.link(dve.tensor_copy(halves[:], ps[:, 2, 0:8 * NE].rearrange("p (a e) -> p a e", e=NE)))
            v0, v1, i0, i1, first = halves[:, 0, :], halves[:, 5, :], halves[:, 2, :], halves[:, 7, :], halves[:, 1, :]
            dve.tensor_tensor(val_c[:], v0, v1, ALU.max).then_inc(idx_ok, 1)
            t.mark(dve.tensor_tensor(first, v0, v1, ALU.is_ge))
            t.link(dve.tensor_scalar(i1, i1, float(S // 2), None, ALU.add))
            t.link(dve.tensor_tensor(i0, i0, i1, ALU.subtract))
            t.link(dve.tensor_tensor(i0, i0, first, ALU.mult))
            dve.tensor_tensor(idx_c[:], i0, i1, ALU.add).then_inc(idx_ok, 1)
            dve.wait_ge(idx_ok, 2)

            def split(n, turn=0):
                dve.wait_ge(hi_ok, turn * UNITS + n + 1)
                low_part(w_lo[:, n % RING, :], w_raw[:, n % RING, :], w_hi[:, n % RING, :]).then_inc(lo_ok, 1)

            def rows_in(e):
                for b in range(2):
                    dve.wait_ge(xeT_hi_ok, e * 2 + b + 1)
                    rows = slice(4 * b, 4 * b + 4)
                    low_part(xeT_lo[:, rows, :], ps[:, b, :].rearrange("p (a c) -> p a c", a=4),
                             xeT_hi[:, rows, :]).then_inc(xeT_lo_ok, 1)

            def activate(e, j):
                dve.wait_ge(silu_e, e * 2 + j + 1)
                dve.tensor_tensor(act_r[:, j, :], ps[:, 2 * j + 1, :], silu_g[:, j, :], ALU.mult).then_inc(act_ok, 1)

            def act_in(e, j):
                dve.wait_ge(aT_hi_ok, e * 2 + j + 1)
                rows = slice(4 * j, 4 * j + 4)
                low_part(act_T_lo[:, rows, :], ps[:, 6 + j, :].rearrange("p (a c) -> p a c", a=4),
                         act_T_hi[:, rows, :]).then_inc(aT_lo_ok, 1)

            def affinity(e):
                dve.tensor_copy(val_s[:], val_c[:, bass.ds(e, 1)]).then_inc(val_ok, 1)

            rows_in(0)
            for n in range(FIRST):
                split(n)
                if n == 8 + LEAD - 1:
                    activate(0, 0)
            with dve.Fori(0, NE - 1) as e:
                for u in range(UNITS):
                    split(FIRST + u, e)
                    if u == LEAD - 1:
                        act_in(e, 0)
                        activate(e, 1)
                        rows_in(e + 1)
                    if u == 4 + LEAD - 1:
                        act_in(e, 1)
                    if u == 12 + LEAD - 1:
                        activate(e + 1, 0)
                        dve.wait_ge(ye_ok, e + CREDIT)
                        affinity(e)
            for u in range(8):
                split(FIRST + (NE - 1) * UNITS + u)
                if u == LEAD - 1:
                    act_in(NE - 1, 0)
                    activate(NE - 1, 1)
                if u == 4 + LEAD - 1:
                    act_in(NE - 1, 1)
            dve.wait_ge(ye_ok, NE - 1 + CREDIT)
            affinity(NE - 1)

        @block.scalar
        def _(act):
            nc.scalar.preload_act_table_set("natural_log_exp_and_others")
            a_st = Steps(act, act_a)
            for t in range(NT):
                act.wait_ge(x_in[t], 16)
                nc.scalar.activation(sq_a[:], xs[:, t, :], ACT.Square, accum_out=stat[:, 0, t:t + 1]).then_inc(ssq_x, 1)
                act.wait_ge(ssq_x, t + 1)
            act.wait_ge(g_mix_in, 16)
            for c in range(1, 2 * KD, 2):
                half, k = divmod(c, KD)
                act.wait_ge(hT_tr, c + 1)
                nc.scalar.activation(hT[:, k, half * HALF:(half + 1) * HALF], ps[:, c % 4, :], ACT.Copy,
                                     scale=g_mix_c[:, k:k + 1]).then_inc(hT_act, 1)
            for j, tbl in enumerate((sin_t, cos_t)):
                act.wait_ge(trig_arg, j + 1)
                nc.scalar.activation(tbl[:], tbl[:], ACT.Sin).then_inc(trig, 1)
            act.wait_ge(small_in, 16 * small_loads)
            for t in range(NT):
                act.wait_ge(lat_ev, t + 1)
                a_st.link(nc.scalar.activation(sq_a[:, 0:QR], lat_r[:, t, 2 * RANK:LA], ACT.Square,
                                               accum_out=stat[:, 1, t:t + 1]))
                a_st.link(nc.scalar.activation(sq_a[:, 0:KVR], lat_r[:, t, LA:LA + KVR], ACT.Square,
                                               accum_out=stat[:, 2, t:t + 1]))
                nc.scalar.activation(sq_a[:, 0:ROPE], lat_r[:, t, LA + KVR:LAT], ACT.Square,
                                     accum_out=stat[:, 3, t:t + 1]).then_inc(lat_sq, 1)
                act.wait_ge(lat_sq, t + 1)
            for c in range(1, 14, 2):
                half, j = divmod(c, 7)
                cols = slice(half * HALF, (half + 1) * HALF)
                act.wait_ge(lat_tr, c + 1)
                if j < 2:
                    ins = nc.scalar.activation(gateT[:, j, cols], ps[0:RANK, c % 4, :], ACT.Copy)
                elif j < 5:
                    ins = nc.scalar.activation(cqT[:, j - 2, cols], ps[:, c % 4, :], ACT.Copy,
                                               scale=qn_c[:, j - 2:j - 1])
                else:
                    ins = nc.scalar.activation(ckvT[:, j - 5, cols], ps[:, c % 4, :], ACT.Copy,
                                               scale=kvn_c[:, j - 5:j - 4])
                ins.then_inc(latT_act, 1)

            act.wait_ge(h_out, 16)
            act.wait_ge(k_rot_ok, 1)
            act.wait_ge(lat_tr, 14)

            def take(n, g):
                act.wait_ge(prj_mm, n * 8 + g + 1)
                width = HQ if g < 4 else NOPE + MV
                dst = (qR[:, :, 0:HQ] if g < 4 else kvR)[:, 2 * (g % 4):2 * (g % 4) + 2, :]
                if g == 4 and not isinstance(n, int):
                    act.wait_ge(v_ok, n)
                nc.scalar.activation(dst, ps[:, project_bank(n, g), 0:2 * width].rearrange("p (a c) -> p a c", a=2),
                                     ACT.Copy).then_inc(prj_ev, 1)
                if g == 3:
                    act.wait_ge(prj_ev, n * 8 + 4)
                    act.wait_ge(head_ms, n * 2)
                    nc.scalar.activation(sq_q[:], qR[:, :, 0:HQ], ACT.Square).then_inc(head_sq, 1)

            def k_squares(n):
                act.wait_ge(prj_ev, n * 8 + 8)
                act.wait_ge(head_n, n * 2 + 1)
                nc.scalar.activation(sq_q[:, :, 0:NOPE], kvR[:, :, 0:NOPE], ACT.Square).then_inc(head_sq, 1)

            for g in range(8):
                take(0, g)
            k_squares(0)

            def seam_high(i, c):
                what, half = divmod(c, 2)
                cols = slice(half * HALF, (half + 1) * HALF)
                act.wait_ge(seam_tr, i * 8 + c + 1)
                if what % 2 == 0:
                    ins = nc.scalar.activation((qT_hi, kT_hi)[what // 2][:, cols], ps[:, SEAM_BANKS[c], :], ACT.Copy,
                                           scale=(qhn_c, khn_c)[what // 2][:, 0:1])
                else:
                    ins = nc.scalar.activation((qr_T, kr_T)[what // 2][:, cols], ps[:, SEAM_BANKS[c], :], ACT.Copy)
                ins.then_inc(seam_hi, 1)

            for c in range(8):
                seam_high(0, c)

            def mla_head(i, last):
                act.wait_ge(pv_mm, i * 2 + CREDIT)
                nc.scalar.activation(v_hi[:], kvR[:, :, NOPE:NOPE + MV], ACT.Copy).then_inc(v_hi_ok, 1)
                for n in range(10):
                    if n < 8:
                        act.wait_ge(max_ok, i * 8 + n + 1)
                        if n >= 3:
                            act.wait_ge(p_tr, i * 16 + 2 * (n - 3) + 2)
                        nc.scalar.activation(probs[:, n % 3, :].rearrange("p (a c) -> p a c", a=2),
                                             ps[:, 2 * (n % 2):2 * (n % 2) + 2, :], ACT.Exp, bias=row_max[:, n:n + 1],
                                             accum_out=row_sum[:, n:n + 1]).then_inc(exp_ok, 1)
                        if not last and n < 6:
                            take(i + 1, AFTER_SCORES[n])
                    if n == 8 and not last:
                        seam_high(i + 1, 0)
                    if n == 9 and not last:
                        seam_high(i + 1, 1)
                        seam_high(i + 1, 2)
                    if n >= 2:
                        q = n - 2
                        for b in range(2):
                            act.wait_ge(p_tr, i * 16 + 2 * q + b + 1)
                            at = (slice(None), q // 4, slice(4 * b, 4 * b + 4), slice((q % 4) * P, (q % 4 + 1) * P))
                            nc.scalar.activation(pT_hi[at], ps[:, 4 + b, :].rearrange("p (a c) -> p a c", a=4),
                                                 ACT.Copy).then_inc(pt_hi, 1)
                        if not last and n in AFTER_TRANSPOSES:
                            take(i + 1, AFTER_TRANSPOSES[n])
                    if n == 6 and not last:
                        k_squares(i + 1)
                    if n == 9 and not last:
                        for c in range(3, 8):
                            seam_high(i + 1, c)

            def dense_hi(n, before=0):
                act.wait_ge(d_in[n % 2], before * 16 + 32 * (n // 2) + 32)
                if not isinstance(before, int) or before + n >= 2:
                    act.wait_ge(d_used, before + n - 1)
                nc.scalar.activation(d_hi[:, n % 2, :], d_raw[:, n % 2, :], ACT.Copy).then_inc(d_hi_ok, 1)

            with act.Fori(0, MH - 1) as i:
                mla_head(i, False)
            dense_hi(0)
            dense_hi(1)
            mla_head(MH - 1, True)


            act.wait_ge(hT_in, 16)
            act.wait_ge(pv_mm, 2 * MH + CREDIT)
            for k in range(KD):
                nc.scalar.activation(hT_hi[:, k, :], hT_again[:, k, :], ACT.Copy).then_inc(hT_hi_ok, 1)

            def outputs_odd(h):
                for c in (1, 3):
                    half, j = divmod(c, 2)
                    act.wait_ge(o_tr, h * 4 + c + 1)
                    nc.scalar.activation(oaS[:, j, half * HALF:(half + 1) * HALF], ps[:, 4 + c, :], ACT.Copy,
                                         scale=onorm_c[:, j:j + 1]).then_inc(oa_act, 1)

            def gla_head(h, first=False):
                mine = h * GLA_UNITS

                def take_qk():
                    act.wait_ge(d_used, mine + 2)
                    for c in range(4):
                        j, half = divmod(c, 2)
                        nc.scalar.activation(qk_T[:, j, half * HALF:(half + 1) * HALF], ps[:, c, :], ACT.Copy,
                                             scale=DK ** -0.5 if j == 0 else 1.0).then_inc(qk_ev, 1)

                def take_vr(t):
                    if t < NT - 1:
                        act.wait_ge(vr_mm, h * (NT - 1) + t + 1)
                    else:
                        act.wait_ge(d_used, mine + GLA_UNITS)
                    nc.scalar.activation(vr[:, t, :], ps[:, t, :], ACT.Copy).then_inc(vr_ev, 1)

                for d in range(2):
                    act.wait_ge(z_dve, h * 2 + d + 1)
                    if d == 1:
                        act.wait_ge(b_ok, h * 2 + 1)
                    nc.scalar.activation(eT[:], zT[:], ACT.Abs).then_inc(z_act, 1)
                    act.wait_ge(z_act, h * 6 + 3 * d + 1)
                    nc.scalar.activation(eT[:], eT[:], ACT.Exp, scale=-1.0).then_inc(z_act, 1)
                    act.wait_ge(z_act, h * 6 + 3 * d + 2)
                    nc.scalar.activation(eT[:], eT[:], ACT.Ln, bias=1.0).then_inc(z_act, 1)
                    dense_hi((2, 4)[d], mine)
                    act.wait_ge(b_ok, h * 2 + d + 1)
                    nc.scalar.activation(qt[:, d, :], bT[:], ACT.Exp, scale=1 / GATE_DIV).then_inc(e_ok, 1)
                    nc.scalar.activation(kt[:, d, :], bT[:], ACT.Exp, scale=-1 / GATE_DIV).then_inc(e_ok, 1)
                    if d == 0 and not first:
                        outputs_odd(h - 1)
                    act.wait_ge(tail_ok, h * 2 + d + 1)
                    nc.scalar.activation(kd[:, d, :], zT[:], ACT.Exp, scale=1 / GATE_DIV).then_inc(ed_ok, 1)
                    if d == 0:
                        dense_hi(3, mine)
                        take_qk()
                    else:
                        dense_hi(5, mine)
                        dense_hi(6, mine)
                if not first:
                    act.wait_ge(oa_out, h * 16)
                for t in range(NT):
                    take_vr(t)
                act.wait_ge(vr_ev, h * NT + NT)
                nc.scalar.activation(vr[:, :, DV:2 * DV], vr[:, :, DV:2 * DV], ACT.Silu).then_inc(silu_ok, 1)
                nc.scalar.preload_act_table_set("natural_log_exp_and_others")
                dense_hi(7, mine)
                act.wait_ge(att_mm, h * 4 + 4)
                for t in range(NT):
                    act.wait_ge(o_ev, h * NT + t + 1)
                    nc.scalar.activation(o_sqr[:, t, :], oR[:, t, :], ACT.Square,
                                         accum_out=stat[:, 6, t:t + 1]).then_inc(o_sq, 1)

            gla_head(0, first=True)
            with act.Fori(1, GH) as h:
                gla_head(h)
            outputs_odd(GH - 1)

            def gate(b, i, n, turns=0):
                act.wait_ge(d_used, turns * 4 + n + 1)
                if not isinstance(turns, int) or b * KD + i >= 2:
                    act.wait_ge(y_ev, turns * 2 + b * KD + i - 1 + PAIRS)
                if b and i >= 2:
                    act.wait_ge(m_ok, turns * 2 + i - 1)
                k = i % 2
                nc.scalar.activation(sg[:, k, :].rearrange("p (a c) -> p a c", a=2), ps[:, 2 * k:2 * k + 2, :],
                                     ACT.Sigmoid).then_inc(g_ev, 1)

            def merged_hi(k):
                act.wait_ge(m_ok, k + 1)
                nc.scalar.activation(mT_hi[:, k, :], mT[:, k, :], ACT.Copy).then_inc(mT_hi_ok, 1)

            for b in range(2):
                n = MERGE0 + b * JOBS
                for k in range(KD):
                    if b:
                        act.wait_ge(d_used, n)
                        act.wait_ge(stage_in[k % 2], 16 * (k // 2) + 16)
                    else:
                        act.wait_ge(oa_back, 16 if k < 6 else 32)
                    src = stage[:, k % 2, :] if b else mT[:, k, :]
                    nc.scalar.activation(oT_hi[:, k, :], src, ACT.Copy).then_inc(oT_hi_ok, 1)
                dense_hi(n + 2)
                gate(b, 0, n)
                dense_hi(n + 3)
                gate(b, 1, n + 1)
                with act.Fori(0, 3) as r:
                    for i in range(2):
                        dense_hi(n + 4 + 2 * i, r * 4)
                        dense_hi(n + 5 + 2 * i, r * 4)
                        gate(b, i + 2, n + 3 + 2 * i, r)
                if b:
                    act.wait_ge(d_used, OUT0 - 2)
                    for k in range(6):
                        merged_hi(k)
                for i in (6, 7):
                    dense_hi(n + 10 + i)
                    if b:
                        merged_hi(i)
            for g in range(2):
                for k in range(KD):
                    if g * KD + k + 2 < 2 * KD:
                        dense_hi(OUT0 + g * KD + k + 2)
                for j in range(4):
                    t = 4 * g + j
                    act.wait_ge(f_ev, g * 8 + 2 * j + 2)
                    nc.scalar.activation(h2[:, t, :], x1[:, t, :], ACT.Square, accum_out=stat[:, 7, t:t + 1]) \
                        .then_inc(x1_sq, 1)
            for t in range(NT):
                act.wait_ge(h2_tr, 2 * t + 2)
                if t >= 2:
                    act.wait_ge(lg_mm, t - 1)
                nc.scalar.activation(h2T[:, t % 2, 4:8, :], ps[:, 2 * (t % 2) + 1, :].rearrange("p (a c) -> p a c", a=4),
                                     ACT.Copy).then_inc(h2T_act, 1)
            act.wait_ge(soft, 2)
            nc.scalar.activation(aff[:], aff[:], ACT.Exp).then_inc(soft_exp, 1)

            def split(n, turn=0):
                act.wait_ge(raw_in[n % RING], turn * 32 + 16 * (n // RING) + 16)
                if n >= RING:
                    act.wait_ge(w_used, turn * UNITS + n - RING + 1)
                nc.scalar.activation(w_hi[:, n % RING, :], w_raw[:, n % RING, :], ACT.Copy).then_inc(hi_ok, 1)

            def rows_in(e):
                for b in range(2):
                    act.wait_ge(xe_tr, e * 2 + b + 1)
                    nc.scalar.activation(xeT_hi[:, 4 * b:4 * b + 4, :], ps[:, b, :].rearrange("p (a c) -> p a c", a=4),
                                         ACT.Copy).then_inc(xeT_hi_ok, 1)

            def silu(e, j, used):
                act.wait_ge(w_used, used)
                nc.scalar.activation(silu_g[:, j, :], ps[:, 2 * j, :], ACT.Silu).then_inc(silu_e, 1)

            def act_in(e, j):
                act.wait_ge(a_tr, e * 2 + j + 1)
                nc.scalar.activation(act_T_hi[:, 4 * j:4 * j + 4, :], ps[:, 6 + j, :].rearrange("p (a c) -> p a c", a=4),
                                     ACT.Copy).then_inc(aT_hi_ok, 1)

            def results(e, used):
                act.wait_ge(w_used, used)
                act.wait_ge(ye_free, e + CREDIT)
                act.wait_ge(val_ok, e + 1)
                nc.scalar.activation(ye[:].rearrange("p (a c) -> p a c", a=2), ps[:, 4:6, :], ACT.Copy,
                                     scale=val_s[:, 0:1]).then_inc(ye_ok, 1)

            rows_in(0)
            for n in range(FIRST):
                split(n)
                if n == 8 + LEAD - 1:
                    silu(0, 0, 8)
            with act.Fori(0, NE - 1) as e:
                for u in range(UNITS):
                    split(FIRST + u, e)
                    if u == LEAD - 1:
                        act_in(e, 0)
                        silu(e, 1, e * UNITS + FIRST)
                        rows_in(e + 1)
                    if u == 4 + LEAD - 1:
                        act_in(e, 1)
                    if u == 12 + LEAD - 1:
                        silu(e + 1, 0, e * UNITS + FIRST + 12)
                    if u == 16 + LEAD - 1:
                        results(e, e * UNITS + FIRST + 16)
            end = FIRST + (NE - 1) * UNITS
            for u in range(8):
                split(end + u)
                if u == LEAD - 1:
                    act_in(NE - 1, 0)
                    silu(NE - 1, 1, end)
                if u == 4 + LEAD - 1:
                    act_in(NE - 1, 1)
            results(NE - 1, end + 8)


_INS = ["x", "positions", "g_mix", "w_in", "gla_wa2_f", "gla_ba_f", "gla_wa2_b", "gla_ba_b", "gla_onorm", "w_gla_out",
        "mla_q_norm", "w_uq", "mla_kv_norm", "w_ukv", "q_head_norm", "k_head_norm", "w_mla_out", "w_o", "g_ffn",
        "w_router", "w_gate_e", "w_up_e", "w_down_e"]


def kernel(**inputs):
    import concourse.bacc as bacc
    from concourse.bass_utils import run_bass_kernel_spmd

    nc = bacc.Bacc("TRN2", target_bir_lowering=False, num_devices=1)
    arrays, args = {}, []
    for name in _INS:
        a = np.ascontiguousarray(inputs[name])
        arrays[f"in_{name}"] = a
        args.append(nc.dram_tensor(f"in_{name}", a.shape, mybir.dt.from_np(a.dtype), kind="ExternalInput").ap())
    args.append(nc.dram_tensor("layer_out", (1, S, D), F32, kind="ExternalOutput").ap())
    hybrid_layer(nc, *args)
    r = run_bass_kernel_spmd(nc, [arrays], core_ids=[0])
    return r.results[0]["layer_out"]
```
